# Optimizing a Trainium2 kernel written in Bass

```python
import math
import jax, jax.numpy as jnp
from jax import lax
import numpy as np

D_MODEL = 2048
BATCH = 1
SEQ = 256
DEPTH = 1

N_META = 16
HEAD_DIM = 64
ATTN_WIDTH = D_MODEL // 2
N_HEADS = ATTN_WIDTH // HEAD_DIM
N_KV_HEADS = N_HEADS // 4
KV_GROUP = N_HEADS // N_KV_HEADS
KV_WIDTH = N_KV_HEADS * HEAD_DIM
SSM_WIDTH = D_MODEL - ATTN_WIDTH
SSM_GROUP_CH = 16
SSM_GROUPS = SSM_WIDTH // SSM_GROUP_CH
SSM_STATE = 64
WINDOW = 128
BLOCK = 128
PAD = BLOCK - N_META
D_FF = 4 * D_MODEL
IN_WIDTH = ATTN_WIDTH + 2 * KV_WIDTH + SSM_WIDTH
NORM_EPS = 1e-6
NEG_INF = -1e30
STEP_MIN = 1e-3
STEP_MAX = 1e-1


def _rmsnorm(x, g):
    xf = x.astype(jnp.float32)
    y = xf * lax.rsqrt(jnp.mean(xf * xf, axis=-1, keepdims=True) + NORM_EPS)
    return (y * g.astype(jnp.float32)).astype(x.dtype)

def _alibi_slopes():
    h = jnp.arange(1, N_HEADS + 1, dtype=jnp.float32)
    return jnp.exp2(-8.0 * h / N_HEADS)

def _sliding_window_attention(q, k, v, sinks):
    b, L = q.shape[0], q.shape[1]
    dtype = q.dtype
    Lp = L + PAD
    nb = Lp // BLOCK
    qf = q.astype(jnp.float32)
    kf = k.astype(jnp.float32)
    vf = v.astype(jnp.float32)
    pad4 = ((0, 0), (PAD, 0), (0, 0), (0, 0))
    qp = jnp.pad(qf, pad4).reshape(b, nb, BLOCK, N_KV_HEADS, KV_GROUP, HEAD_DIM)
    kp = jnp.pad(kf, pad4).reshape(b, nb, BLOCK, N_KV_HEADS, HEAD_DIM)
    vp = jnp.pad(vf, pad4).reshape(b, nb, BLOCK, N_KV_HEADS, HEAD_DIM)
    pad5 = ((0, 0), (1, 0), (0, 0), (0, 0), (0, 0))
    k_band = jnp.concatenate([jnp.pad(kp, pad5)[:, :-1], kp], axis=2)
    v_band = jnp.concatenate([jnp.pad(vp, pad5)[:, :-1], vp], axis=2)
    k_meta = kf[:, :N_META]
    v_meta = vf[:, :N_META]

    n_idx = jnp.arange(nb)[:, None, None]
    i_idx = jnp.arange(BLOCK)[None, :, None]
    j_idx = jnp.arange(2 * BLOCK)[None, None, :]
    t_pos = n_idx * BLOCK + i_idx - PAD
    s_pos = (n_idx - 1) * BLOCK + j_idx - PAD
    band_mask = (s_pos >= N_META) & (s_pos <= t_pos) & (t_pos - s_pos < WINDOW)
    band_dist = jnp.abs(t_pos - s_pos).astype(jnp.float32)
    m_pos = jnp.arange(N_META)[None, None, :]
    meta_mask = m_pos <= t_pos
    meta_dist = jnp.abs(t_pos - m_pos).astype(jnp.float32)

    slopes = _alibi_slopes().reshape(N_KV_HEADS, KV_GROUP, 1, 1)
    scale = 1.0 / math.sqrt(HEAD_DIM)
    s_band = jnp.einsum('bnqkgd,bnskd->bnkgqs', qp, k_band) * scale
    s_band = s_band - slopes * band_dist[:, None, None]
    s_band = jnp.where(band_mask[:, None, None], s_band, NEG_INF)
    s_meta = jnp.einsum('bnqkgd,bmkd->bnkgqm', qp, k_meta) * scale
    s_meta = s_meta - slopes * meta_dist[:, None, None]
    s_meta = jnp.where(meta_mask[:, None, None], s_meta, NEG_INF)
    sink = jnp.broadcast_to(sinks.astype(jnp.float32).reshape(N_KV_HEADS, KV_GROUP, 1, 1),
                            s_band.shape[:-1] + (1,))
    probs = jax.nn.softmax(jnp.concatenate([s_band, s_meta, sink], axis=-1), axis=-1)
    p_band = probs[..., :2 * BLOCK]
    p_meta = probs[..., 2 * BLOCK:2 * BLOCK + N_META]
    out = (jnp.einsum('bnkgqs,bnskd->bnqkgd', p_band, v_band)
           + jnp.einsum('bnkgqm,bmkd->bnqkgd', p_meta, v_meta))
    out = out.reshape(b, Lp, ATTN_WIDTH)[:, PAD:]
    return out.astype(dtype)

def _ssm_combine(e_i, e_j):
    a_i, b_i = e_i
    a_j, b_j = e_j
    return a_j * a_i, a_j * b_i + b_j

def _s5_mixer(u, lam_re, lam_im, log_step, b_re, b_im, c_re, c_im, d, w_glu, b_glu):
    dtype = u.dtype
    b, L = u.shape[0], u.shape[1]
    ul = jnp.moveaxis(u.astype(jnp.float32).reshape(b, L, SSM_GROUPS, SSM_GROUP_CH), 1, 0)
    lam = lax.complex(lam_re.astype(jnp.float32), lam_im.astype(jnp.float32))
    delta = jnp.exp(log_step.astype(jnp.float32))[:, None]
    lam_bar = jnp.exp(lam * delta)
    b_c = lax.complex(b_re.astype(jnp.float32), b_im.astype(jnp.float32))
    b_bar = ((lam_bar - 1.0) / lam)[..., None] * b_c
    c_c = lax.complex(c_re.astype(jnp.float32), c_im.astype(jnp.float32))
    bu = jnp.einsum('lbgh,gph->lbgp', ul.astype(jnp.complex64), b_bar)
    a = jnp.broadcast_to(lam_bar, (L, 1, SSM_GROUPS, SSM_STATE))
    _, states = lax.associative_scan(_ssm_combine, (a, bu), axis=0)
    y = jnp.real(jnp.einsum('lbgp,ghp->lbgh', states, c_c))
    y = y + d.astype(jnp.float32).reshape(SSM_GROUPS, SSM_GROUP_CH) * ul
    y = jnp.moveaxis(y, 0, 1).reshape(b, L, SSM_WIDTH)
    g = jax.nn.gelu(y)
    out = g * jax.nn.sigmoid(g @ w_glu.astype(jnp.float32) + b_glu.astype(jnp.float32))
    return out.astype(dtype)

def first_inputs(seed: int = 0) -> dict:
    key = jax.random.key(seed)
    ks = jax.random.split(key, 24)
    f32 = jnp.float32
    nrm = lambda k, shape, s: jax.random.normal(k, shape, f32) * s
    x = jax.random.normal(ks[0], (BATCH, SEQ, D_MODEL), f32)
    meta_tokens = nrm(ks[1], (N_META, D_MODEL), 1.0)
    norm_mix_g = 1.0 + nrm(ks[2], (DEPTH, D_MODEL), 0.02)
    w_in = nrm(ks[3], (DEPTH, D_MODEL, IN_WIDTH), D_MODEL ** -0.5)
    q_norm_g = 1.0 + nrm(ks[4], (DEPTH, HEAD_DIM), 0.02)
    k_norm_g = 1.0 + nrm(ks[5], (DEPTH, HEAD_DIM), 0.02)
    attn_sinks = nrm(ks[6], (DEPTH, N_HEADS), 0.5)
    n = jnp.arange(SSM_STATE, dtype=f32)
    ssm_lambda_re = -0.5 + nrm(ks[7], (DEPTH, SSM_GROUPS, SSM_STATE), 1e-3)
    ssm_lambda_im = math.pi * n + nrm(ks[8], (DEPTH, SSM_GROUPS, SSM_STATE), 1e-3)
    ssm_log_step = jax.random.uniform(ks[9], (DEPTH, SSM_GROUPS), f32,
                                      math.log(STEP_MIN), math.log(STEP_MAX))
    bs = (SSM_GROUP_CH ** -0.5) / math.sqrt(2.0)
    cs = (SSM_STATE ** -0.5) / math.sqrt(2.0)
    ssm_b_re = nrm(ks[10], (DEPTH, SSM_GROUPS, SSM_STATE, SSM_GROUP_CH), bs)
    ssm_b_im = nrm(ks[11], (DEPTH, SSM_GROUPS, SSM_STATE, SSM_GROUP_CH), bs)
    ssm_c_re = nrm(ks[12], (DEPTH, SSM_GROUPS, SSM_GROUP_CH, SSM_STATE), cs)
    ssm_c_im = nrm(ks[13], (DEPTH, SSM_GROUPS, SSM_GROUP_CH, SSM_STATE), cs)
    ssm_d = nrm(ks[14], (DEPTH, SSM_WIDTH), 1.0)
    w_glu = nrm(ks[15], (DEPTH, SSM_WIDTH, SSM_WIDTH), SSM_WIDTH ** -0.5)
    b_glu = nrm(ks[16], (DEPTH, SSM_WIDTH), 0.01)
    attn_out_g = 1.0 + nrm(ks[17], (DEPTH, ATTN_WIDTH), 0.02)
    ssm_out_g = 1.0 + nrm(ks[18], (DEPTH, SSM_WIDTH), 0.02)
    w_out = nrm(ks[19], (DEPTH, D_MODEL, D_MODEL), D_MODEL ** -0.5)
    norm_mlp_g = 1.0 + nrm(ks[20], (DEPTH, D_MODEL), 0.02)
    w_up = nrm(ks[21], (DEPTH, D_MODEL, D_FF), D_MODEL ** -0.5)
    w_down = nrm(ks[22], (DEPTH, D_FF, D_MODEL), D_FF ** -0.5)
    return {"x": x, "meta_tokens": meta_tokens, "norm_mix_g": norm_mix_g, "w_in": w_in,
            "q_norm_g": q_norm_g, "k_norm_g": k_norm_g, "attn_sinks": attn_sinks,
            "ssm_lambda_re": ssm_lambda_re, "ssm_lambda_im": ssm_lambda_im,
            "ssm_log_step": ssm_log_step, "ssm_b_re": ssm_b_re, "ssm_b_im": ssm_b_im,
            "ssm_c_re": ssm_c_re, "ssm_c_im": ssm_c_im, "ssm_d": ssm_d,
            "w_glu": w_glu, "b_glu": b_glu, "attn_out_g": attn_out_g, "ssm_out_g": ssm_out_g,
            "w_out": w_out, "norm_mlp_g": norm_mlp_g, "w_up": w_up, "w_down": w_down}

def first_block(x, meta_tokens, norm_mix_g, w_in, q_norm_g, k_norm_g, attn_sinks,
              ssm_lambda_re, ssm_lambda_im, ssm_log_step, ssm_b_re, ssm_b_im,
              ssm_c_re, ssm_c_im, ssm_d, w_glu, b_glu, attn_out_g, ssm_out_g,
              w_out, norm_mlp_g, w_up, w_down):
    b = x.shape[0]
    meta = jnp.broadcast_to(meta_tokens.astype(x.dtype)[None], (b, N_META, D_MODEL))
    h_res = jnp.concatenate([meta, x], axis=1)
    L = h_res.shape[1]
    for l in range(DEPTH):
        h = _rmsnorm(h_res, norm_mix_g[l])
        proj = h @ w_in[l]
        q = proj[..., :ATTN_WIDTH].reshape(b, L, N_HEADS, HEAD_DIM)
        k = proj[..., ATTN_WIDTH:ATTN_WIDTH + KV_WIDTH].reshape(b, L, N_KV_HEADS, HEAD_DIM)
        v = proj[..., ATTN_WIDTH + KV_WIDTH:ATTN_WIDTH + 2 * KV_WIDTH].reshape(b, L, N_KV_HEADS, HEAD_DIM)
        u = proj[..., ATTN_WIDTH + 2 * KV_WIDTH:]
        q = _rmsnorm(q, q_norm_g[l])
        k = _rmsnorm(k, k_norm_g[l])
        attn = _sliding_window_attention(q, k, v, attn_sinks[l])
        ssm = _s5_mixer(u, ssm_lambda_re[l], ssm_lambda_im[l], ssm_log_step[l],
                        ssm_b_re[l], ssm_b_im[l], ssm_c_re[l], ssm_c_im[l], ssm_d[l],
                        w_glu[l], b_glu[l])
        mix = jnp.concatenate([_rmsnorm(attn, attn_out_g[l]), _rmsnorm(ssm, ssm_out_g[l])], axis=-1)
        h_res = h_res + mix @ w_out[l]
        h2 = _rmsnorm(h_res, norm_mlp_g[l])
        h_res = h_res + jnp.square(jax.nn.relu(h2 @ w_up[l])) @ w_down[l]
    return h_res[:, N_META:]


_first_inputs = first_inputs


def first_inputs(seed=0):
    import zlib

    import numpy as np

    out = dict(_first_inputs(seed))
    spreads = {}
    factors = {}
    for name, (base, spread) in spreads.items():
        noise = np.random.default_rng([zlib.crc32(name.encode()), seed]).standard_normal(out[name].shape)
        drawn = base * np.exp(spread * noise) if base else spread * noise
        out[name] = __import__('jax').numpy.asarray(drawn.astype(out[name].dtype))
    for name, factor in factors.items():
        out[name] = (out[name] * factor).astype(out[name].dtype)
    return out


_narrow_inputs = first_inputs


def first_inputs(seed=0):

    out = dict(_narrow_inputs(seed))
    wider = {'norm_mix_g': 3.13,
     'q_norm_g': 7.95,
     'k_norm_g': 6.8,
     'ssm_lambda_re': 12.0,
     'b_glu': 12.0,
     'attn_out_g': 6.04,
     'ssm_out_g': 6.48,
     'norm_mlp_g': 4.27}
    for name, times in wider.items():
        mean = out[name].mean()
        out[name] = (mean + times * (out[name] - mean)).astype(out[name].dtype)
    return out


GRID_W = 64
CTX_LEN = 256

BRANCH_WIDTH = 1024
N_BRANCH = 3

HY_WIDTH = BRANCH_WIDTH
HY_ORDER = 2
HY_CONV = 3
HY_EMB = 33
HY_BANDS = (HY_EMB - 1) // 2
HY_FILTER_HIDDEN = 64
HY_DECAY_TARGET = 1e-2
HY_FAST_DECAY = 0.3
HY_SLOW_DECAY = 1.5

HG_HEADS = 8
HG_DK = 128
HG_DV = BRANCH_WIDTH // HG_HEADS
HG_FWIDTH = HG_HEADS * HG_DK
HG_WIDTH = HG_HEADS * HG_DV
HG_F_MIN = 1e-30

DN_QK_HEADS = 4
DN_V_HEADS = 8
DN_DK = 128
DN_DV = BRANCH_WIDTH // DN_V_HEADS
DN_QK_WIDTH = DN_QK_HEADS * DN_DK
DN_WIDTH = DN_V_HEADS * DN_DV
DN_CONV = 3

CHUNK = 64
D_FF_2 = 4 * D_MODEL
ALPHA = (2 * DEPTH) ** 0.25
BETA_INIT = (8 * DEPTH) ** -0.25
LN_EPS = 1e-5
RMS_EPS = 1e-6

STATE_SIZES = (HG_FWIDTH, HG_FWIDTH, HG_WIDTH, DN_QK_WIDTH, DN_WIDTH, 2 * DN_V_HEADS, 2 * DN_V_HEADS)
READ_SIZES = (HG_FWIDTH, HG_WIDTH, DN_QK_WIDTH, DN_WIDTH)
IN_SIZES = STATE_SIZES + READ_SIZES + ((HY_ORDER + 1) * HY_WIDTH, N_BRANCH * D_MODEL)
STATE_COLS = sum(STATE_SIZES)
IN_COLS = sum(IN_SIZES)


def _split(h, sizes):
    idx = [int(i) for i in np.cumsum(sizes)[:-1]]
    return jnp.split(h, idx, axis=-1)

def _flip(t):
    return None if t is None else jnp.flip(t, axis=1)

def _layernorm(x, g, b):
    xf = x.astype(jnp.float32)
    mu = jnp.mean(xf, -1, keepdims=True)
    var = jnp.mean(jnp.square(xf - mu), -1, keepdims=True)
    return ((xf - mu) * lax.rsqrt(var + LN_EPS) * g + b).astype(x.dtype)

def _rmsnorm_2(o, w):
    of = o.astype(jnp.float32)
    return of * lax.rsqrt(jnp.mean(of * of, -1, keepdims=True) + RMS_EPS) * w

def _l2norm(t):
    t = t.astype(jnp.float32)
    return t * lax.rsqrt(jnp.sum(t * t, -1, keepdims=True) + 1e-6)

def _modulate(x, shift, scale):
    return x * (1.0 + scale) + shift

def _short_conv(x, w, is_grid):
    b, l, ch = x.shape
    xs = x.reshape(b, l // GRID_W, GRID_W, ch) if is_grid else x
    k = w.shape[0]
    n = xs.shape[-2]
    xp = jnp.pad(xs, [(0, 0)] * (xs.ndim - 2) + [(k // 2, k // 2), (0, 0)])
    y = xp[..., 0:n, :] * w[0]
    for j in range(1, k):
        y = y + xp[..., j:j + n, :] * w[j]
    return y.reshape(b, l, ch)

def _hyena_filters(L, w1, b1, w2, b2, w3):
    f32 = jnp.float32
    t = jnp.linspace(0.0, 1.0, L, dtype=f32)[:, None]
    ang = (2.0 * math.pi / L) * jnp.arange(L, dtype=f32)[:, None]
    bands = jnp.linspace(1e-4, HY_BANDS - 1, HY_BANDS, dtype=f32)[None, :]
    feats = jnp.concatenate([t, jnp.cos(bands * ang), -jnp.sin(bands * ang)], axis=-1)
    hid = jnp.sin(feats @ w1.astype(f32) + b1.astype(f32))
    hid = jnp.sin(hid @ w2.astype(f32) + b2.astype(f32))
    h = (hid @ w3.astype(f32)).reshape(L, HY_ORDER, 2, HY_WIDTH)
    deltas = jnp.abs(jnp.linspace(math.log(HY_DECAY_TARGET) / HY_SLOW_DECAY,
                                  math.log(HY_DECAY_TARGET) / HY_FAST_DECAY, HY_WIDTH, dtype=f32))
    window = jnp.exp(-t * deltas)
    return h * window[:, None, None, :]

def _fft_long_conv(u, h_fwd, h_bwd, skip):
    L = u.shape[1]
    kfull = jnp.concatenate([h_fwd, jnp.zeros_like(h_fwd[:1]), h_bwd[:0:-1]], axis=0)
    uf = jnp.fft.rfft(u.astype(jnp.float32), n=2 * L, axis=1)
    kf = jnp.fft.rfft(kfull.astype(jnp.float32), n=2 * L, axis=0)
    y = jnp.fft.irfft(uf * kf[None], n=2 * L, axis=1)[:, :L]
    return (y + u.astype(jnp.float32) * skip).astype(u.dtype)

def _hyena(hh, conv_w, conv_b, filt_params, skip, is_grid):
    L = hh.shape[1]
    filt = _hyena_filters(L, *filt_params)
    z = _short_conv(hh, conv_w, is_grid) + conv_b
    v, *gates = jnp.split(z, HY_ORDER + 1, axis=-1)
    y = v
    for n, gate in enumerate(gates):
        y = gate * _fft_long_conv(y, filt[:, n, 0], filt[:, n, 1], skip[n])
    return y

def _to_chunks(t):
    b, l = t.shape[:2]
    t = t.reshape(b, l // CHUNK, CHUNK, *t.shape[2:])
    return jnp.moveaxis(t, (1, 2), (0, 3))

def _from_chunks(t):
    t = jnp.moveaxis(t, (0, 3), (1, 2))
    return t.reshape(t.shape[0], t.shape[1] * t.shape[2], *t.shape[3:])

def _gla_scan(q, k, v, log_f, s0):
    with_output = q is not None
    tri = jnp.tril(jnp.ones((CHUNK, CHUNK), bool))[:, :, None]
    xs = tuple(_to_chunks(t.astype(jnp.float32)) for t in (k, v, log_f))
    if with_output:
        xs = xs + (_to_chunks(q.astype(jnp.float32)),)

    def step(s, inp):
        kc, vc, gc = inp[:3]
        bc = jnp.cumsum(gc, axis=-2)
        b_last = bc[..., -1:, :]
        s_new = jnp.exp(b_last[..., 0, :])[..., None] * s + jnp.einsum(
            'bhsk,bhsv->bhkv', kc * jnp.exp(b_last - bc), vc)
        if not with_output:
            return s_new, None
        qc = inp[3]
        diff = bc[..., :, None, :] - bc[..., None, :, :]
        w = jnp.where(tri, jnp.exp(jnp.where(tri, diff, 0.0)), 0.0)
        att = jnp.einsum('bhtk,bhsk,bhtsk->bhts', qc, kc, w)
        o = jnp.einsum('bhtk,bhkv->bhtv', qc * jnp.exp(bc), s) + jnp.einsum('bhts,bhsv->bhtv', att, vc)
        return s_new, o

    s_fin, ys = lax.scan(step, s0, xs)
    return (_from_chunks(ys) if with_output else None), s_fin

def _delta_scan(q, k, v, g, beta, s0):
    with_output = q is not None
    tri = jnp.tril(jnp.ones((CHUNK, CHUNK), bool))
    strict = jnp.tril(jnp.ones((CHUNK, CHUNK), bool), -1)
    eye = jnp.eye(CHUNK, dtype=jnp.float32)
    xs = tuple(_to_chunks(t.astype(jnp.float32)) for t in (k, v, g, beta))
    if with_output:
        xs = xs + (_to_chunks(q.astype(jnp.float32)),)

    def step(s, inp):
        kc, vc, gc, bc = inp[:4]
        dv = vc.shape[-1]
        gcum = jnp.cumsum(gc, axis=-1)
        diff = gcum[..., :, None] - gcum[..., None, :]
        decay = jnp.where(tri, jnp.exp(jnp.where(tri, diff, 0.0)), 0.0)
        kb = kc * bc[..., None]
        a = eye + jnp.where(strict, jnp.einsum('bhtk,bhsk->bhts', kb, kc) * decay, 0.0)
        rhs = jnp.concatenate([vc * bc[..., None], kb * jnp.exp(gcum)[..., None]], axis=-1)
        sol = lax.linalg.triangular_solve(a, rhs, left_side=True, lower=True, unit_diagonal=False)
        u, w = sol[..., :dv], sol[..., dv:]
        v_new = u - jnp.einsum('bhtk,bhkv->bhtv', w, s)
        g_last = gcum[..., -1:]
        s_new = jnp.exp(g_last)[..., None] * s + jnp.einsum(
            'bhsk,bhsv->bhkv', kc * jnp.exp(g_last - gcum)[..., None], v_new)
        if not with_output:
            return s_new, None
        qc = inp[4]
        att = jnp.einsum('bhtk,bhsk->bhts', qc, kc) * decay
        o = jnp.einsum('bhtk,bhkv->bhtv', qc * jnp.exp(gcum)[..., None], s) + jnp.einsum(
            'bhts,bhsv->bhtv', att, v_new)
        return s_new, o

    s_fin, ys = lax.scan(step, s0, xs)
    return (_from_chunks(ys) if with_output else None), s_fin

def _hgrn2(q, f_f, f_b, i, g, lb_f, lb_b, norm_w, states):
    bsz, L = i.shape[:2]
    heads = lambda t: t.reshape(bsz, L, HG_HEADS, -1)

    def forget(fz, lb):
        fz = fz.astype(jnp.float32)
        f = lb + (1.0 - lb) * jax.nn.sigmoid(fz)
        return heads(jnp.log(jnp.maximum(f, HG_F_MIN))), heads((1.0 - lb) * jax.nn.sigmoid(-fz))

    lf_f, k_f = forget(f_f, lb_f)
    lf_b, k_b = forget(f_b, lb_b)
    ih = heads(i)
    qh = None if q is None else heads(jax.nn.silu(q))
    o_f, s_f = _gla_scan(qh, k_f, ih, lf_f, states[0])
    o_b, s_b = _gla_scan(_flip(qh), _flip(k_b), _flip(ih), _flip(lf_b), states[1])
    if q is None:
        return None, (s_f, s_b)
    o = _rmsnorm_2(o_f + _flip(o_b), norm_w) * jax.nn.sigmoid(heads(g).astype(jnp.float32))
    return o.reshape(bsz, L, HG_WIDTH).astype(i.dtype), (s_f, s_b)

def _gated_deltanet(q_raw, k_raw, v_raw, z, a_all, b_all, conv_q, conv_k, conv_v,
                    a_log, dt_bias, norm_w, states, is_grid):
    bsz, L = k_raw.shape[:2]
    rep = DN_V_HEADS // DN_QK_HEADS
    k = _l2norm(jax.nn.silu(_short_conv(k_raw, conv_k, is_grid)).reshape(bsz, L, DN_QK_HEADS, DN_DK))
    k = jnp.repeat(k, rep, axis=2)
    v = jax.nn.silu(_short_conv(v_raw, conv_v, is_grid)).reshape(bsz, L, DN_V_HEADS, DN_DV)
    a_f, a_b = jnp.split(a_all.astype(jnp.float32), 2, axis=-1)
    b_f, b_b = jnp.split(b_all.astype(jnp.float32), 2, axis=-1)
    g_f = -jnp.exp(a_log[0]) * jax.nn.softplus(a_f + dt_bias[0])
    g_b = -jnp.exp(a_log[1]) * jax.nn.softplus(a_b + dt_bias[1])
    q = None
    if q_raw is not None:
        q = _l2norm(jax.nn.silu(_short_conv(q_raw, conv_q, is_grid)).reshape(bsz, L, DN_QK_HEADS, DN_DK))
        q = jnp.repeat(q * DN_DK ** -0.5, rep, axis=2)
    o_f, s_f = _delta_scan(q, k, v, g_f, jax.nn.sigmoid(b_f), states[0])
    o_b, s_b = _delta_scan(_flip(q), _flip(k), _flip(v), _flip(g_b), _flip(jax.nn.sigmoid(b_b)), states[1])
    if q is None:
        return None, (s_f, s_b)
    zh = z.reshape(bsz, L, DN_V_HEADS, DN_DV).astype(jnp.float32)
    o = _rmsnorm_2(o_f + _flip(o_b), norm_w) * jax.nn.silu(zh)
    return o.reshape(bsz, L, DN_WIDTH).astype(k_raw.dtype), (s_f, s_b)

def _token_mixers(u, lp, init_states, is_grid, with_output):
    bsz, L, _ = u.shape
    if with_output:
        parts = _split(u @ lp["w_in"], IN_SIZES)
    else:
        parts = _split(u @ lp["w_in"][:, :STATE_COLS], STATE_SIZES) + [None] * (len(IN_SIZES) - len(STATE_SIZES))
    hg_ff, hg_fb, hg_i, dn_k, dn_v, dn_a, dn_b, hg_q, hg_g, dn_q, dn_z, hy_in, gate_in = parts
    hg_out, hg_states = _hgrn2(hg_q, hg_ff, hg_fb, hg_i, hg_g, lp["lb_fwd"], lp["lb_bwd"],
                               lp["hg_norm_w"], init_states[0])
    dn_out, dn_states = _gated_deltanet(dn_q, dn_k, dn_v, dn_z, dn_a, dn_b, lp["dn_conv_q"], lp["dn_conv_k"],
                                        lp["dn_conv_v"], lp["dn_a_log"], lp["dn_dt_bias"], lp["dn_norm_w"],
                                        init_states[1], is_grid)
    states = (hg_states, dn_states)
    if not with_output:
        return None, states
    hy_out = _hyena(hy_in, lp["hy_conv_w"], lp["hy_conv_b"], lp["hy_filt"], lp["hy_skip"], is_grid)
    branches = jnp.stack([hy_out, hg_out, dn_out], axis=2)
    proj = jnp.einsum('blgc,gcd->blgd', branches, lp["w_branch"])
    gate = jax.nn.sigmoid(gate_in.reshape(bsz, L, N_BRANCH, D_MODEL))
    y = jnp.sum(gate * proj, axis=2) @ lp["w_out"]
    return y, states

def _sq_relu_mlp(u, w1, w2):
    return jnp.square(jax.nn.relu(u @ w1)) @ w2

def second_inputs(seed: int = 0) -> dict:
    key = jax.random.key(seed)
    ks = jax.random.split(key, 40)
    f32 = jnp.float32
    nrm = lambda k, shape, s: s * jax.random.normal(k, shape, f32)
    dt = jnp.exp(jax.random.uniform(ks[22], (DEPTH, 2, DN_V_HEADS), f32, math.log(1e-3), math.log(1e-1)))
    return {
        "x": nrm(ks[0], (BATCH, SEQ, D_MODEL), 1.0),
        "c": nrm(ks[1], (BATCH, D_MODEL), 1.0),
        "ctx": nrm(ks[2], (BATCH, CTX_LEN, D_MODEL), 1.0),
        "c_ctx": nrm(ks[3], (D_MODEL,), 1.0),
        "w_ada": nrm(ks[4], (DEPTH, D_MODEL, 6 * D_MODEL), 0.5 * D_MODEL ** -0.5),
        "b_ada": nrm(ks[5], (DEPTH, 6 * D_MODEL), 0.02),
        "w_in": nrm(ks[6], (DEPTH, D_MODEL, IN_COLS), D_MODEL ** -0.5),
        "hy_conv_w": nrm(ks[7], (DEPTH, HY_CONV, (HY_ORDER + 1) * HY_WIDTH), HY_CONV ** -0.5),
        "hy_conv_b": nrm(ks[8], (DEPTH, (HY_ORDER + 1) * HY_WIDTH), 0.02),
        "hy_filt_w1": nrm(ks[9], (DEPTH, HY_EMB, HY_FILTER_HIDDEN), HY_EMB ** -0.5),
        "hy_filt_b1": nrm(ks[10], (DEPTH, HY_FILTER_HIDDEN), 0.02),
        "hy_filt_w2": nrm(ks[11], (DEPTH, HY_FILTER_HIDDEN, HY_FILTER_HIDDEN), HY_FILTER_HIDDEN ** -0.5),
        "hy_filt_b2": nrm(ks[12], (DEPTH, HY_FILTER_HIDDEN), 0.02),
        "hy_filt_w3": nrm(ks[13], (DEPTH, HY_FILTER_HIDDEN, HY_ORDER * 2 * HY_WIDTH), 0.1 * HY_FILTER_HIDDEN ** -0.5),
        "hy_skip": nrm(ks[14], (DEPTH, HY_ORDER, HY_WIDTH), 1.0),
        "hg_lb_logits": nrm(ks[15], (2, DEPTH, HG_FWIDTH), 0.1),
        "hg_norm_w": 1.0 + nrm(ks[16], (DEPTH, HG_DV), 0.02),
        "dn_conv_q": nrm(ks[17], (DEPTH, DN_CONV, DN_QK_WIDTH), DN_CONV ** -0.5),
        "dn_conv_k": nrm(ks[18], (DEPTH, DN_CONV, DN_QK_WIDTH), DN_CONV ** -0.5),
        "dn_conv_v": nrm(ks[19], (DEPTH, DN_CONV, DN_WIDTH), DN_CONV ** -0.5),
        "dn_a_log": jnp.log(jax.random.uniform(ks[20], (DEPTH, 2, DN_V_HEADS), f32, 1.0, 16.0)),
        "dn_dt_bias": dt + jnp.log(-jnp.expm1(-dt)),
        "dn_norm_w": 1.0 + nrm(ks[21], (DEPTH, DN_DV), 0.02),
        "w_branch": nrm(ks[23], (DEPTH, N_BRANCH, BRANCH_WIDTH, D_MODEL), BRANCH_WIDTH ** -0.5),
        "w_out": nrm(ks[24], (DEPTH, D_MODEL, D_MODEL), BETA_INIT * D_MODEL ** -0.5),
        "ln1_g": 1.0 + nrm(ks[25], (DEPTH, D_MODEL), 0.02),
        "ln1_b": nrm(ks[26], (DEPTH, D_MODEL), 0.02),
        "w_ff1": nrm(ks[27], (DEPTH, D_MODEL, D_FF_2), D_MODEL ** -0.5),
        "w_ff2": nrm(ks[28], (DEPTH, D_FF_2, D_MODEL), BETA_INIT * D_FF_2 ** -0.5),
        "ln2_g": 1.0 + nrm(ks[29], (DEPTH, D_MODEL), 0.02),
        "ln2_b": nrm(ks[30], (DEPTH, D_MODEL), 0.02),
    }

def second_block(x, c, ctx, c_ctx, w_ada, b_ada, w_in, hy_conv_w, hy_conv_b, hy_filt_w1, hy_filt_b1,
              hy_filt_w2, hy_filt_b2, hy_filt_w3, hy_skip, hg_lb_logits, hg_norm_w, dn_conv_q, dn_conv_k,
              dn_conv_v, dn_a_log, dn_dt_bias, dn_norm_w, w_branch, w_out, ln1_g, ln1_b, w_ff1, w_ff2,
              ln2_g, ln2_b):
    f32 = jnp.float32
    bsz = x.shape[0]
    p = jax.nn.softmax(hg_lb_logits.astype(f32), axis=1)
    lower_bounds = jnp.cumsum(p, axis=1) - p[:, :1]
    h_ctx = ctx
    for l in range(DEPTH):
        last = l == DEPTH - 1
        lp = {
            "w_in": w_in[l], "hy_conv_w": hy_conv_w[l], "hy_conv_b": hy_conv_b[l],
            "hy_filt": (hy_filt_w1[l], hy_filt_b1[l], hy_filt_w2[l], hy_filt_b2[l], hy_filt_w3[l]),
            "hy_skip": hy_skip[l], "lb_fwd": lower_bounds[0, l], "lb_bwd": lower_bounds[1, l],
            "hg_norm_w": hg_norm_w[l], "dn_conv_q": dn_conv_q[l], "dn_conv_k": dn_conv_k[l],
            "dn_conv_v": dn_conv_v[l], "dn_a_log": dn_a_log[l], "dn_dt_bias": dn_dt_bias[l],
            "dn_norm_w": dn_norm_w[l], "w_branch": w_branch[l], "w_out": w_out[l],
        }
        zero_hg = jnp.zeros((bsz, HG_HEADS, HG_DK, HG_DV), f32)
        zero_dn = jnp.zeros((bsz, DN_V_HEADS, DN_DK, DN_DV), f32)
        init = ((zero_hg, zero_hg), (zero_dn, zero_dn))
        n_mod = 2 if last else 6
        mod_c = jax.nn.silu(c_ctx) @ w_ada[l][:, :n_mod * D_MODEL] + b_ada[l][:n_mod * D_MODEL]
        mods_c = jnp.split(mod_c, n_mod)
        y_ctx, ctx_states = _token_mixers(_modulate(h_ctx, mods_c[0], mods_c[1]), lp, init, False, not last)
        if not last:
            h_ctx = _layernorm(ALPHA * h_ctx + mods_c[2] * y_ctx, ln1_g[l], ln1_b[l])
            h_ctx = _layernorm(ALPHA * h_ctx + mods_c[5] * _sq_relu_mlp(_modulate(h_ctx, mods_c[3], mods_c[4]),
                                                                          w_ff1[l], w_ff2[l]), ln2_g[l], ln2_b[l])
        mod = jax.nn.silu(c) @ w_ada[l] + b_ada[l]
        sh1, sc1, g1, sh2, sc2, g2 = [m[:, None, :] for m in jnp.split(mod, 6, axis=-1)]
        y, _ = _token_mixers(_modulate(x, sh1, sc1), lp, ctx_states, True, True)
        x = _layernorm(ALPHA * x + g1 * y, ln1_g[l], ln1_b[l])
        x = _layernorm(ALPHA * x + g2 * _sq_relu_mlp(_modulate(x, sh2, sc2), w_ff1[l], w_ff2[l]),
                       ln2_g[l], ln2_b[l])
    return x


_first_inputs_2 = second_inputs


def second_inputs(seed=0):
    import zlib

    import numpy as np

    out = dict(_first_inputs_2(seed))
    spreads = {}
    factors = {'ctx': 7.118,
     'c_ctx': 8.0,
     'b_ada': 2.961,
     'hy_conv_b': 8.0,
     'hy_filt_b1': 8.0,
     'hy_filt_b2': 8.0,
     'hg_norm_w': 8.0,
     'dn_a_log': 5.893,
     'dn_norm_w': 8.0,
     'ln1_g': 2.712,
     'ln1_b': 2.902,
     'ln2_g': 2.85,
     'ln2_b': 2.77}
    for name, (base, spread) in spreads.items():
        noise = np.random.default_rng([zlib.crc32(name.encode()), seed]).standard_normal(out[name].shape)
        drawn = base * np.exp(spread * noise) if base else spread * noise
        out[name] = __import__('jax').numpy.asarray(drawn.astype(out[name].dtype))
    for name, factor in factors.items():
        out[name] = (out[name] * factor).astype(out[name].dtype)
    return out


_narrow_inputs_2 = second_inputs


def second_inputs(seed=0):

    out = dict(_narrow_inputs_2(seed))
    wider = {'hy_filt_b1': 3.22,
     'hy_filt_b2': 3.01,
     'hg_norm_w': 9.02,
     'dn_norm_w': 8.06,
     'ln2_g': 3.21,
     'ln2_b': 3.21}
    for name, times in wider.items():
        mean = out[name].mean()
        out[name] = (mean + times * (out[name] - mean)).astype(out[name].dtype)
    return out


def setup_inputs(seed=0):
    out = dict(first_inputs(seed))
    for name, value in second_inputs(seed + 1).items():
        if name != "x":
            out[name + "_2"] = value
    return out


def reference(
    x, meta_tokens, norm_mix_g, w_in, q_norm_g, k_norm_g, attn_sinks, ssm_lambda_re,
    ssm_lambda_im, ssm_log_step, ssm_b_re, ssm_b_im, ssm_c_re, ssm_c_im, ssm_d, w_glu, b_glu,
    attn_out_g, ssm_out_g, w_out, norm_mlp_g, w_up, w_down, c_2, ctx_2, c_ctx_2, w_ada_2,
    b_ada_2, w_in_2, hy_conv_w_2, hy_conv_b_2, hy_filt_w1_2, hy_filt_b1_2, hy_filt_w2_2,
    hy_filt_b2_2, hy_filt_w3_2, hy_skip_2, hg_lb_logits_2, hg_norm_w_2, dn_conv_q_2,
    dn_conv_k_2, dn_conv_v_2, dn_a_log_2, dn_dt_bias_2, dn_norm_w_2, w_branch_2, w_out_2,
    ln1_g_2, ln1_b_2, w_ff1_2, w_ff2_2, ln2_g_2, ln2_b_2,
):
    x = first_block(
        x, meta_tokens, norm_mix_g, w_in, q_norm_g, k_norm_g, attn_sinks, ssm_lambda_re,
        ssm_lambda_im, ssm_log_step, ssm_b_re, ssm_b_im, ssm_c_re, ssm_c_im, ssm_d, w_glu,
        b_glu, attn_out_g, ssm_out_g, w_out, norm_mlp_g, w_up, w_down,
    )
    return second_block(
        x, c_2, ctx_2, c_ctx_2, w_ada_2, b_ada_2, w_in_2, hy_conv_w_2, hy_conv_b_2,
        hy_filt_w1_2, hy_filt_b1_2, hy_filt_w2_2, hy_filt_b2_2, hy_filt_w3_2, hy_skip_2,
        hg_lb_logits_2, hg_norm_w_2, dn_conv_q_2, dn_conv_k_2, dn_conv_v_2, dn_a_log_2,
        dn_dt_bias_2, dn_norm_w_2, w_branch_2, w_out_2, ln1_g_2, ln1_b_2, w_ff1_2, w_ff2_2,
        ln2_g_2, ln2_b_2,
    )


_drawn_inputs = setup_inputs


def setup_inputs(seed=0):
    import zlib

    import numpy as np

    out = dict(_drawn_inputs(seed))
    spreads = {}
    factors = {'ssm_lambda_re': 200.0,
     'c_ctx_2': 2.767,
     'ssm_lambda_im': 28.672,
     'ssm_log_step': 29.92,
     'ssm_b_re': 38.952,
     'ssm_b_im': 39.184,
     'ssm_c_re': 39.288,
     'ssm_c_im': 38.672}
    for name, (base, spread) in spreads.items():
        noise = np.random.default_rng([zlib.crc32(name.encode()), seed]).standard_normal(out[name].shape)
        drawn = base * np.exp(spread * noise) if base else spread * noise
        out[name] = __import__('jax').numpy.asarray(drawn.astype(out[name].dtype))
    for name, factor in factors.items():
        out[name] = (out[name] * factor).astype(out[name].dtype)
    return out
```

```python
from contextlib import contextmanager

import numpy as np

import concourse.bass as bass
from concourse import mybir
from concourse.alu_op_type import AluOpType as ALU

F32 = mybir.dt.float32
I32 = mybir.dt.int32
ACT = mybir.ActivationFunctionType
AX = mybir.AxisListType
ds = bass.ds

P = 128
DM = 2048
KD = DM // P
NMETA = 16
T = 256
L = T + NMETA
HD = 64
NH = 16
NKV = 4
DFF = 8192
TWO_PI_BELOW = 6.283185
MAGIC = 12582912.0


class Sem:

    def __init__(self, prog, name, unit=1):
        self.prog, self.name, self.count = prog, name, unit
        self.sem = prog.nc.alloc_semaphore(name)
        assert not prog.begun, name
        prog.nc.gpsimd.sem_inc(self.sem, unit)
        prog.sems.append(self)

    def value(self, count):
        v = count
        for turn, per_turn in self.prog.loops:
            if per_turn.get(self.name, 0):
                v = turn * per_turn[self.name] + v
        return v

    def add(self, ins, n=1):
        ins.then_inc(self.sem, n)
        self.count += n
        return (self, self.count)

    def now(self):
        return (self, self.count)


class Engine:

    def __init__(self, prog, eng, name):
        self.prog, self.eng, self.name = prog, eng, name
        self.done = Sem(prog, "done_" + name)

    def wait(self, *tokens):
        for t in tokens:
            if t is None:
                continue
            if isinstance(t, list):
                self.wait(*t)
            elif not (isinstance(t[1], int) and t[1] <= 0 and not self.prog.loops):
                self.eng.wait_ge(t[0].sem, t[0].value(t[1]))

    def do(self, op, *args, after=(), chain=True, **kw):
        if chain:
            self.wait(self.done.now())
        self.wait(*after)
        return self.done.add(op(*args, **kw))


class Program:
    def __init__(self, nc, per_turn, dumps=()):
        self.begun = False
        self.nc, self.sems, self.loops, self.per_turn, self.seen = nc, [], [], per_turn, {}
        self.pe = Engine(self, nc.tensor, "pe")
        self.dve = Engine(self, nc.vector, "dve")
        self.act = Engine(self, nc.scalar, "act")
        self.pool = Engine(self, nc.gpsimd, "pool")
        keys = ["inputs", "kdup", "ssm_in", "ctx", "mixer_in", "hy_in", "out"] + ["st%d" % m for m in range(4)]
        self.dma_sems = {k: Sem(self, "dma_" + k, 16) for k in keys + list(dumps)}
        self.relu_done = [Sem(self, f"relu{m}") for m in range(4)]
        self.gate_in = [Sem(self, f"gate_in{m}", 16) for m in range(8)]

    def begin(self):
        ready = self.nc.alloc_semaphore("ready")
        self.nc.gpsimd.sem_inc(ready, 1)
        for eng in (self.nc.tensor, self.nc.vector, self.nc.scalar, self.nc.sync, self.nc.gpsimd):
            eng.wait_ge(ready, 1)
        self.begun = True

    @contextmanager
    def loop(self, n, name):
        start = {s.name: s.count for s in self.sems}
        with self.nc.Fori(0, n) as turn:
            self.loops.append((turn, self.per_turn.get(name, {})))
            yield turn
            self.loops.pop()
        made = {s.name: s.count - start.get(s.name, 0) for s in self.sems}
        assert name not in self.seen, name
        self.seen[name] = made
        for s in self.sems:
            s.count = start.get(s.name, 0) + n * made[s.name]

    def dma(self, engine, key, out, in_, after=()):
        engine.wait(*after)
        return self.dma_sems[key].add(engine.eng.dma_start(out, in_), 16)

    def join(self, *more):
        engines = (self.pe, self.dve, self.act, self.pool)
        tokens = [e.done.now() for e in engines]
        for e in engines:
            e.wait(*tokens, *more)


class Gemm:

    SLOTS, KPER, COLS, BANKS = 8, 2, 512, 4

    def __init__(self, prog):
        nc = prog.nc
        self.prog = prog
        self.ring = nc.alloc_sbuf_tensor("weights_ring", [P, self.SLOTS, self.KPER, self.COLS], F32)
        self.psum = [nc.alloc_psum_tensor(f"acc{m}", [P, 512], F32) for m in range(self.BANKS)]
        self.sp = Engine(prog, nc.sync, "sp")
        self.arrived = [Sem(prog, f"arrived{s}", 16) for s in range(self.SLOTS)]
        self.consumed = [Sem(prog, f"consumed{s}") for s in range(self.SLOTS)]
        self.summed = [Sem(prog, f"summed{m}") for m in range(self.BANKS)]
        self.drained = [Sem(prog, f"drained{m}") for m in range(self.BANKS)]

    def run(self, name, weights, kchunks, ncols, moving, tokens, evacuate, after=(), groups=1):
        prog, sp, pe = self.prog, self.sp, self.prog.pe
        w = weights.rearrange("(c p) n -> p c n", p=P)
        pe.wait(*after)
        slots = kchunks // self.KPER
        assert (groups * slots) % self.SLOTS == 0 and ncols % (self.COLS * groups) == 0, name
        with prog.loop(ncols // self.COLS // groups, name) as turn:
            for g in range(groups):
                group = turn * groups + g
                sums = {}
                for s in range(slots):
                    slot = (g * slots + s) % self.SLOTS
                    sp.wait(self.consumed[slot].now())
                    src = w[:, s * self.KPER:(s + 1) * self.KPER, ds(group * self.COLS, self.COLS)]
                    self.arrived[slot].add(sp.eng.dma_start(self.ring[:, slot, :, :], src), 16)
                    pe.wait(self.arrived[slot].now())
                    for m in range(self.BANKS):
                        if s == 0:
                            pe.wait(self.drained[m].now())
                        for k in range(self.KPER):
                            kc = s * self.KPER + k
                            mm = pe.eng.matmul(
                                self.psum[m][:, 0:tokens],
                                self.ring[:, slot, k, m * P:(m + 1) * P],
                                moving(kc),
                                start=kc == 0, stop=kc == kchunks - 1)
                            if m == self.BANKS - 1 and k == self.KPER - 1:
                                sums[m] = self.consumed[slot].add(mm)
                            elif kc == kchunks - 1:
                                sums[m] = self.summed[m].add(mm)
                for m in range(self.BANKS):
                    evacuate(group * self.BANKS + m, m, self.psum[m][:, 0:tokens], sums[m])


def layout_params(i):
    def col(v):
        return np.ascontiguousarray(np.asarray(v).reshape(-1, P).T)

    def every(v):
        v = np.asarray(v).reshape(1, -1)
        return np.broadcast_to(v, (P, v.shape[1]))

    def twice(v):
        v = np.asarray(v).T
        return np.concatenate([v, v], axis=0)

    parts = {
        "norm_mix_g": col(i["norm_mix_g"]),
        "norm_mlp_g": col(i["norm_mlp_g"]),
        "qk_g": np.concatenate(
            [np.repeat(np.tile(i["q_norm_g"][0], 2)[:, None], 8, 1),
             np.repeat(np.tile(i["k_norm_g"][0], 2)[:, None], 2, 1)], axis=1),
        "sinks": every(i["attn_sinks"]),
        "attn_out_g": col(i["attn_out_g"]),
        "ssm_out_g": col(i["ssm_out_g"]),
        "b_glu": col(i["b_glu"]),
        "ssm_d": col(i["ssm_d"]),
        "lam_re": twice(i["ssm_lambda_re"][0]),
        "lam_im": twice(i["ssm_lambda_im"][0]),
        "log_step": every(i["ssm_log_step"]),
        "c": np.stack([i["c_2"][0].reshape(KD, P).T, i["c_ctx_2"].reshape(KD, P).T], axis=2).reshape(P, -1),
        "b_ada": col(i["b_ada_2"]),
        "lb_logits": col(i["hg_lb_logits_2"]),
        "hg_norm_w": col(i["hg_norm_w_2"]),
        "dn_norm_w": col(i["dn_norm_w_2"]),
        "dn_conv_q": col(i["dn_conv_q_2"]),
        "dn_conv_k": col(i["dn_conv_k_2"]),
        "dn_conv_v": col(i["dn_conv_v_2"]),
        "a_log": every(i["dn_a_log_2"]),
        "dt_bias": every(i["dn_dt_bias_2"]),
        "hy_conv_w": col(i["hy_conv_w_2"]),
        "hy_conv_b": col(i["hy_conv_b_2"]),
        "hy_b1": np.tile(i["hy_filt_b1_2"][0], 2)[:, None],
        "hy_b2": np.tile(i["hy_filt_b2_2"][0], 2)[:, None],
        "ln1_g": col(i["ln1_g_2"]), "ln1_b": col(i["ln1_b_2"]),
        "ln2_g": col(i["ln2_g_2"]), "ln2_b": col(i["ln2_b_2"]),
    }
    offsets, at = {}, 0
    for k, v in parts.items():
        offsets[k] = (at, at + v.shape[1])
        at += v.shape[1]
    return np.ascontiguousarray(np.concatenate(list(parts.values()), axis=1), dtype=np.float32), offsets


def layout_ssm(i):
    br, bi = (np.asarray(i[n][0]).transpose(0, 2, 1).reshape(8, P, 64) for n in ("ssm_b_re", "ssm_b_im"))
    cr, ci = (np.asarray(i[n][0]).transpose(2, 0, 1) for n in ("ssm_c_re", "ssm_c_im"))
    return {
        "ssm_b1": np.ascontiguousarray(np.concatenate([br, bi], axis=2).transpose(1, 0, 2)),
        "ssm_b2": np.ascontiguousarray(np.concatenate([bi, br], axis=2).transpose(1, 0, 2)),
        "ssm_cr": np.ascontiguousarray(np.concatenate([cr, cr], axis=0)),
        "ssm_ci": np.ascontiguousarray(np.concatenate([ci, ci], axis=0)),
    }


def constants():
    c = {}
    p = np.arange(P)
    c["ident"] = np.eye(P)
    c["ones"] = np.ones((P, P))
    c["ones_heads"] = np.kron(np.eye(2), np.ones((HD, HD)))
    t = np.arange(L)
    dist = np.zeros((P, 2, L))
    for q in range(2):
        tq = NMETA + P * q + p[:, None]
        d = tq - t[None, :]
        seen = (d >= 0) & ((d < 128) | (t[None, :] < NMETA))
        dist[:, q] = np.where(seen, np.abs(d), 1e33)
    c["dist"] = dist.reshape(P, -1)
    c["slopes"] = np.broadcast_to(-np.exp2(-8.0 * np.arange(1, NH + 1) / NH), (P, NH))
    c["steps"] = np.broadcast_to(t, (P, L))
    c["group_mask"] = (p[:, None] // 16 == np.arange(8)[None]).astype(float)
    i, j = p[:, None], p[None, :]
    masks = np.zeros((2, 7, P, P))
    for level in range(7):
        half = P >> (level + 1)
        joins = (i // (2 * half) == j // (2 * half)) & (i // half % 2 == 0) & (j // half % 2 == 1)
        masks[0, level], masks[1, level] = joins, joins.T
    c["masks"] = masks.transpose(2, 0, 1, 3).reshape(P, -1)
    c["upto"] = np.concatenate([i <= j, i >= j], axis=1).astype(float)
    c["half_pi"] = np.full((P, 1), np.pi / 2)
    c["top"] = np.where(p < 64, 1.0, -1.0)[:, None]
    offsets, at = {}, 0
    for k, v in c.items():
        offsets[k] = (at, at + v.shape[1])
        at += v.shape[1]
    return np.ascontiguousarray(np.concatenate(list(c.values()), axis=1), dtype=np.float32), offsets


def fourier():
    n = 2 * T
    t, f = np.arange(T)[:, None], np.arange(T)[None, :]
    ang = 2 * np.pi * ((t * f) % n) / n
    re, im = np.cos(ang), -np.sin(ang)
    im[:, 0] = (-1.0) ** t[:, 0]
    back_re, back_im = 2 * re.T / n, 2 * im.T / n
    back_re[0] /= 2
    back_im[0] /= 2
    m = np.stack([re, im, back_re, back_im])
    return np.ascontiguousarray(m.reshape(4, 2, P, T).transpose(2, 0, 1, 3).reshape(P, 4, 2 * T), dtype=np.float32)


def filter_features():
    bands = 16
    t = np.linspace(0, 1, T)
    ang = 2 * np.pi / T * np.arange(T)
    b = np.linspace(1e-4, bands - 1, bands)[:, None]
    feats = np.concatenate([t[None], np.cos(b * ang), -np.sin(b * ang)])
    deltas = np.abs(np.linspace(np.log(1e-2) / 1.5, np.log(1e-2) / 0.3, 1024))
    window = np.exp(-t[:, None] * deltas).reshape(2, P, 1024).transpose(1, 0, 2)
    return feats.astype(np.float32), np.ascontiguousarray(window, dtype=np.float32)


class Arena:

    def __init__(self, tensor, size):
        self.tensor, self.size, self.at = tensor, size, 0

    def reset(self, at=0):
        self.at = at

    def take(self, *dims):
        n = int(np.prod(dims))
        assert self.at + n <= self.size, (self.at, n, self.size)
        v = self.tensor[:, self.at:self.at + n]
        self.at += n
        if len(dims) == 2:
            v = v.rearrange("p (a b) -> p a b", b=dims[1])
        if len(dims) == 3:
            v = v.rearrange("p (a b c) -> p a b c", b=dims[1], c=dims[2])
        return v


ARENA = 22000
ALPHA = 2 ** 0.25
LN_1E30 = float(30 * np.log(10.0))


class Chain:

    def __init__(self, tokens):
        self.last = tokens

    def __call__(self, engine, op, *args, **kw):
        self.last = [engine.do(op, *args, after=self.last, chain=False, **kw)]


def lockstep(strands):
    strands = list(strands)
    while strands:
        for s in list(strands):
            try:
                next(s)
            except StopIteration:
                strands.remove(s)


class Kernel:
    def __init__(self, nc, io, per_turn, pofs, cofs, stop=None):
        self.nc, self.io, self.stop = nc, io, stop
        self.prog = pr = Program(nc, per_turn, ["dump_" + k for k in io] if stop else ())
        self.pe, self.dve, self.act, self.pool = pr.pe, pr.dve, pr.act, pr.pool
        self.gemm = Gemm(pr)
        pr.begin()
        self.bank = [nc.alloc_psum_tensor(f"bank{b}", [P, 512], F32) for b in range(4)]
        pn = max(b for a, b in pofs.values())
        cn = max(b for a, b in cofs.values())
        self.params = nc.alloc_sbuf_tensor("params_sb", [P, pn], F32)
        self.consts = nc.alloc_sbuf_tensor("consts_sb", [P, cn], F32)
        self.pofs, self.cofs = pofs, cofs
        self.res = nc.alloc_sbuf_tensor("residual", [P, KD, L], F32)
        self.xin = nc.alloc_sbuf_tensor("moving", [P, KD, 512], F32)
        self.mix = nc.alloc_sbuf_tensor("mixed", [P, 16, T], F32)
        self.rstd = nc.alloc_sbuf_tensor("rstd", [P, L], F32)
        masks = self.c("masks").rearrange("p (r l t) -> p r l t", r=2, l=7)
        self.masks = [masks[:, r] for r in range(2)]
        self.upto = [self.c("upto")[:, P * r:P * r + P] for r in range(2)]
        self.mods = nc.alloc_sbuf_tensor("mods", [P, 96, 2], F32)
        small = nc.alloc_sbuf_tensor("small", [P, 64], F32)
        self.cc, self.cc_sig = small[:, 0:32], small[:, 32:64]
        self.ab = nc.alloc_sbuf_tensor("ab", [P, 4, 32], F32)
        self.whole_i32 = nc.alloc_sbuf_tensor("whole_i32", [P, 64], I32)[:, :]
        self.arena = Arena(nc.alloc_sbuf_tensor("arena", [P, ARENA], F32), ARENA)

    def p(self, name):
        a, b = self.pofs[name]
        return self.params[:, a:b]

    def c(self, name):
        a, b = self.cofs[name]
        return self.consts[:, a:b]


    def rsqrt(self, out, src, scale, eps, after=()):
        d, a = self.dve, self.act
        t = d.do(d.eng.tensor_scalar, out, src, scale, eps, ALU.mult, ALU.add, after=after)
        t = a.do(a.eng.activation, out, out, ACT.Sqrt, after=[t])
        return d.do(d.eng.reciprocal, out, out, after=[t])

    def feature_rms(self, name, src, chunks, n, eps, squares, bank):
        pe, a = self.pe, self.act
        t = a.do(a.eng.activation, squares, src, ACT.Square)
        pe.wait(t)
        for c in range(chunks):
            mm = pe.eng.matmul(bank[:, 0:n], self.c("ones"), squares[:, c, :], start=c == 0, stop=c == chunks - 1)
        t = pe.done.add(mm)
        return self.rsqrt(self.rstd[:, 0:n], bank[:, 0:n], 1.0 / (chunks * P), eps, after=[t])

    def normalise(self, name, src, gain, dst, chunks, n):
        d = self.dve
        for c in range(chunks):
            t = d.do(d.eng.scalar_tensor_tensor, dst[:, c, 0:n], src[:, c, :], gain[:, c:c + 1],
                     self.rstd[:, 0:n], ALU.mult, ALU.mult, chain=c == 0)
        return t

    def exp_precise(self, dst, src, whole, tmp):
        d = self.dve

        def ts(o, i, s1, s2, a, b):
            return d.do(d.eng.tensor_scalar, o, i, s1, s2, a, b)
        ts(tmp, src, 88.0, -87.0, ALU.min, ALU.max)
        ts(dst, tmp, 1.4426950408889634, MAGIC, ALU.mult, ALU.add)
        ts(dst, dst, -MAGIC, None, ALU.add, ALU.bypass)
        d.do(d.eng.scalar_tensor_tensor, tmp, dst, -0.693359375, tmp, ALU.mult, ALU.add)
        d.do(d.eng.scalar_tensor_tensor, tmp, dst, 2.12194440e-4, tmp, ALU.mult, ALU.add)
        ts(whole, dst, 127.0, 8388608.0, ALU.add, ALU.mult)
        coef = [1.0 / 5040, 1.0 / 720, 1.0 / 120, 1.0 / 24, 1.0 / 6, 0.5, 1.0]
        ts(dst, tmp, coef[0], coef[1], ALU.mult, ALU.add)
        for cf in coef[2:]:
            d.do(d.eng.tensor_tensor, dst, dst, tmp, ALU.mult)
            ts(dst, dst, cf, None, ALU.add, ALU.bypass)
        d.do(d.eng.tensor_tensor, dst, dst, tmp, ALU.mult)
        ts(dst, dst, 1.0, None, ALU.add, ALU.bypass)
        return d.do(d.eng.tensor_tensor, dst, dst, whole.bitcast(F32), ALU.mult)

    def copy(self, out, src):
        return self.dve.eng.tensor_scalar(out, src, 1.0, None, ALU.mult, ALU.bypass)

    def dump(self, name, src, after=()):
        if self.stop and name in self.io:
            self.prog.join()
            self.prog.join(self.prog.dma(self.act, "dump_" + name, self.io[name], src))


    def load_inputs(self):
        pr, io = self.prog, self.io
        t = [pr.dma(self.act, "inputs", self.params[:, :], io["params"]),
             pr.dma(self.act, "inputs", self.consts[:, :], io["consts"]),
             pr.dma(self.act, "inputs", self.res[:, :, :], io["hT"].rearrange("(c p) t -> p c t", p=P))]
        pr.join(t[-1])

    def block1_project(self):
        d, a, g = self.dve, self.act, self.gemm
        self.arena.reset()
        self.pj = self.arena.take(20, L)
        squares = self.arena.take(KD, L)
        self.feature_rms("rms1", self.res[:, :, :], KD, L, 1e-6, squares, self.bank[0])
        t = self.normalise("norm1", self.res[:, :, :], self.p("norm_mix_g"), self.xin[:, :, :], KD, L)

        def evacuate(chunk, m, psum, summed):
            d.wait(summed)
            g.drained[m].add(self.copy(self.pj[:, ds(chunk, 1), :], psum))
        g.run("w_in", self.io["w_in"], KD, 2560, lambda kc: self.xin[:, kc, 0:L], L, evacuate, after=[t])
        self.join_gemm()
        self.dump("pj", self.pj)

    def join_gemm(self):
        self.prog.join(*[s.now() for s in self.gemm.drained])

    def attention(self):
        nc, d, a, pe, pr = self.nc, self.dve, self.act, self.pe, self.prog
        pj, ar, bank = self.pj, self.arena, self.bank
        ar.reset(20 * L)
        sq = ar.take(L)
        rs = ar.take(L)
        with pr.loop(10, "qk_norm") as c:
            t = d.do(d.eng.tensor_tensor, sq, pj[:, ds(c, 1), :], pj[:, ds(c, 1), :], ALU.mult, after=[pe.done.now()])
            t = pe.do(pe.eng.matmul, bank[0][:, 0:L], self.c("ones_heads"), sq, start=True, stop=True,
                      after=[t, d.done.now()])
            self.rsqrt(rs, bank[0][:, 0:L], 1.0 / HD, 1e-6, after=[t])
            d.do(d.eng.scalar_tensor_tensor, pj[:, ds(c, 1), :], pj[:, ds(c, 1), :],
                 self.p("qk_g")[:, ds(c, 1)], rs, ALU.mult, ALU.mult)
        pr.join()
        kdup = ar.take(NKV, L)
        for dst in range(2):
            for par in range(2):
                t_k = pr.dma(a, "kdup", kdup[64 * dst:64 * dst + 64, par::2, :],
                             pj[64 * par:64 * par + 64, 8:10, :])
        vt = ar.take(3, NKV * P)
        keys = [(0, 128), (128, 128), (256, 16)]
        for kt, (k0, kn) in enumerate(keys):
            for c in range(2):
                b = bank[(2 * kt + c) % 4]
                t = pe.do(pe.eng.transpose, b[0:kn, 0:P], pj[:, 10 + c, k0:k0 + kn], self.c("ident"),
                          after=[d.done.now()])
                dst = vt[0:kn, kt, 2 * P * c:2 * P * (c + 1)].rearrange("p (a b d) -> p a b d", a=2, b=2)
                for twin in range(2):
                    d.do(d.eng.tensor_copy, dst[:, :, twin, :],
                         b[0:kn, 0:P].rearrange("p (a d) -> p a d", a=2), after=[t])
        self.attn = ar.take(8, T)
        qs = ar.take(2, T)
        ks = ar.take(L)
        vs = ar.take(3, P)
        s = ar.take(2, L)
        st = ar.take(2, 8)
        pt = ar.take(2, 3 * P)
        dist = self.c("dist").rearrange("p (q t) -> p q t", q=2)
        pr.join(t_k)
        with pr.loop(NKV, "attention") as kv:
            t_q = d.do(d.eng.tensor_scalar, qs, pj[:, ds(kv * 2, 2), NMETA:L], HD ** -0.5, None,
                       ALU.mult, ALU.bypass, after=[pe.done.now()])
            d.do(self.copy, ks, kdup[:, ds(kv, 1), :])
            t_k = d.do(self.copy, vs[:, 0:2, :], vt[:, 0:2, ds(kv * P, P)])
            t_k = d.do(self.copy, vs[0:16, 2, :], vt[0:16, 2, ds(kv * P, P)])
            prev = [None, None]
            for u in range(8):
                hh, qt, b = u // 2, u % 2, u % 2
                half = 64 * (hh % 2)
                ps_s, ps_o = bank[b], bank[2 + b]
                t = pe.do(pe.eng.matmul, ps_s[:, 0:L], qs[half:half + 64, hh // 2, P * qt:P * qt + P],
                          ks[half:half + 64, :], start=True, stop=True, after=[t_k, prev[b]])
                d.do(d.eng.scalar_tensor_tensor, s[:, b, :], dist[:, qt, :], self.c("slopes")[:, ds(kv * 4 + hh, 1)],
                     ps_s[:, 0:L], ALU.mult, ALU.add, after=[t])
                m, nm, z, es, r = (st[:, b, k:k + 1] for k in range(5))
                sink = self.p("sinks")[:, ds(kv * 4 + hh, 1)]
                d.do(d.eng.reduce_max, m, s[:, b, :], AX.X)
                snk = st[:, b, 5:6]
                d.do(self.copy, snk, sink)
                t = d.do(d.eng.tensor_scalar, nm, m, sink, -1.0, ALU.max, ALU.mult)
                a.do(a.eng.activation, s[:, b, :], s[:, b, :], ACT.Exp, bias=nm, accum_out=z, after=[t])
                t = a.do(a.eng.activation, es, snk, ACT.Exp, bias=nm)
                d.do(d.eng.tensor_tensor, z, z, es, ALU.add, after=[t])
                d.do(d.eng.reciprocal, r, z)
                t = d.do(d.eng.tensor_scalar, s[:, b, :], s[:, b, :], r, None, ALU.mult, ALU.bypass)
                pe.wait(t)
                for kt, (k0, kn) in enumerate(keys):
                    mm = pe.eng.transpose(ps_s[0:kn, P * kt:P * kt + P], s[:, b, k0:k0 + kn], self.c("ident"))
                t = pe.done.add(mm)
                d.do(d.eng.tensor_copy, pt[:, b, 0:2 * P], ps_s[:, 0:2 * P], after=[t])
                t = d.do(d.eng.tensor_copy, pt[0:16, b, 2 * P:], ps_s[0:16, 2 * P:3 * P])
                pe.wait(t)
                for kt, (k0, kn) in enumerate(keys):
                    mm = pe.eng.matmul(ps_o[:, 0:P], vs[0:kn, kt, :], pt[0:kn, b, P * kt:P * kt + P],
                                       start=kt == 0, stop=kt == 2)
                t = pe.done.add(mm)
                prev[b] = d.do(self.copy, self.attn[half:half + 64, ds(kv * 2 + hh // 2, 1), P * qt:P * qt + P],
                               ps_o[half:half + 64, 0:P], after=[t])
        pr.join()
        self.dump("attn", self.attn)
        sq = ar.take(8, T)
        self.feature_rms("rms_attn", self.attn, 8, T, 1e-6, sq, bank[0])
        self.normalise("norm_attn", self.attn, self.p("attn_out_g"), self.mix[:, :, :], 8, T)
        pr.join()

    def ssm(self):
        d, a, pe, pr, bank, io = self.dve, self.act, self.pe, self.prog, self.bank, self.io
        pj, ar, g = self.pj, self.arena, self.gemm
        G, S, N = 64, 64, 16
        ar.reset(20 * L)
        lre, lim = self.p("lam_re"), self.p("lam_im")
        p1, p2 = ar.take(G), ar.take(G)
        r, turns = ar.take(G), ar.take(G)
        b1, b2 = ar.take(8, P), ar.take(8, P)
        l1, l2 = ar.take(G, N), ar.take(G, N)
        keep = ar.at
        t_in = [pr.dma(a, "ssm_in", b1, io["ssm_b1"]), pr.dma(a, "ssm_in", b2, io["ssm_b2"])]
        t0, t1, t2, t3, t4, t5, whole = (ar.take(G) for _ in range(7))
        cr, ci, tc = ar.take(G, N), ar.take(G, N), ar.take(G, N)
        t_in += [pr.dma(a, "ssm_in", cr, io["ssm_cr"]), pr.dma(a, "ssm_in", ci, io["ssm_ci"])]

        def ts(o, x, s1, s2, o1, o2=ALU.bypass, after=()):
            return d.do(d.eng.tensor_scalar, o, x, s1, s2, o1, o2, after=after)

        def tt(o, x, y, op, after=()):
            return d.do(d.eng.tensor_tensor, o, x, y, op, after=after)
        wh = self.whole_i32
        self.exp_precise(t0, self.p("log_step"), wh, t1)
        tt(t1, lre, t0, ALU.mult)
        self.exp_precise(r, t1, wh, t2)
        tt(t1, lim, t0, ALU.mult)
        ts(turns, t1, 1.0 / (2 * np.pi), MAGIC, ALU.mult, ALU.add)
        ts(turns, turns, -MAGIC, None, ALU.add)
        for part in (6.28125, 1.9350051879882812e-3, 3.0199159819e-7):
            d.do(d.eng.scalar_tensor_tensor, t1, turns, -part, t1, ALU.mult, ALU.add)
        ts(turns, t1, 1.0 / (2 * np.pi), 0.5, ALU.mult, ALU.min)
        ts(turns, turns, -0.5, None, ALU.max)
        a.do(a.eng.activation, t2, turns, ACT.Sin, scale=TWO_PI_BELOW, after=[d.done.now()])
        t = a.do(a.eng.activation, t3, turns, ACT.Sin, scale=TWO_PI_BELOW / 2)
        tt(t3, t3, t3, ALU.mult, after=[t])
        ts(t3, t3, -2.0, None, ALU.mult)
        tt(t2, t2, r, ALU.mult)
        tt(t3, t3, r, ALU.mult)
        ts(t4, r, -1.0, None, ALU.add)
        tt(t3, t3, t4, ALU.add)
        tt(t4, lre, lre, ALU.mult)
        tt(t5, lim, lim, ALU.mult)
        tt(t4, t4, t5, ALU.add)
        d.do(d.eng.reciprocal, t4, t4)
        tt(t0, t3, lre, ALU.mult)
        tt(t5, t2, lim, ALU.mult)
        tt(t0, t0, t5, ALU.add)
        tt(t0, t0, t4, ALU.mult)
        tt(t1, t2, lre, ALU.mult)
        tt(t5, t3, lim, ALU.mult)
        tt(t1, t1, t5, ALU.subtract)
        tt(t1, t1, t4, ALU.mult)
        d.do(d.eng.tensor_copy, p1[0:64, :], t0[0:64, :])
        d.do(d.eng.tensor_scalar, p1[64:, :], t1[64:, :], -1.0, None, ALU.mult, ALU.bypass)
        d.do(d.eng.tensor_scalar, p2[0:64, :], t1[0:64, :], -1.0, None, ALU.mult, ALU.bypass)
        d.do(d.eng.tensor_scalar, p2[64:, :], t0[64:, :], -1.0, None, ALU.mult, ALU.bypass)
        p1b = p1.unsqueeze(2).broadcast_to((P, G, N))
        p2b = p2.unsqueeze(2).broadcast_to((P, G, N))
        tt(l1, cr, p1b, ALU.mult, after=[t_in[-1]])
        tt(tc, ci, p2b, ALU.mult)
        tt(l1, l1, tc, ALU.add)
        tt(l2, cr, p2b, ALU.mult)
        tt(tc, ci, p1b, ALU.mult)
        tt(l2, l2, tc, ALU.subtract)
        ts(b2[:, :, 64:], b2[:, :, 64:], -1.0, None, ALU.mult)
        pr.join()

        ar.reset(keep)
        lb1, lb2 = ar.take(8, P), ar.take(8, P)
        lp1, lp2 = ar.take(8 * (P + N)), ar.take(8 * (P + N))
        w, cs, sn = ar.take(8, L), ar.take(8, L), ar.take(8, L)
        z = w
        t_u = ar.take(L)
        y = self.mix[:, 8:16, :]
        for lp in (lp1, lp2):
            d.do(d.eng.memset, lp, 0.0)
        mask = self.c("group_mask").unsqueeze(2).broadcast_to((P, 8, P))
        steps = self.c("steps")
        blocks1 = lp1.rearrange("p (j x) -> p j x", x=P + N)[:, :, 0:N]
        blocks2 = lp2.rearrange("p (j x) -> p j x", x=P + N)[:, :, 0:N]
        pr.join()
        with pr.loop(8, "ssm") as c:
            pe_before = pe.done.now()
            d.wait(pe_before)
            tt(lb1, b1[:, ds(c, 1), :].broadcast_to((P, 8, P)), mask, ALU.mult)
            tt(lb2, b2[:, ds(c, 1), :].broadcast_to((P, 8, P)), mask, ALU.mult)
            d.do(self.copy, blocks1, l1[:, ds(c * 8, 8), :])
            d.do(self.copy, blocks2, l2[:, ds(c * 8, 8), :])
            t_w = d.do(self.copy, t_u, pj[:, ds(12 + c, 1), :])
            for j in range(8):
                t = d.do(d.eng.tensor_scalar, w[:, j, :], steps, turns[:, ds(c * 8 + j, 1)], None,
                         ALU.mult, ALU.bypass, chain=j == 0)
            ts(cs, w, MAGIC, -MAGIC, ALU.add, ALU.add)
            t = tt(w, w, cs, ALU.subtract)
            t_s = a.do(a.eng.activation, sn, w, ACT.Sin, scale=TWO_PI_BELOW, after=[t])
            t = d.do(d.eng.scalar_tensor_tensor, w, w, -1.0, w, ALU.mult, ALU.max, after=[t_s])
            t_s = a.do(a.eng.activation, cs, w, ACT.Sin, scale=-TWO_PI_BELOW, bias=self.c("half_pi"), after=[t])
            pe.wait(t_w)
            freed = [None, None]
            for j in range(8):
                b = j % 2
                pe.do(pe.eng.matmul, bank[2 * b][:, 0:L], lb1[:, j, :], t_u, start=True, stop=True, after=[freed[b]], chain=False)
                t = pe.do(pe.eng.matmul, bank[2 * b + 1][:, 0:L], lb2[:, j, :], t_u, start=True, stop=True, chain=False)
                d.wait(t)
                d.do(d.eng.tensor_tensor, w[:, j, :], cs[:, j, :], bank[2 * b][:, 0:L], ALU.mult, after=[t_s])
                freed[b] = d.do(d.eng.tensor_tensor, self.rstd[:, 0:L], sn[:, j, :], bank[2 * b + 1][:, 0:L], ALU.mult)
                tt(w[:, j, :], w[:, j, :], self.rstd[:, 0:L], ALU.add)
                d.do(d.eng.tensor_tensor_scan, w[:, j, :], self.rcol(r, c * 8 + j), w[:, j, :], 0.0, ALU.mult, ALU.add)
            tt(cs, cs, z, ALU.mult)
            t = tt(sn, sn, z, ALU.mult)
            pe.wait(t)
            for j in range(8):
                pe.eng.matmul(bank[0][:, 0:L], lp1[:, P * j:P * j + P], cs[:, j, :], start=j == 0, stop=False)
                mm = pe.eng.matmul(bank[0][:, 0:L], lp2[:, P * j:P * j + P], sn[:, j, :], start=False, stop=j == 7)
            t = pe.done.add(mm)
            d.do(d.eng.tensor_scalar, t_u, t_u, self.p("ssm_d")[:, ds(c, 1)], None, ALU.mult, ALU.bypass, after=[t])
            tt(y[:, ds(c, 1), :], t_u[:, NMETA:], bank[0][:, NMETA:L], ALU.add)
        pr.join()
        self.dump("y", y)
        ar.reset(20 * L)
        t3, gl, gate = ar.take(8, T), ar.take(8, T), ar.take(8, T)
        tt(t3, y, y, ALU.mult)
        ts(t3, t3, 0.044715, 1.0, ALU.mult, ALU.add)
        t = tt(t3, t3, y, ALU.mult)
        t = a.do(a.eng.activation, t3, t3, ACT.Sigmoid, scale=2 * np.sqrt(2 / np.pi), after=[t])
        t = tt(gl, y, t3, ALU.mult, after=[t])

        def evacuate(chunk, m, psum, summed):
            d.wait(summed)
            g.drained[m].add(d.eng.tensor_scalar(gate[:, ds(chunk, 1), :], psum, self.p("b_glu")[:, ds(chunk, 1)],
                                                 None, ALU.add, ALU.bypass))
        g.run("w_glu", io["w_glu"], 8, 1024, lambda kc: gl[:, kc, :], T, evacuate, after=[t], groups=2)
        self.join_gemm()
        t = a.do(a.eng.activation, gate, gate, ACT.Sigmoid)
        t = tt(gl, gl, gate, ALU.mult, after=[t])
        pr.join()
        self.dump("ssm", gl)
        self.feature_rms("rms_ssm", gl, 8, T, 1e-6, t3, bank[0])
        self.normalise("norm_ssm", gl, self.p("ssm_out_g"), self.mix[:, 8:16, :], 8, T)
        pr.join()

    def rcol(self, r, col):
        return r[:, ds(col, 1)].broadcast_to((P, L))

    def add_to_residual(self, dst):
        d, g = self.dve, self.gemm

        def evacuate(chunk, m, psum, summed):
            d.wait(summed)
            g.drained[m].add(d.eng.tensor_tensor(dst[:, ds(chunk, 1), :], dst[:, ds(chunk, 1), :], psum, ALU.add))
        return evacuate

    def squared_relu(self, hid):
        d, a, g, pr = self.dve, self.act, self.gemm, self.prog

        def evacuate(chunk, m, psum, summed):
            tmp = self.sq_tmp[:, m, :]
            d.wait(summed)
            t = pr.relu_done[m].add(d.eng.tensor_scalar(tmp, psum, 0.0, None, ALU.max, ALU.bypass))
            d.wait(t)
            g.drained[m].add(d.eng.tensor_tensor(hid[:, ds(chunk, 1), :], tmp, tmp, ALU.mult))
        return evacuate

    def block1_mlp(self):
        d, g, io, pr = self.dve, self.gemm, self.io, self.prog
        x = self.res[:, :, NMETA:]
        g.run("w_out", io["w_out"], KD, DM, lambda kc: self.mix[:, kc, :], T, self.add_to_residual(x))
        self.join_gemm()
        self.arena.reset()
        hid = self.arena.take(DFF // P, T)
        self.sq_tmp = self.arena.take(4, T)
        self.feature_rms("rms2", x, KD, T, 1e-6, self.mix[:, :, :], self.bank[0])
        t = self.normalise("norm2", x, self.p("norm_mlp_g"), self.xin[:, :, :], KD, T)
        g.run("w_up", io["w_up"], KD, DFF, lambda kc: self.xin[:, kc, 0:T], T, self.squared_relu(hid), after=[t])
        self.join_gemm()
        g.run("w_down", io["w_down"], DFF // P, DM, lambda kc: hid[:, kc, :], T, self.add_to_residual(x))
        self.join_gemm()
        self.dump("blk1", x)


    def modulation(self):
        d, a, g, pr = self.dve, self.act, self.gemm, self.prog
        cc = self.cc
        sig = self.cc_sig
        t = a.do(a.eng.activation, sig, self.p("c"), ACT.Sigmoid)
        t = d.do(d.eng.tensor_tensor, cc, self.p("c"), sig, ALU.mult, after=[t])
        ccv = cc.rearrange("p (c m) -> p c m", m=2)

        def evacuate(chunk, m, psum, summed):
            d.wait(summed)
            g.drained[m].add(d.eng.tensor_scalar(self.mods[:, ds(chunk, 1), :], psum, self.p("b_ada")[:, ds(chunk, 1)],
                                                 None, ALU.add, ALU.bypass))
        g.run("w_ada", self.io["w_ada"], KD, 6 * DM, lambda kc: ccv[:, kc, :], 2, evacuate, after=[t])
        self.join_gemm()
        for c in (16, 64):
            d.do(d.eng.tensor_scalar, self.mods[:, c:c + 16, :], self.mods[:, c:c + 16, :], 1.0, None, ALU.add, ALU.bypass)

    def modulate(self, src, dst, shift, scale, which):
        d = self.dve
        for c in range(KD):
            t = d.do(d.eng.tensor_scalar, dst[:, c, :], src[:, c, :], self.mods[:, scale + c, which:which + 1],
                     self.mods[:, shift + c, which:which + 1], ALU.mult, ALU.add, chain=c == 0)
        return t

    def storing(self, scratch, tokens, key, func=None):
        d, a, g, pr = self.dve, self.act, self.gemm, self.prog
        stage = self.stage
        view = scratch.rearrange("(c p) t -> p c t", p=P)

        def evacuate(chunk, m, psum, summed):
            d.wait(summed, pr.dma_sems["st%d" % m].now())
            t = g.drained[m].add(d.eng.tensor_copy(stage[:, m, 0:tokens], psum))
            if func is not None:
                t = a.do(a.eng.activation, stage[:, m, 0:tokens], stage[:, m, 0:tokens], func, after=[t])
            pr.dma(a, "st%d" % m, view[:, ds(chunk, 1), :], stage[:, m, 0:tokens], after=[t])
        return evacuate

    def block2_project(self):
        d, a, pe, pr, g, io = self.dve, self.act, self.pe, self.prog, self.gemm, self.io
        self.arena.reset()
        self.stage = self.arena.take(4, 512)
        ab_w = self.arena.take(KD, 32)
        x = self.res[:, :, NMETA:]
        ctx = self.xin[:, :, T:]
        pr.join()
        t_in = pr.dma(a, "ctx", ctx, io["ctxT"].rearrange("(c p) t -> p c t", p=P))
        t_ab = pr.dma(a, "ctx", ab_w, io["w_in2"][:, 4608:4640].rearrange("(c p) n -> p c n", p=P))
        self.modulate(x, self.xin[:, :, 0:T], 0, 16, 0)
        d.wait(t_ab)
        t = self.modulate(ctx, ctx, 0, 16, 1)
        pr.join()
        for tt in range(4):
            bank = self.bank[tt]
            for kc in range(KD):
                mm = pe.eng.matmul(bank[:, 0:32], self.xin[:, kc, P * tt:P * tt + P], ab_w[:, kc, :], start=kc == 0, stop=kc == KD - 1)
            t1 = pe.done.add(mm)
            d.do(d.eng.tensor_copy, self.ab[:, tt, :], bank[:, 0:32], after=[t1])
        g.run("w_in2a", io["w_in2"][:, 0:4608], KD, 4608, lambda kc: self.xin[:, kc, :], 2 * T,
              self.storing(io["s_state"], 2 * T, "a"), after=[t])
        g.run("w_in2b", io["w_in2"][:, 4640:4640 + 6656], KD, 6656, lambda kc: self.xin[:, kc, 0:T], T,
              self.storing(io["s_read"], T, "b"))
        g.run("w_in2c", io["w_in2"][:, 11296:], KD, 6144, lambda kc: self.xin[:, kc, 0:T], T,
              self.storing(io["s_gate"], T, "c", ACT.Sigmoid))
        self.join_gemm()
        pr.join(*[pr.dma_sems["st%d" % m].now() for m in range(4)])
        self.branch = self.xin[:, 0:12, :].rearrange("p a b -> p (a b)").rearrange("p (g c t) -> p g c t", g=3, c=8)

    def hgrn2(self):
        d, a, pe, pr, io, ar = self.dve, self.act, self.pe, self.prog, self.io, self.arena
        NT = 4
        C = P + 2
        ar.reset()
        fz, k, e1 = [ar.take(NT, P) for _ in range(2)], [ar.take(NT, P) for _ in range(2)], [ar.take(NT, P) for _ in range(2)]
        cum = [ar.take(NT, C) for _ in range(2)]
        ks, kst = [ar.take(NT, P) for _ in range(2)], [ar.take(NT, P) for _ in range(2)]
        att, qe = [ar.take(2, P) for _ in range(2)], [ar.take(2, P) for _ in range(2)]
        lev = [[ar.take(2, P) for _ in range(2)] for _ in range(2)]
        st = [ar.take(P) for _ in range(2)]
        eend = [ar.take(NT) for _ in range(2)]
        vf, vt, q, gt = ar.take(NT, P), ar.take(NT, P), ar.take(2, P), ar.take(2, P)
        ones = ar.take(P)
        o, sq = ar.take(T), ar.take(T)
        lb = ar.take(2, 8)
        lb1 = ar.take(2, 8)
        state = io["s_state"].rearrange("(c p) t -> p c t", p=P)
        read = io["s_read"].rearrange("(c p) t -> p c t", p=P)
        logits = self.p("lb_logits").rearrange("p (a c) -> p a c", a=2)
        d.do(d.eng.tensor_tensor, lb, logits, logits, ALU.subtract)
        t = a.do(a.eng.activation, lb, lb, ACT.Exp, after=[d.done.now()])
        d.do(d.eng.reciprocal, lb1, lb, after=[t])
        d.do(d.eng.tensor_tensor, lb1, lb1, lb, ALU.mult)
        d.do(d.eng.tensor_tensor, lb, lb1, lb1, ALU.subtract)
        d.do(d.eng.tensor_scalar, lb1, lb, -1.0, 1.0, ALU.mult, ALU.add)
        d.do(d.eng.memset, ones, 1.0)
        for r in range(2):
            d.do(d.eng.memset, cum[r][:, :, 0:1], 0.0)
        pr.join()
        banks = [[self.bank[0], self.bank[1], self.gemm.psum[0]], [self.bank[2], self.bank[3], self.gemm.psum[1]]]
        po = [self.gemm.psum[2], self.gemm.psum[3]]

        def direction(r, h, ch):
            fwd = r == 0
            bl, bs, bt = banks[r]
            f, kk, cm = fz[r], k[r], cum[r]
            lbc, lb1c = lb[:, r, ds(h, 1)], lb1[:, r, ds(h, 1)]
            ch(d, d.eng.tensor_scalar, e1[r], f, -1.0, LN_1E30, ALU.mult, ALU.min)
            yield
            ch(a, a.eng.activation, e1[r], e1[r], ACT.Exp)
            yield
            ch(d, d.eng.tensor_scalar, f, e1[r], 1.0, None, ALU.add, ALU.bypass)
            ch(d, d.eng.reciprocal, f, f)
            ch(d, d.eng.tensor_tensor, kk, e1[r], f, ALU.mult)
            ch(d, d.eng.tensor_scalar, kk, kk, lb1c, None, ALU.mult, ALU.bypass)
            ch(d, d.eng.tensor_scalar, f, f, lb1c, lbc, ALU.mult, ALU.add)
            ch(d, d.eng.tensor_scalar, f, f, 1e-30, None, ALU.max, ALU.bypass)
            ch(d, d.eng.tensor_scalar, ks[r], f, 2.0 ** -50, None, ALU.is_lt, ALU.bypass)
            ch(d, d.eng.tensor_scalar, e1[r], ks[r], 2.0 ** 50 - 1, 1.0, ALU.mult, ALU.add)
            ch(d, d.eng.tensor_tensor, f, f, e1[r], ALU.mult)
            yield
            ch(a, a.eng.activation, f, f, ACT.Ln)
            yield
            ch(d, d.eng.scalar_tensor_tensor, f, ks[r], -50 * float(np.log(2.0)), f, ALU.mult, ALU.add)
            for j in range(NT):
                ch(d, d.eng.tensor_tensor_scan, cm[:, j, 1:P + 1], ones, f[:, j, :], 0.0, ALU.mult, ALU.add)
            after, before, end = cm[:, :, 1:P + 1], cm[:, :, 0:P], cm[:, :, P:P + 1]
            if fwd:
                ch(d, d.eng.tensor_tensor, ks[r], end.broadcast_to((P, NT, P)), after, ALU.subtract)
            else:
                ch(d, d.eng.tensor_copy, ks[r], before)
            yield
            ch(a, a.eng.activation, ks[r], ks[r], ACT.Exp)
            ch(a, a.eng.activation, eend[r], cm[:, :, P], ACT.Exp)
            yield
            ch(d, d.eng.tensor_tensor, ks[r], ks[r], kk, ALU.mult)
            yield
            ch(pe, lambda: [pe.eng.transpose(bt[:, P * j:P * j + P], ks[r][:, j, :], self.c("ident")) for j in range(NT)][-1])
            yield
            ch(d, d.eng.tensor_copy, kst[r], bt[:, :])
            if fwd:
                ch(a, a.eng.activation, qe[r], after[:, 0:2, :], ACT.Exp)
            else:
                ch(d, d.eng.tensor_tensor, qe[r], end[:, 0:2, :].broadcast_to((P, 2, P)), before[:, 0:2, :], ALU.subtract)
                ch(a, a.eng.activation, qe[r], qe[r], ACT.Exp)
            yield
            ch(d, d.eng.tensor_tensor, qe[r], qe[r], q, ALU.mult)
            ch(pe, lambda: [pe.eng.matmul(bs[:, P * j:P * j + P], kk[:, j, :], q[:, j, :], start=True, stop=True) for j in range(2)][-1])
            yield
            ident = self.c("ident").unsqueeze(1).broadcast_to((P, 2, P))
            ch(d, d.eng.tensor_tensor, att[r], bs[:, 0:T].rearrange("p (j t) -> p j t", j=2), ident, ALU.mult)
            for level in range(7):
                half = P >> (level + 1)
                nb = P // (2 * half)
                m = lev[r][level % 2]

                def halves(x):
                    v = x.rearrange("p j (b two n) -> p j b two n", two=2, n=half)
                    return v[:, :, :, 0, :], v[:, :, :, 1, :]
                mid = cm[:, 0:2, 0:P].rearrange("p j (b n) -> p j b n", n=2 * half)[:, :, :, half:half + 1].broadcast_to((P, 2, nb, half))
                c0, c1 = halves((after if fwd else before)[:, 0:2, :])
                m0, m1 = halves(m)
                k0, k1 = halves(kk[:, 0:2, :])
                q0, q1 = halves(q)
                for j in range(2):
                    ch(d, d.eng.tensor_tensor, m0[:, j], mid[:, j], c0[:, j], ALU.subtract)
                    ch(d, d.eng.tensor_tensor, m1[:, j], c1[:, j], mid[:, j], ALU.subtract)
                yield
                ch(a, a.eng.activation, m, m, ACT.Exp)
                yield
                for j in range(2):
                    ch(d, d.eng.tensor_tensor, m0[:, j], m0[:, j], (k0 if fwd else q0)[:, j], ALU.mult)
                    ch(d, d.eng.tensor_tensor, m1[:, j], m1[:, j], (q1 if fwd else k1)[:, j], ALU.mult)
                yield
                ch(pe, lambda: [pe.eng.matmul(bl[:, P * j:P * j + P], m[:, j, :], m[:, j, :], start=True, stop=True) for j in range(2)][-1])
                yield
                mask = self.masks[r][:, level, :].unsqueeze(1).broadcast_to((P, 2, P)).bitcast(mybir.dt.uint32)
                ch(d, self.copy, eend[r][:, 0:1], eend[r][:, 0:1])
                d.do(d.eng.copy_predicated, att[r], mask, bl[:, 0:T].rearrange("p (j t) -> p j t", j=2), chain=False)
                ch.last = [d.done.now()]
                yield
            order = (2, 3, 0, 1) if fwd else (3, 2, 1, 0)
            for n, j in enumerate(order):
                if j < 2:
                    def out():
                        pe.eng.matmul(po[r][:, P * j:P * j + P], vt[:, j, :], att[r][:, j, :], start=True, stop=False)
                        return pe.eng.matmul(po[r][:, P * j:P * j + P], st[r], qe[r][:, j, :], start=False, stop=True)
                    ch(pe, out)
                if n < 3:
                    ch(pe, lambda: pe.eng.matmul(bs[:, 0:P], kst[r][:, j, :], vt[:, j, :], start=True, stop=True))
                    yield
                    if n == 0:
                        ch(d, d.eng.tensor_copy, st[r], bs[:, 0:P])
                    else:
                        ch(d, d.eng.scalar_tensor_tensor, st[r], st[r], eend[r][:, j:j + 1], bs[:, 0:P], ALU.mult, ALU.add)
                    yield

        with pr.loop(8, "hgrn2") as h:
            a.wait(d.done.now(), pe.done.now())
            flat = "p j t -> p (j t)"
            for r in range(2):
                pr.dma(a, "mixer_in", fz[r].rearrange(flat), state[:, ds(h + 8 * r, 1), :])
            pr.dma(a, "mixer_in", vf.rearrange(flat), state[:, ds(h + 16, 1), :])
            pr.dma(a, "mixer_in", q.rearrange(flat), read[:, ds(h, 1), :])
            t = pr.dma(a, "mixer_in", gt.rearrange(flat), read[:, ds(h + 8, 1), :])
            for e in (a, d, pe):
                e.wait(t, a.done.now(), d.done.now(), pe.done.now())
            t = pe.do(lambda: [pe.eng.transpose(po[0][:, P * j:P * j + P], vf[:, j, :], self.c("ident")) for j in range(NT)][-1])
            t_v = d.do(d.eng.tensor_copy, vt, po[0][:, :], after=[t])
            t = a.do(a.eng.activation, sq, q.rearrange(flat), ACT.Sigmoid)
            t_q = d.do(d.eng.tensor_tensor, q.rearrange(flat), q.rearrange(flat), sq, ALU.mult, after=[t])
            t_g = a.do(a.eng.activation, gt, gt, ACT.Sigmoid)
            chains = [Chain([t_q, t_g, t_v]) for _ in range(2)]
            lockstep([direction(r, h, chains[r]) for r in range(2)])
            d.do(d.eng.tensor_copy, sq, po[1][:, 0:T], after=[pe.done.now(), a.done.now()])
            t = d.do(d.eng.tensor_tensor, o, po[0][:, 0:T], sq, ALU.add)
            self.head_norm_gate(o, sq, self.p("hg_norm_w"), gt.rearrange(flat), self.branch[:, 1, ds(h, 1), :], self.bank[0])
        pr.join()
        self.dump("hg", self.branch[:, 1])

    def head_norm_gate(self, o, sq, w, gate, dst, bank):
        d, pe = self.dve, self.pe
        t = d.do(d.eng.tensor_tensor, sq, o, o, ALU.mult)
        t = pe.do(pe.eng.matmul, bank[:, 0:T], self.c("ones"), sq, start=True, stop=True, after=[t])
        self.rsqrt(sq, bank[:, 0:T], 1.0 / P, 1e-6, after=[t])
        d.do(d.eng.scalar_tensor_tensor, o, o, w, sq, ALU.mult, ALU.mult)
        d.do(d.eng.tensor_tensor, dst, o, gate, ALU.mult)

    def conv(self, dst, src, w, at, rows):
        d = self.dve
        y, x = (v.rearrange("p (r n) -> p r n", r=rows) for v in (dst, src))
        n = x.shape[2]
        d.do(d.eng.tensor_scalar, y, x, w(1), None, ALU.mult, ALU.bypass)
        d.do(d.eng.scalar_tensor_tensor, y[:, :, 1:], x[:, :, 0:n - 1], w(0), y[:, :, 1:], ALU.mult, ALU.add)
        return d.do(d.eng.scalar_tensor_tensor, y[:, :, 0:n - 1], x[:, :, 1:], w(2), y[:, :, 0:n - 1], ALU.mult, ALU.add)

    def deltanet(self):
        d, a, pe, pr, io, ar = self.dve, self.act, self.pe, self.prog, self.io, self.arena
        NT, W = 4, 512
        ident = self.c("ident")
        ar.reset()
        kf, qf = ar.take(4, W), ar.take(4, T)
        kt, vt = ar.take(NT, 4 * P), ar.take(NT, 8 * P)
        beta, gl, gc = ar.take(NT, 16), ar.take(NT, 16), ar.take(NT, 16)
        keep = ar.at
        state = io["s_state"].rearrange("(c p) t -> p c t", p=P)
        read = io["s_read"].rearrange("(c p) t -> p c t", p=P)
        raw, y, z = ar.take(W), ar.take(W), ar.take(W)
        pr.join()

        def taps(name, n, c):
            col = self.p(name).rearrange("p (j c) -> p j c", j=3)
            return lambda j: col[:, j, ds(c, 1)]

        def stream(name, rows, n, w_name, wn, tokens, finish):
            with pr.loop(n, name) as c:
                t = pr.dma(a, "mixer_in", raw[:, 0:tokens], rows(c), after=[d.done.now(), pe.done.now()])
                d.wait(t, a.done.now(), pe.done.now())
                t = self.conv(y[:, 0:T], raw[:, 0:T], taps(w_name, wn, c), 0, 4)
                if tokens > T:
                    t = self.conv(y[:, T:], raw[:, T:], taps(w_name, wn, c), 0, 1)
                t = a.do(a.eng.activation, z[:, 0:tokens], y[:, 0:tokens], ACT.Sigmoid, after=[t])
                d.do(d.eng.tensor_tensor, y[:, 0:tokens], y[:, 0:tokens], z[:, 0:tokens], ALU.mult, after=[t])
                finish(c)
            pr.join()

        def unit_length(dst, c, tokens, scale):
            t = d.do(d.eng.tensor_tensor, z[:, 0:tokens], y[:, 0:tokens], y[:, 0:tokens], ALU.mult)
            t = pe.do(pe.eng.matmul, self.bank[0][:, 0:tokens], self.c("ones"), z[:, 0:tokens], start=True, stop=True, after=[t])
            self.rsqrt(z[:, 0:tokens], self.bank[0][:, 0:tokens], 1.0, 1e-6, after=[t])
            t = d.do(d.eng.scalar_tensor_tensor, y[:, 0:tokens], y[:, 0:tokens], scale, z[:, 0:tokens], ALU.mult, ALU.mult)
            d.do(self.copy, dst[:, ds(c, 1), :], y[:, 0:tokens])

        def to_tokens(dst, c):
            t = pe.do(lambda: [pe.eng.transpose(self.bank[1][:, P * j:P * j + P], y[:, P * j:P * j + P], ident) for j in range(NT)][-1],
                      after=[d.done.now()])
            d.do(self.copy, dst[:, :, ds(c * P, P)], self.bank[1][:, :].rearrange("p (j t) -> p j t", j=NT), after=[t])

        def finish_k(c):
            unit_length(kf, c, W, 1.0)
            to_tokens(kt, c)
        stream("dn_k", lambda c: state[:, ds(c + 24, 1), :], 4, "dn_conv_k", 4, W, finish_k)
        stream("dn_q", lambda c: read[:, ds(c + 16, 1), :], 4, "dn_conv_q", 4, T, lambda c: unit_length(qf, c, T, P ** -0.5))
        stream("dn_v", lambda c: state[:, ds(c + 28, 1), :], 8, "dn_conv_v", 8, W, lambda c: to_tokens(vt, c))

        ar.reset(keep)
        x, u, v, w2 = (ar.take(NT * 16) for _ in range(4))
        ea, tmp16 = ar.take(16), ar.take(16)

        def per_tile(c):
            return c.unsqueeze(1).broadcast_to((P, NT, 16))
        sh = "p (j c) -> p j c"
        x3 = x.rearrange(sh, j=NT)
        a.do(a.eng.activation, beta, self.ab[:, :, 16:32], ACT.Sigmoid)
        d.do(d.eng.tensor_tensor, x3, self.ab[:, :, 0:16], per_tile(self.p("dt_bias")), ALU.add)
        d.do(d.eng.scalar_tensor_tensor, u, x, -1.0, x, ALU.mult, ALU.min)
        self.exp_precise(v, u, self.whole_i32, w2)
        d.do(d.eng.tensor_scalar, u, v, 2.0, None, ALU.add, ALU.bypass)
        d.do(d.eng.reciprocal, u, u)
        d.do(d.eng.tensor_tensor, v, v, u, ALU.mult)
        d.do(d.eng.tensor_tensor, u, v, v, ALU.mult)
        d.do(d.eng.tensor_scalar, w2, u, 1.0 / 17, 1.0 / 15, ALU.mult, ALU.add)
        for n in (13, 11, 9, 7, 5, 3, 1):
            d.do(d.eng.tensor_tensor, w2, w2, u, ALU.mult)
            d.do(d.eng.tensor_scalar, w2, w2, 1.0 / n, None, ALU.add, ALU.bypass)
        d.do(d.eng.scalar_tensor_tensor, w2, w2, 2.0, v, ALU.mult, ALU.mult)
        d.do(d.eng.tensor_scalar, x, x, 0.0, None, ALU.max, ALU.bypass)
        d.do(d.eng.tensor_tensor, x, x, w2, ALU.add)
        self.exp_precise(ea, self.p("a_log"), self.whole_i32[:, 0:16], tmp16)
        d.do(d.eng.tensor_tensor, gl, x3, per_tile(ea), ALU.mult)
        d.do(d.eng.tensor_scalar, gl, gl, -1.0, None, ALU.mult, ALU.bypass)
        for j in range(NT):
            b = self.bank[j]
            t = d.done.now()
            pe.do(pe.eng.matmul, b[:, 0:8], self.upto[0], gl[:, j, 0:8], start=True, stop=True, after=[t])
            t = pe.do(pe.eng.matmul, b[:, 8:16], self.upto[1], gl[:, j, 8:16], start=True, stop=True)
            d.do(d.eng.tensor_copy, gc[:, j, :], b[:, 0:16], after=[t])
        pr.join()
        self.dump("gc", gc)
        self.dump("kf", kf)
        self.dump("beta", beta)

        ar.reset(keep)
        kf_h, qf_h, kt_h, vt_h = ar.take(NT, P), ar.take(2, P), ar.take(NT, P), ar.take(NT, P)
        B = []
        for r in range(2):
            B.append(dict(y=ar.take(NT, P), dec=ar.take(NT, P), nt=ar.take(NT, P), x=ar.take(NT, P),
                          xt=ar.take(NT, P), mt=ar.take(NT, P), att=ar.take(2, P), qe=ar.take(2, P),
                          vn=ar.take(P), s=ar.take(P), cols=ar.take(6, NT)))
        o, sq, zg = ar.take(T), ar.take(T), ar.take(T)
        banks = [self.bank, self.gemm.psum]

        def each(op, out, lhs, rhs, n=NT):
            return lambda: [op(out[:, P * j:P * j + P], lhs[:, j, :], rhs(j), start=True, stop=True) for j in range(n)][-1]

        def tiles(b, n=NT):
            return b[:, 0:n * P].rearrange("p (j t) -> p j t", j=n)

        def direction(r, head, ch):
            fwd = r == 0
            b0, b1, b2, b3 = banks[r]
            v = B[r]
            y, dec, nt, x, xt, mt, att, qe, vn, s = (v[n] for n in ("y", "dec", "nt", "x", "xt", "mt", "att", "qe", "vn", "s"))
            g_, gc_, be, eg, el, ek = (v["cols"][:, i, :] for i in range(6))
            hd = head + 8 * r
            for dst, src in ((g_, gl), (gc_, gc), (be, beta)):
                ch(d, self.copy, dst, src[:, :, ds(hd, 1)])
            ch(d, d.eng.tensor_scalar, y, g_.unsqueeze(2).broadcast_to((P, NT, P)), 1.0, None, ALU.mult, ALU.bypass)
            ch(d, d.eng.tensor_scalar, mt, be.unsqueeze(2).broadcast_to((P, NT, P)), 1.0, None, ALU.mult, ALU.bypass)
            yield
            ch(pe, each(pe.eng.matmul, b0, y, lambda j: self.upto[r]))
            ch(pe, each(pe.eng.matmul, b1, mt, lambda j: ident))
            ch(pe, each(pe.eng.matmul, b2, kf_h, lambda j: kf_h[:, j, :]))
            ch(pe, each(pe.eng.matmul, b3, kf_h, lambda j: qf_h[:, j, :], 2))
            yield
            for j in range(NT):
                ch(d, d.eng.tensor_scalar, dec[:, j, :], b0[:, P * j:P * j + P], gc_[:, j:j + 1], 0.0, ALU.subtract, ALU.min)
            end = P - 1 if fwd else 0
            ch(d, d.eng.tensor_copy, el, tiles(b0)[:, :, end])
            ch(d, d.eng.tensor_tensor, ek, el, gc_, ALU.subtract)
            yield
            ch(a, a.eng.activation, dec, dec, ACT.Exp)
            ch(a, a.eng.activation, qe, tiles(b0, 2), ACT.Exp)
            ch(a, a.eng.activation, eg, gc_, ACT.Exp)
            ch(a, a.eng.activation, el, el, ACT.Exp)
            ch(a, a.eng.activation, ek, ek, ACT.Exp)
            yield
            ch(d, d.eng.tensor_tensor, qe, qe, qf_h, ALU.mult)
            ch(d, d.eng.tensor_tensor, nt, dec, tiles(b2), ALU.mult)
            ch(d, d.eng.tensor_tensor, nt, nt, tiles(b1), ALU.mult)
            ch(d, d.eng.tensor_tensor, att, dec[:, 0:2, :], tiles(b3, 2), ALU.mult)
            ch(d, d.eng.tensor_tensor, att, att, self.upto[r].unsqueeze(1).broadcast_to((P, 2, P)), ALU.mult)
            idb = ident.unsqueeze(1).broadcast_to((P, NT, P))
            ch(d, d.eng.tensor_copy, x, idb)
            ch(d, d.eng.tensor_copy, xt, idb)
            for level in range(6, -1, -1):
                mask = self.masks[r][:, level, :].unsqueeze(1).broadcast_to((P, NT, P))
                ch(d, d.eng.tensor_tensor, mt, nt, mask, ALU.mult)
                yield
                ch(pe, each(pe.eng.matmul, b0, mt, lambda j: x[:, j, :]))
                yield
                ch(a, a.eng.copy, y, tiles(b0))
                yield
                if level:
                    ch(pe, each(pe.eng.matmul, b1, xt, lambda j: y[:, j, :]))
                ch(pe, each(pe.eng.matmul, b2, y, lambda j: xt[:, j, :]))
                yield
                if level:
                    ch(d, d.eng.tensor_tensor, x, x, tiles(b1), ALU.subtract)
                ch(d, d.eng.tensor_tensor, xt, xt, tiles(b2), ALU.subtract)
            colb = lambda c: c.unsqueeze(2).broadcast_to((P, NT, P))
            ch(d, d.eng.tensor_tensor, nt, vt_h, colb(be), ALU.mult)
            ch(d, d.eng.tensor_tensor, eg, eg, be, ALU.mult)
            ch(d, d.eng.tensor_tensor, mt, kt_h, colb(eg), ALU.mult)
            ch(d, d.eng.tensor_tensor, x, kt_h, colb(ek), ALU.mult)
            yield
            ch(pe, each(pe.eng.matmul, b0, mt, lambda j: xt[:, j, :]))
            yield
            ch(d, d.eng.tensor_scalar, y, tiles(b0), -1.0, None, ALU.mult, ALU.bypass)
            order = (2, 3, 0, 1) if fwd else (3, 2, 1, 0)
            for n, j in enumerate(order):
                def solve():
                    mm = pe.eng.matmul(b1[:, 0:P], xt[:, j, :], nt[:, j, :], start=True, stop=n == 0)
                    return mm if n == 0 else pe.eng.matmul(b1[:, 0:P], y[:, j, :], s, start=False, stop=True)
                ch(pe, solve)
                yield
                ch(d, d.eng.tensor_copy, vn, b1[:, 0:P])
                yield
                if j < 2:
                    def out():
                        pe.eng.matmul(b3[:, P * j:P * j + P], vn, att[:, j, :], start=True, stop=False)
                        return pe.eng.matmul(b3[:, P * j:P * j + P], s, qe[:, j, :], start=False, stop=True)
                    ch(pe, out)
                if n < 3:
                    ch(pe, lambda: pe.eng.matmul(b2[:, 0:P], x[:, j, :], vn, start=True, stop=True))
                    yield
                    if n == 0:
                        ch(d, d.eng.tensor_copy, s, b2[:, 0:P])
                    else:
                        ch(d, d.eng.scalar_tensor_tensor, s, s, el[:, j:j + 1], b2[:, 0:P], ALU.mult, ALU.add)
                    yield

        with pr.loop(4, "deltanet") as h:
            d.wait(pe.done.now(), a.done.now())
            d.do(self.copy, kf_h.rearrange("p j t -> p (j t)"), kf[:, ds(h, 1), :])
            d.do(self.copy, qf_h.rearrange("p j t -> p (j t)"), qf[:, ds(h, 1), :])
            d.do(self.copy, kt_h, kt[:, :, ds(h * P, P)])
            for twin in range(2):
                head = h * 2 + twin
                a.wait(d.done.now())
                t = pr.dma(a, "mixer_in", zg, read[:, ds(head + 20, 1), :])
                t_v = d.do(self.copy, vt_h, vt[:, :, ds(head * P, P)], after=[pe.done.now()])
                sg = a.do(a.eng.activation, sq, zg, ACT.Sigmoid, after=[t, d.done.now()])
                t_z = d.do(d.eng.tensor_tensor, zg, zg, sq, ALU.mult, after=[sg])
                chains = [Chain([t_z, t_v, pe.done.now(), a.done.now()]) for _ in range(2)]
                lockstep([direction(r, head, chains[r]) for r in range(2)])
                d.do(d.eng.tensor_copy, sq, banks[1][3][:, 0:T], after=[pe.done.now(), a.done.now()])
                d.do(d.eng.tensor_tensor, o, banks[0][3][:, 0:T], sq, ALU.add)
                self.head_norm_gate(o, sq, self.p("dn_norm_w"), zg, self.branch[:, 2, ds(head, 1), :], self.bank[0])
        pr.join()
        self.dump("dn", self.branch[:, 2])

    def hyena(self):
        d, a, pe, pr, io, ar = self.dve, self.act, self.pe, self.prog, self.io, self.arena
        H = 1024
        ident = self.c("ident")
        ar.reset()
        z = ar.take(2, 3 * H)
        mats = ar.take(4, 2 * T)
        hs, hd, kr, ki = (ar.take(2, H) for _ in range(4))
        win = ar.take(2, H)
        w3 = ar.take(2, H)
        hid = ar.take(T)
        row = ar.take(H)
        raw, y = row[:, 0:T], row[:, T:2 * T]
        fwd_re, fwd_im, inv_re, inv_im = (mats[:, i, :].rearrange("p (a b) -> p a b", a=2) for i in range(4))
        B = self.bank
        pr.join()
        pr.dma(a, "hy_in", mats, io["dft"])
        t_w = pr.dma(a, "hy_in", win, io["window"])
        hy = io["s_read"].rearrange("(c p) t -> p c t", p=P)
        taps = self.p("hy_conv_w").rearrange("p (j c) -> p j c", j=3)
        with pr.loop(24, "hy_conv") as c:
            t = pr.dma(a, "mixer_in", raw, hy[:, ds(c + 28, 1), :], after=[d.done.now()])
            d.wait(t, pe.done.now())
            self.conv(y, raw, lambda j: taps[:, j, ds(c, 1)], 0, 4)
            t = d.do(d.eng.tensor_scalar, y, y, self.p("hy_conv_b")[:, ds(c, 1)], None, ALU.add, ALU.bypass)
            t = pe.do(lambda: [pe.eng.transpose(B[0][:, P * j:P * j + P], y[:, P * j:P * j + P], ident) for j in range(2)][-1],
                      after=[t])
            d.do(self.copy, z[:, :, ds(c * P, P)], B[0][:, 0:T].rearrange("p (j t) -> p j t", j=2), after=[t])
        pr.join(t_w)

        feats, w1, w2 = kr[0:33, 0, 0:T], kr[0:33, 0, T:T + 64], kr[0:64, 1, 0:64]
        pr.dma(a, "hy_in", feats, io["feats"])
        pr.dma(a, "hy_in", w1, io["hy_w1"])
        t = pr.dma(a, "hy_in", w2, io["hy_w2"])
        pe.wait(t)
        h64, r64 = hid[0:64, :], raw[0:64, :]
        for lhs, rhs, bias in ((w1, feats, "hy_b1"), (w2, h64, "hy_b2")):
            t = pe.do(pe.eng.matmul, B[0][0:64, 0:T], lhs, rhs, start=True, stop=True, after=[a.done.now()])
            d.do(d.eng.tensor_scalar, h64, B[0][0:64, 0:T], self.p(bias)[0:64, :], None, ALU.add, ALU.bypass, after=[t])
            d.do(d.eng.tensor_scalar, r64, h64, 1.0 / (2 * np.pi), MAGIC, ALU.mult, ALU.add)
            d.do(d.eng.tensor_scalar, r64, r64, -MAGIC, None, ALU.add, ALU.bypass)
            for part in (6.28125, 1.9350051879882812e-3, 3.0199159819e-7):
                d.do(d.eng.scalar_tensor_tensor, h64, r64, -part, h64, ALU.mult, ALU.add)
            t = d.do(d.eng.tensor_scalar, h64, h64, 3.1415925, -3.1415925, ALU.min, ALU.max)
            a.do(a.eng.activation, h64, h64, ACT.Sin, after=[t])
        pr.join()

        def transform(dst, mat, src, first=None):
            for m in range(2):
                for half in range(2):
                    b = B[2 * m + half]
                    for j in range(2):
                        mm = pe.eng.matmul(b[:, :], mat[:, j, P * m:P * m + P], src(j, half), start=j == 0, stop=j == 1)
                    t = pe.done.add(mm)
                    d.do(d.eng.tensor_copy, dst[:, m, 512 * half:512 * half + 512], b[:, :], after=[t])
            pe.wait(d.done.now())

        def cols(buf):
            return lambda j, half: buf[:, j, 512 * half:512 * half + 512]

        u = lambda j, half: z[:, j, 512 * half:512 * half + 512]
        for n in range(2):
            t = pr.dma(a, "hy_in", w3[0:64, :, :].rearrange("p a b -> p (a b)"), io["hy_w3"][:, 2 * H * n:2 * H * (n + 1)])
            t = pr.dma(a, "hy_in", row[0:1, :], io["hy_skip"][n:n + 1, :])
            pe.wait(t)
            d.wait(t)
            for m in range(2):
                for half in range(2):
                    bf, bb = B[2 * (half % 2)], B[2 * (half % 2) + 1]
                    sl = slice(512 * half, 512 * half + 512)
                    pe.wait(d.done.now())
                    pe.eng.matmul(bf[:, :], h64[:, P * m:P * m + P], w3[0:64, 0, sl], start=True, stop=True)
                    t = pe.done.add(pe.eng.matmul(bb[:, :], h64[:, P * m:P * m + P], w3[0:64, 1, sl], start=True, stop=True))
                    tmp = kr[:, 0, 0:512]
                    d.do(d.eng.tensor_copy, tmp, bb[:, :], after=[t])
                    if m == 0:
                        d.do(d.eng.memset, tmp[0:1, :], 0.0)
                    d.do(d.eng.tensor_tensor, hs[:, m, sl], bf[:, :], tmp, ALU.add)
                    d.do(d.eng.tensor_tensor, hd[:, m, sl], bf[:, :], tmp, ALU.subtract)
            d.do(d.eng.tensor_tensor, hs, hs, win, ALU.mult)
            d.do(d.eng.tensor_tensor, hd, hd, win, ALU.mult)
            t = d.do(d.eng.tensor_tensor, hs[0:1, 0, :], hs[0:1, 0, :], row[0:1, :], ALU.add)
            pe.wait(t)
            transform(kr, fwd_re, cols(hs))
            transform(ki, fwd_im, cols(hd))
            for half in range(2):
                for j in range(2):
                    mm = pe.eng.matmul(B[half][0:1, :], fwd_im[:, j, 0:1], cols(hs)(j, half), start=j == 0, stop=j == 1)
                t = pe.done.add(mm)
                d.do(d.eng.tensor_copy, ki[0:1, 0, 512 * half:512 * half + 512], B[half][0:1, :], after=[t])
            pe.wait(d.done.now())
            ur, ui, tmp = hs, hd, w3
            transform(ur, fwd_re, u)
            transform(ui, fwd_im, u)
            d.do(d.eng.tensor_tensor, tmp, ui, ki, ALU.mult)
            d.do(d.eng.tensor_copy, row[0:1, :], tmp[0:1, 0, :])
            d.do(d.eng.memset, tmp[0:1, 0, :], 0.0)
            d.do(d.eng.tensor_tensor, ki, ur, ki, ALU.mult)
            d.do(d.eng.tensor_tensor, ui, ui, kr, ALU.mult)
            d.do(d.eng.tensor_tensor, ur, ur, kr, ALU.mult)
            d.do(d.eng.tensor_tensor, ur, ur, tmp, ALU.subtract)
            d.do(d.eng.tensor_tensor, ui, ui, ki, ALU.add)
            t = d.do(d.eng.tensor_copy, ui[0:1, 0, :], row[0:1, :])
            pe.wait(t)
            gate = H * (n + 1)
            for m in range(2):
                for half in range(2):
                    b = B[2 * m + half]
                    for j in range(2):
                        pe.eng.matmul(b[:, :], inv_re[:, j, P * m:P * m + P], cols(ur)(j, half), start=j == 0, stop=False)
                        mm = pe.eng.matmul(b[:, :], inv_im[:, j, P * m:P * m + P], cols(ui)(j, half), start=False, stop=j == 1)
                    t = pe.done.add(mm)
                    d.do(d.eng.tensor_tensor, z[:, m, 512 * half:512 * half + 512], b[:, :],
                         z[:, m, gate + 512 * half:gate + 512 * half + 512], ALU.mult, after=[t])
            pr.join()
        for c in range(8):
            b = B[c % 4]
            t = pe.do(lambda: [pe.eng.transpose(b[:, P * j:P * j + P], z[:, j, P * c:P * c + P], ident) for j in range(2)][-1],
                      after=[d.done.now()])
            d.do(d.eng.tensor_copy, self.branch[:, 0, c, :], b[:, 0:T], after=[t])
        pr.join()
        self.dump("hy", self.branch[:, 0])

    def merge(self):
        d, a, g, pr, io = self.dve, self.act, self.gemm, self.prog, self.io
        self.arena.reset()
        gates = self.arena.take(8, T)
        tmp = self.arena.take(4, T)
        view = io["s_gate"].rearrange("(c p) t -> p c t", p=P)
        for n in range(3):
            def evacuate(chunk, m, psum, summed, n=n, count=[0]):
                slot = (count[0] % 8)
                count[0] += 1
                a.wait(d.done.now())
                t = pr.gate_in[slot].add(a.eng.dma_start(gates[:, slot, :], view[:, ds(chunk + 16 * n, 1), :]), 16)
                d.wait(t, summed)
                t = g.drained[m].add(d.eng.tensor_tensor(tmp[:, m, :], psum, gates[:, slot, :], ALU.mult))
                dst = self.mix[:, ds(chunk, 1), :]
                d.wait(t)
                if n == 0:
                    d.done.add(self.copy(dst, tmp[:, m, :]))
                else:
                    d.done.add(d.eng.tensor_tensor(dst, dst, tmp[:, m, :], ALU.add))
            g.run("w_branch%d" % n, io["w_branch%d" % n], 8, DM, lambda kc: self.branch[:, n, kc, :], T, evacuate, groups=2)
            self.join_gemm()
        self.dump("merged", self.mix[:, :, :])

    def layernorm(self, x, gain, bias, eps, tmp):
        d, a, pe, bank = self.dve, self.act, self.pe, self.bank[0]
        rs = self.rstd[:, 0:T]
        for c in range(KD):
            mm = pe.eng.matmul(bank[:, 0:T], self.c("ones"), x[:, c, :], start=c == 0, stop=c == KD - 1)
        t = pe.done.add(mm)
        d.do(d.eng.tensor_scalar, rs, bank[:, 0:T], 1.0 / DM, None, ALU.mult, ALU.bypass, after=[t])
        t = d.do(d.eng.tensor_tensor, x, x, rs.unsqueeze(1).broadcast_to((P, KD, T)), ALU.subtract)
        t = a.do(a.eng.activation, tmp, x, ACT.Square, after=[t])
        pe.wait(t)
        for c in range(KD):
            mm = pe.eng.matmul(bank[:, 0:T], self.c("ones"), tmp[:, c, :], start=c == 0, stop=c == KD - 1)
        t = pe.done.add(mm)
        self.rsqrt(rs, bank[:, 0:T], 1.0 / DM, eps, after=[t])
        for c in range(KD):
            d.do(d.eng.scalar_tensor_tensor, x[:, c, :], x[:, c, :], gain[:, c:c + 1], rs, ALU.mult, ALU.mult)
            t = d.do(d.eng.tensor_scalar, x[:, c, :], x[:, c, :], bias[:, c:c + 1], None, ALU.add, ALU.bypass)
        return t

    def gated_residual(self, x, gate):
        d, g = self.dve, self.gemm
        d.do(d.eng.tensor_scalar, x, x, ALPHA, None, ALU.mult, ALU.bypass)
        col = self.mods[:, gate:gate + KD, 0]

        def evacuate(chunk, m, psum, summed):
            d.wait(d.done.now(), summed)
            dst = x[:, ds(chunk, 1), :]
            g.drained[m].add(d.eng.scalar_tensor_tensor(dst, psum, col[:, ds(chunk, 1)], dst, ALU.mult, ALU.add))
        return evacuate

    def block2_end(self):
        d, a, g, io, pr = self.dve, self.act, self.gemm, self.io, self.prog
        x = self.res[:, :, NMETA:]
        g.run("w_out2", io["w_out2"], KD, DM, lambda kc: self.mix[:, kc, :], T, self.gated_residual(x, 32))
        self.join_gemm()
        self.layernorm(x, self.p("ln1_g"), self.p("ln1_b"), 1e-5, self.mix[:, :, :])
        pr.join()
        self.dump("ln1", x)
        t = self.modulate(x, self.xin[:, :, 0:T], 48, 64, 0)
        self.arena.reset()
        hid = self.arena.take(DFF // P, T)
        self.sq_tmp = self.arena.take(4, T)
        g.run("w_ff1", io["w_ff1"], KD, DFF, lambda kc: self.xin[:, kc, 0:T], T, self.squared_relu(hid), after=[t])
        self.join_gemm()
        g.run("w_ff2", io["w_ff2"], DFF // P, DM, lambda kc: hid[:, kc, :], T, self.gated_residual(x, 80))
        self.join_gemm()
        t = self.layernorm(x, self.p("ln2_g"), self.p("ln2_b"), 1e-5, self.mix[:, :, :])
        pr.dma(a, "out", io["out"].rearrange("(c p) t -> p c t", p=P), x, after=[t])


def program(nc, io, per_turn, pofs, cofs, stop=None):
    k = Kernel(nc, io, per_turn, pofs, cofs, stop)
    k.load_inputs()
    k.block1_project()
    k.attention()
    k.ssm()
    k.block1_mlp()
    k.modulation()
    k.block2_project()
    k.hgrn2()
    k.deltanet()
    k.hyena()
    k.merge()
    k.block2_end()
    k.act.wait(*[s.now() for n, s in k.prog.dma_sems.items()])
    return k.prog.seen


def kernel(_dumps=None, **inputs):
    import concourse.bacc as bacc
    from concourse.bass_utils import run_bass_kernel_spmd as run

    i = {k: np.asarray(v) for k, v in inputs.items()}
    params, pofs = layout_params(i)
    consts, cofs = constants()
    feats, window = filter_features()
    arrays = {
        "params": params, "consts": consts,
        "hT": np.ascontiguousarray(np.concatenate([i["meta_tokens"], i["x"][0]], axis=0).T),
        "w_in": i["w_in"][0], "w_glu": i["w_glu"][0], "w_out": i["w_out"][0],
        "w_up": i["w_up"][0], "w_down": i["w_down"][0],
        **layout_ssm(i),
        "w_ada": i["w_ada_2"][0], "w_in2": i["w_in_2"][0], "ctxT": np.ascontiguousarray(i["ctx_2"][0].T),
        "dft": fourier(), "feats": feats, "window": window,
        "hy_w1": i["hy_filt_w1_2"][0], "hy_w2": i["hy_filt_w2_2"][0], "hy_w3": i["hy_filt_w3_2"][0],
        "hy_skip": i["hy_skip_2"][0],
        **{"w_branch%d" % n: i["w_branch_2"][0, n] for n in range(3)},
        "w_out2": i["w_out_2"][0], "w_ff1": i["w_ff1_2"][0], "w_ff2": i["w_ff2_2"][0],
    }
    outs = {"out": (DM, T), **(_dumps or {})}
    scratch = {"s_state": (4608, 2 * T), "s_read": (6656, T), "s_gate": (6144, T)}

    def built(per_turn):
        nc = bacc.Bacc("TRN2", target_bir_lowering=False, num_devices=1)
        io = {k: nc.dram_tensor("in_" + k, v.shape, F32, kind="ExternalInput").ap() for k, v in arrays.items()}
        io |= {k: nc.dram_tensor("out_" + k, s, F32, kind="ExternalOutput").ap() for k, s in outs.items()}
        io |= {k: nc.dram_tensor(k, s, F32, kind="Internal").ap() for k, s in scratch.items()}
        return nc, program(nc, io, per_turn, pofs, cofs, stop=bool(_dumps))

    _, seen = built({})
    nc, again = built(seen)
    assert seen == again
    r = run(nc, [{"in_" + k: v for k, v in arrays.items()}], core_ids=[0])
    return np.ascontiguousarray(r.results[0]["out_out"].T)[None]
```

```python
from contextlib import contextmanager

import numpy as np

import concourse.bass as bass
from concourse import mybir
from concourse.alu_op_type import AluOpType as ALU

F32 = mybir.dt.float32
I32 = mybir.dt.int32
F32R = mybir.dt.float32r
ACT = mybir.ActivationFunctionType
AX = mybir.AxisListType
ds = bass.ds

P = 128
DM = 2048
KD = DM // P
NMETA = 16
T = 256
L = T + NMETA
HD = 64
NH = 16
NKV = 4
DFF = 8192
TWO_PI_BELOW = 6.283185
MAGIC = 12582912.0


class Sem:

    def __init__(self, prog, name, unit=1):
        self.prog, self.name, self.count = prog, name, unit
        self.sem = prog.nc.alloc_semaphore(name)
        assert not prog.begun, name
        prog.nc.gpsimd.sem_inc(self.sem, unit)
        prog.sems.append(self)

    def value(self, count):
        v = count
        for turn, per_turn in self.prog.loops:
            if per_turn.get(self.name, 0):
                v = turn * per_turn[self.name] + v
        return v

    def add(self, ins, n=1):
        ins.then_inc(self.sem, n)
        self.count += n
        return (self, self.count)

    def now(self):
        return (self, self.count)


class Engine:

    def __init__(self, prog, eng, name):
        self.prog, self.eng, self.name = prog, eng, name
        self.done = Sem(prog, "done_" + name)

    def wait(self, *tokens):
        for t in tokens:
            if t is None:
                continue
            if isinstance(t, list):
                self.wait(*t)
            elif not (isinstance(t[1], int) and t[1] <= 0 and not self.prog.loops):
                self.eng.wait_ge(t[0].sem, t[0].value(t[1]))

    def do(self, op, *args, after=(), chain=True, **kw):
        if chain:
            self.wait(self.done.now())
        self.wait(*after)
        return self.done.add(op(*args, **kw))


class Program:
    def __init__(self, nc, per_turn):
        self.begun = False
        self.nc, self.sems, self.loops, self.per_turn, self.seen = nc, [], [], per_turn, {}
        self.pe = Engine(self, nc.tensor, "pe")
        self.dve = Engine(self, nc.vector, "dve")
        self.act = Engine(self, nc.scalar, "act")
        self.pool = Engine(self, nc.gpsimd, "pool")
        keys = ["mods", "dn_out", "inputs", "kdup", "ssm_in", "ctx", "mixer_in", "hy_in", "out"] + ["st%d" % m for m in range(4)]
        self.dma_sems = {k: Sem(self, "dma_" + k, 16) for k in keys}
        self.relu_done = [Sem(self, f"relu{m}") for m in range(4)]
        self.gate_in = [Sem(self, f"gate_in{m}", 16) for m in range(8)]

    def begin(self):
        ready = self.nc.alloc_semaphore("ready")
        self.nc.gpsimd.sem_inc(ready, 1)
        for eng in (self.nc.tensor, self.nc.vector, self.nc.scalar, self.nc.sync, self.nc.gpsimd):
            eng.wait_ge(ready, 1)
        self.begun = True

    @contextmanager
    def loop(self, n, name):
        start = {s.name: s.count for s in self.sems}
        with self.nc.Fori(0, n) as turn:
            self.loops.append((turn, self.per_turn.get(name, {})))
            yield turn
            self.loops.pop()
        made = {s.name: s.count - start.get(s.name, 0) for s in self.sems}
        assert name not in self.seen, name
        self.seen[name] = made
        for s in self.sems:
            s.count = start.get(s.name, 0) + n * made[s.name]

    def dma(self, engine, key, out, in_, after=()):
        engine.wait(*after)
        return self.dma_sems[key].add(engine.eng.dma_start(out, in_), 16)

    def join(self, *more):
        engines = (self.pe, self.dve, self.act, self.pool)
        tokens = [e.done.now() for e in engines]
        for e in engines:
            e.wait(*tokens, *more)


class Gemm:

    SLOTS, KPER, COLS, BANKS = 8, 1, 512, 4

    def __init__(self, prog):
        nc = prog.nc
        self.prog = prog
        self.ring = nc.alloc_sbuf_tensor("weights_ring", [P, self.SLOTS, self.KPER, self.COLS], F32)
        self.psum = [nc.alloc_psum_tensor(f"acc{m}", [P, 512], F32) for m in range(self.BANKS)]
        self.sp = Engine(prog, nc.sync, "sp")
        self.hi = nc.alloc_sbuf_tensor("weights_hi", [P, 3, self.COLS], F32R)
        self.lo = nc.alloc_sbuf_tensor("weights_lo", [P, 3, self.COLS], F32R)
        self.xhi = nc.alloc_sbuf_tensor("moving_hi", [P, 1024], F32R)
        self.xlo = nc.alloc_sbuf_tensor("moving_lo", [P, 1024], F32R)
        self.used = [Sem(prog, f"used{b}") for b in range(3)]
        self.arrived = [Sem(prog, f"arrived{s}", 16) for s in range(self.SLOTS)]
        self.consumed = [Sem(prog, f"consumed{s}") for s in range(self.SLOTS)]
        self.summed = [Sem(prog, f"summed{m}") for m in range(2 * self.BANKS)]
        self.drained = [Sem(prog, f"drained{m}") for m in range(2 * self.BANKS)]

    def group(self, w, kchunks, moving, tokens, evacuate, group, first_slot=0, side=0, step=1):
        sp, pe = self.sp, self.prog.pe
        shared = tokens <= 256
        psum = [self.psum[2 * side + m // 2][:, tokens * (m % 2):tokens * (m % 2 + 1)] if shared else self.psum[m][:, 0:tokens]
                for m in range(self.BANKS)]
        sums = {}
        slots = kchunks // self.KPER
        for s in range(slots):
            slot = (first_slot + s * step) % self.SLOTS
            sp.wait(self.consumed[slot].now())
            src = w[:, s * self.KPER:(s + 1) * self.KPER, ds(group * self.COLS, self.COLS)]
            self.arrived[slot].add(sp.eng.dma_start(self.ring[:, slot, :, :], src), 16)
            pe.wait(self.arrived[slot].now())
            for m in range(self.BANKS):
                if s == 0:
                    pe.wait(self.drained[m + 4 * side].now())
                    if shared and m % 2 == 0:
                        pe.wait(self.drained[m + 4 * side + 1].now())
                for k in range(self.KPER):
                    kc = s * self.KPER + k
                    mm = pe.eng.matmul(
                        psum[m], self.ring[:, slot, k, m * P:(m + 1) * P], moving(kc),
                        start=kc == 0 and (not shared or m % 2 == 0), stop=kc == kchunks - 1,
                        skip_group_check=shared)
                    if m == self.BANKS - 1 and k == self.KPER - 1:
                        sums[m] = self.consumed[slot].add(mm)
                    elif kc == kchunks - 1:
                        sums[m] = self.summed[m + 4 * side].add(mm)
                    if m % 2:
                        yield
        for m in range(self.BANKS):
            evacuate(group * self.BANKS + m, m + 4 * side, psum[m], sums[m | 1] if shared else sums[m])
            yield

    def split_group(self, w, kchunks, moving, tokens, evacuate, group, first_slot=0, side=0):
        sp, pe, a, d = self.sp, self.prog.pe, self.prog.act, self.prog.dve
        shared = tokens <= 256
        psum = [self.psum[2 * side + m // 2][:, tokens * (m % 2):tokens * (m % 2 + 1)] if shared else self.psum[m][:, 0:tokens]
                for m in range(self.BANKS)]
        sums = {}
        buffers = 3 if tokens * 3 <= 1024 else 2
        for kc in range(kchunks):
            slot, b = (first_slot + kc) % self.SLOTS, (first_slot + kc) % buffers
            sp.wait(self.consumed[slot].now())
            src = w[:, kc, ds(group * self.COLS, self.COLS)]
            self.arrived[slot].add(sp.eng.dma_start(self.ring[:, slot, 0, :], src), 16)
            hi, lo, xhi, xlo = self.hi[:, b, :], self.lo[:, b, :], *(x[:, b * tokens:(b + 1) * tokens] for x in (self.xhi, self.xlo))
            a.wait(self.used[b].now())
            a.done.add(a.eng.activation(xhi, moving(kc), ACT.Copy))
            a.wait(self.arrived[slot].now())
            t = a.done.add(a.eng.activation(hi, self.ring[:, slot, 0, :], ACT.Copy))
            d.wait(t)
            d.done.add(d.eng.tensor_tensor(xlo, moving(kc), xhi.bitcast(F32), ALU.subtract))
            t = self.consumed[slot].add(d.eng.tensor_tensor(lo, self.ring[:, slot, 0, :], hi.bitcast(F32), ALU.subtract))
            pe.wait(t)
            for m in range(self.BANKS):
                if kc == 0:
                    pe.wait(self.drained[m + 4 * side].now())
                    if shared and m % 2 == 0:
                        pe.wait(self.drained[m + 4 * side + 1].now())
                cols = slice(m * P, (m + 1) * P)
                for n, (wt, x) in enumerate(((lo, xhi), (hi, xlo), (hi, xhi))):
                    mm = pe.eng.matmul(psum[m], wt[:, cols], x,
                                       start=kc == 0 and n == 0 and (not shared or m % 2 == 0),
                                       stop=kc == kchunks - 1 and n == 2, skip_group_check=shared)
                if m == self.BANKS - 1:
                    sums[m] = self.used[b].add(mm)
                elif kc == kchunks - 1:
                    sums[m] = self.summed[m + 4 * side].add(mm)
            if kc == 0:
                yield
        for m in range(self.BANKS):
            evacuate(group * self.BANKS + m, m + 4 * side, psum[m], sums[m | 1] if shared else sums[m])

    def wide_group(self, w, kchunks, stationary, evacuate, group):
        sp, pe = self.sp, self.prog.pe
        rows = stationary(0).shape[1]
        for s in range(kchunks // self.KPER):
            slot = s % self.SLOTS
            sp.wait(self.consumed[slot].now())
            src = w[:, s * self.KPER:(s + 1) * self.KPER, ds(group * self.COLS, self.COLS)]
            self.arrived[slot].add(sp.eng.dma_start(self.ring[:, slot, :, :], src), 16)
            pe.wait(self.arrived[slot].now())
            if s == 0:
                pe.wait(self.drained[0].now(), self.drained[1].now())
            for k in range(self.KPER):
                kc = s * self.KPER + k
                mm = pe.eng.matmul(self.psum[0][0:rows, :], stationary(kc), self.ring[:, slot, k, :],
                                   start=kc == 0, stop=kc == kchunks - 1)
            t = self.consumed[slot].add(mm)
            yield
        yield
        evacuate(group, self.psum[0][0:rows, :], t)

    def rows(self, weights):
        return weights.rearrange("(c p) n -> p c n", p=P)

    def run(self, name, weights, kchunks, ncols, moving, tokens, evacuate, after=(), groups=1):
        for e in (self.prog.pe, self.prog.act, self.prog.dve):
            e.wait(*after)
        slots = kchunks // self.KPER
        assert (groups * slots) % self.SLOTS == 0 and ncols % (self.COLS * groups) == 0, name
        with self.prog.loop(ncols // self.COLS // groups, name) as turn:
            for g in range(groups):
                for _ in self.split_group(self.rows(weights), kchunks, moving, tokens, evacuate, turn * groups + g,
                                          g * slots, side=g % 2 if tokens <= 256 else 0):
                    pass


def layout_params(i):
    def col(v):
        return np.ascontiguousarray(np.asarray(v).reshape(-1, P).T)

    def every(v):
        v = np.asarray(v).reshape(1, -1)
        return np.broadcast_to(v, (P, v.shape[1]))

    def twice(v):
        v = np.asarray(v).T
        return np.concatenate([v, v], axis=0)

    parts = {
        "norm_mix_g": col(i["norm_mix_g"]),
        "norm_mlp_g": col(i["norm_mlp_g"]),
        "qk_g": np.concatenate(
            [np.repeat(np.tile(i["q_norm_g"][0], 2)[:, None], 8, 1),
             np.repeat(np.tile(i["k_norm_g"][0], 2)[:, None], 2, 1)], axis=1),
        "sinks": every(i["attn_sinks"]),
        "attn_out_g": col(i["attn_out_g"]),
        "ssm_out_g": col(i["ssm_out_g"]),
        "b_glu": col(i["b_glu"]),
        "ssm_d": col(i["ssm_d"]),
        "lam_re": twice(i["ssm_lambda_re"][0]),
        "lam_im": twice(i["ssm_lambda_im"][0]),
        "log_step": every(i["ssm_log_step"]),
        "c": np.stack([i["c_2"][0].reshape(KD, P).T, i["c_ctx_2"].reshape(KD, P).T], axis=2).reshape(P, -1),
        "b_ada": col(i["b_ada_2"]),
        "lb_logits": col(i["hg_lb_logits_2"]),
        "hg_norm_w": col(i["hg_norm_w_2"]),
        "dn_norm_w": col(i["dn_norm_w_2"]),
        "dn_conv_q": col(i["dn_conv_q_2"]),
        "dn_conv_k": col(i["dn_conv_k_2"]),
        "dn_conv_v": col(i["dn_conv_v_2"]),
        "a_log": every(i["dn_a_log_2"]),
        "dt_bias": every(i["dn_dt_bias_2"]),
        "hy_conv_w": col(i["hy_conv_w_2"]),
        "hy_conv_b": col(i["hy_conv_b_2"]),
        "hy_b1": np.tile(i["hy_filt_b1_2"][0], 2)[:, None],
        "hy_b2": np.tile(i["hy_filt_b2_2"][0], 2)[:, None],
        "ln1_g": col(i["ln1_g_2"]), "ln1_b": col(i["ln1_b_2"]),
        "ln2_g": col(i["ln2_g_2"]), "ln2_b": col(i["ln2_b_2"]),
    }
    offsets, at = {}, 0
    for k, v in parts.items():
        offsets[k] = (at, at + v.shape[1])
        at += v.shape[1]
    return np.ascontiguousarray(np.concatenate(list(parts.values()), axis=1), dtype=np.float32), offsets


def layout_ssm(i):
    br, bi = (np.asarray(i[n][0]).transpose(0, 2, 1).reshape(8, P, 64) for n in ("ssm_b_re", "ssm_b_im"))
    cr, ci = (np.asarray(i[n][0]).transpose(2, 0, 1) for n in ("ssm_c_re", "ssm_c_im"))
    return {
        "ssm_b1": np.ascontiguousarray(np.concatenate([br, bi], axis=2).transpose(1, 0, 2)),
        "ssm_b2": np.ascontiguousarray(np.concatenate([bi, br], axis=2).transpose(1, 0, 2)),
        "ssm_cr": np.ascontiguousarray(np.concatenate([cr, cr], axis=0)),
        "ssm_ci": np.ascontiguousarray(np.concatenate([ci, ci], axis=0)),
    }


def constants():
    c = {}
    p = np.arange(P)
    c["ident"] = np.eye(P)
    c["ones"] = np.ones((P, P))
    c["ones_heads"] = np.kron(np.eye(2), np.ones((HD, HD)))
    t = np.arange(L)
    dist = np.zeros((P, 2, L))
    for q in range(2):
        tq = NMETA + P * q + p[:, None]
        d = tq - t[None, :]
        seen = (d >= 0) & ((d < 128) | (t[None, :] < NMETA))
        dist[:, q] = np.where(seen, np.abs(d), 1e33)
    c["dist"] = dist.reshape(P, -1)
    c["slopes"] = np.broadcast_to(-np.exp2(-8.0 * np.arange(1, NH + 1) / NH), (P, NH))
    c["steps"] = np.broadcast_to(t, (P, L))
    c["group_mask"] = (p[:, None] // 16 == np.arange(8)[None]).astype(float)
    i, j = p[:, None], p[None, :]
    masks = np.zeros((2, 7, P, P))
    for level in range(7):
        half = P >> (level + 1)
        joins = (i // (2 * half) == j // (2 * half)) & (i // half % 2 == 0) & (j // half % 2 == 1)
        masks[0, level], masks[1, level] = joins, joins.T
    c["masks"] = masks.transpose(2, 0, 1, 3).reshape(P, -1)
    c["upto"] = np.concatenate([i <= j, i >= j], axis=1).astype(float)
    c["half_pi"] = np.full((P, 1), np.pi / 2)
    c["top"] = np.where(p < 64, 1.0, -1.0)[:, None]
    offsets, at = {}, 0
    for k, v in c.items():
        offsets[k] = (at, at + v.shape[1])
        at += v.shape[1]
    return np.ascontiguousarray(np.concatenate(list(c.values()), axis=1), dtype=np.float32), offsets


def fourier():
    n = 2 * T
    t, f = np.arange(T)[:, None], np.arange(T)[None, :]
    ang = 2 * np.pi * ((t * f) % n) / n
    re, im = np.cos(ang), -np.sin(ang)
    im[:, 0] = (-1.0) ** t[:, 0]
    back_re, back_im = 2 * re.T / n, 2 * im.T / n
    back_re[0] /= 2
    back_im[0] /= 2
    m = np.stack([re, im, back_re, back_im])
    return np.ascontiguousarray(m.reshape(4, 2, P, T).transpose(2, 0, 1, 3).reshape(P, 4, 2 * T), dtype=np.float32)


def filter_features():
    bands = 16
    t = np.linspace(0, 1, T)
    ang = 2 * np.pi / T * np.arange(T)
    b = np.linspace(1e-4, bands - 1, bands)[:, None]
    feats = np.concatenate([t[None], np.cos(b * ang), -np.sin(b * ang)])
    deltas = np.abs(np.linspace(np.log(1e-2) / 1.5, np.log(1e-2) / 0.3, 1024))
    window = np.exp(-t[:, None] * deltas).reshape(2, P, 1024).transpose(1, 0, 2)
    return feats.astype(np.float32), np.ascontiguousarray(window, dtype=np.float32)


class Arena:

    def __init__(self, tensor, size):
        self.tensor, self.size, self.at = tensor, size, 0

    def reset(self, at=0):
        self.at = at

    def take(self, *dims):
        n = int(np.prod(dims))
        assert self.at + n <= self.size, (self.at, n, self.size)
        v = self.tensor[:, self.at:self.at + n]
        self.at += n
        if len(dims) == 2:
            v = v.rearrange("p (a b) -> p a b", b=dims[1])
        if len(dims) == 3:
            v = v.rearrange("p (a b c) -> p a b c", b=dims[1], c=dims[2])
        return v


ARENA = 21760
ALPHA = 2 ** 0.25
LN_1E30 = float(30 * np.log(10.0))


class Chain:

    def __init__(self, tokens):
        self.last = tokens

    def __call__(self, engine, op, *args, **kw):
        self.last = [engine.do(op, *args, after=self.last, chain=False, **kw)]


def lockstep(strands):
    strands = list(strands)
    while strands:
        for s in list(strands):
            try:
                next(s)
            except StopIteration:
                strands.remove(s)
        yield


def beside(strand, pieces, background):
    background = list(background)
    total = sum(n for _, n in background)
    gens = [g for g, _ in background]
    done = given = 0
    for _ in strand:
        done += 1
        while gens and given < total * done / pieces:
            try:
                next(gens[0])
                given += 1
            except StopIteration:
                gens.pop(0)
    for g in gens:
        for _ in g:
            pass
    return done


class Kernel:
    def __init__(self, nc, io, per_turn, pofs, cofs):
        self.nc, self.io = nc, io
        self.prog = pr = Program(nc, per_turn)
        self.pe, self.dve, self.act, self.pool = pr.pe, pr.dve, pr.act, pr.pool
        self.gemm = Gemm(pr)
        pr.begin()
        self.bank = [nc.alloc_psum_tensor(f"bank{b}", [P, 512], F32) for b in range(4)]
        pn = max(b for a, b in pofs.values())
        cn = max(b for a, b in cofs.values())
        self.params = nc.alloc_sbuf_tensor("params_sb", [P, pn], F32)
        self.consts = nc.alloc_sbuf_tensor("consts_sb", [P, cn], F32)
        self.pofs, self.cofs = pofs, cofs
        self.res = nc.alloc_sbuf_tensor("residual", [P, KD, L], F32)
        self.xin = nc.alloc_sbuf_tensor("moving", [P, KD, 512], F32)
        self.mix = nc.alloc_sbuf_tensor("mixed", [P, 16, T], F32)
        self.rstd = nc.alloc_sbuf_tensor("rstd", [P, L], F32)
        masks = self.c("masks").rearrange("p (r l t) -> p r l t", r=2, l=7)
        self.masks = [masks[:, r] for r in range(2)]
        self.upto = [self.c("upto")[:, P * r:P * r + P] for r in range(2)]
        self.mods = nc.alloc_sbuf_tensor("mods", [P, 96, 2], F32)
        small = nc.alloc_sbuf_tensor("small", [P, 64], F32)
        self.cc, self.cc_sig = small[:, 0:32], small[:, 32:64]
        self.mods_row = nc.alloc_sbuf_tensor("mods_row", [P, 512], F32)
        self.ab = nc.alloc_sbuf_tensor("ab", [P, 4, 32], F32)
        self.whole_i32 = nc.alloc_sbuf_tensor("whole_i32", [P, 64], I32)[:, :]
        self.arena = Arena(nc.alloc_sbuf_tensor("arena", [P, ARENA], F32), ARENA)

    def p(self, name):
        a, b = self.pofs[name]
        return self.params[:, a:b]

    def c(self, name):
        a, b = self.cofs[name]
        return self.consts[:, a:b]


    def rsqrt(self, out, src, scale, eps, after=()):
        d, a = self.dve, self.act
        t = d.do(d.eng.tensor_scalar, out, src, scale, eps, ALU.mult, ALU.add, after=after)
        t = a.do(a.eng.activation, out, out, ACT.Sqrt, after=[t])
        return d.do(d.eng.reciprocal, out, out, after=[t])

    def feature_rms(self, name, src, chunks, n, eps, squares, bank):
        pe, a = self.pe, self.act
        t = a.do(a.eng.activation, squares, src, ACT.Square)
        pe.wait(t)
        for c in range(chunks):
            mm = pe.eng.matmul(bank[:, 0:n], self.c("ones"), squares[:, c, :], start=c == 0, stop=c == chunks - 1)
        t = pe.done.add(mm)
        return self.rsqrt(self.rstd[:, 0:n], bank[:, 0:n], 1.0 / (chunks * P), eps, after=[t])

    def normalise(self, name, src, gain, dst, chunks, n):
        d = self.dve
        for c in range(chunks):
            t = d.do(d.eng.scalar_tensor_tensor, dst[:, c, 0:n], src[:, c, :], gain[:, c:c + 1],
                     self.rstd[:, 0:n], ALU.mult, ALU.mult, chain=c == 0)
        return t

    def exp_precise(self, dst, src, whole, tmp):
        d = self.dve

        def ts(o, i, s1, s2, a, b):
            return d.do(d.eng.tensor_scalar, o, i, s1, s2, a, b)
        ts(tmp, src, 88.0, -87.0, ALU.min, ALU.max)
        ts(dst, tmp, 1.4426950408889634, MAGIC, ALU.mult, ALU.add)
        ts(dst, dst, -MAGIC, None, ALU.add, ALU.bypass)
        d.do(d.eng.scalar_tensor_tensor, tmp, dst, -0.693359375, tmp, ALU.mult, ALU.add)
        d.do(d.eng.scalar_tensor_tensor, tmp, dst, 2.12194440e-4, tmp, ALU.mult, ALU.add)
        ts(whole, dst, 127.0, 8388608.0, ALU.add, ALU.mult)
        coef = [1.0 / 5040, 1.0 / 720, 1.0 / 120, 1.0 / 24, 1.0 / 6, 0.5, 1.0]
        ts(dst, tmp, coef[0], coef[1], ALU.mult, ALU.add)
        for cf in coef[2:]:
            d.do(d.eng.tensor_tensor, dst, dst, tmp, ALU.mult)
            ts(dst, dst, cf, None, ALU.add, ALU.bypass)
        d.do(d.eng.tensor_tensor, dst, dst, tmp, ALU.mult)
        ts(dst, dst, 1.0, None, ALU.add, ALU.bypass)
        return d.do(d.eng.tensor_tensor, dst, dst, whole.bitcast(F32), ALU.mult)

    def copy(self, out, src):
        return self.dve.eng.tensor_scalar(out, src, 1.0, None, ALU.mult, ALU.bypass)


    def load_inputs(self):
        pr, io = self.prog, self.io
        t = [pr.dma(self.act, "inputs", self.params[:, :], io["params"]),
             pr.dma(self.act, "inputs", self.consts[:, :], io["consts"]),
             pr.dma(self.act, "inputs", self.res[:, :, :], io["hT"].rearrange("(c p) t -> p c t", p=P))]
        pr.join(t[-1])

    def block1_project(self):
        d, a, g = self.dve, self.act, self.gemm
        self.arena.reset()
        self.pj = self.arena.take(20, L)
        squares = self.arena.take(KD, L)
        self.feature_rms("rms1", self.res[:, :, :], KD, L, 1e-6, squares, self.bank[0])
        t = self.normalise("norm1", self.res[:, :, :], self.p("norm_mix_g"), self.xin[:, :, :], KD, L)

        def evacuate(chunk, m, psum, summed):
            d.wait(summed)
            g.drained[m].add(self.copy(self.pj[:, ds(chunk, 1), :], psum))
        g.run("w_in", self.io["w_in"], KD, 2560, lambda kc: self.xin[:, kc, 0:L], L, evacuate, after=[t])
        self.join_gemm()

    def join_gemm(self):
        self.prog.join(*[s.now() for s in self.gemm.drained])

    def attention(self):
        nc, d, a, pe, pr = self.nc, self.dve, self.act, self.pe, self.prog
        pj, ar, bank = self.pj, self.arena, self.bank
        ar.reset(20 * L)
        sq = ar.take(L)
        rs = ar.take(L)
        with pr.loop(10, "qk_norm") as c:
            t = d.do(d.eng.tensor_tensor, sq, pj[:, ds(c, 1), :], pj[:, ds(c, 1), :], ALU.mult, after=[pe.done.now()])
            t = pe.do(pe.eng.matmul, bank[0][:, 0:L], self.c("ones_heads"), sq, start=True, stop=True,
                      after=[t, d.done.now()])
            self.rsqrt(rs, bank[0][:, 0:L], 1.0 / HD, 1e-6, after=[t])
            d.do(d.eng.scalar_tensor_tensor, pj[:, ds(c, 1), :], pj[:, ds(c, 1), :],
                 self.p("qk_g")[:, ds(c, 1)], rs, ALU.mult, ALU.mult)
        pr.join()
        ax = Arena(self.xin[:, :, :].rearrange("p a b -> p (a b)"), KD * 512)
        kdup = ax.take(NKV, L)
        for dst in range(2):
            for par in range(2):
                t_k = pr.dma(a, "kdup", kdup[64 * dst:64 * dst + 64, par::2, :],
                             pj[64 * par:64 * par + 64, 8:10, :])
        vt = ax.take(3, NKV * P)
        keys = [(0, 128), (128, 128), (256, 16)]
        for kt, (k0, kn) in enumerate(keys):
            for c in range(2):
                b = bank[(2 * kt + c) % 4]
                t = pe.do(pe.eng.transpose, b[0:kn, 0:P], pj[:, 10 + c, k0:k0 + kn], self.c("ident"),
                          after=[d.done.now()])
                dst = vt[0:kn, kt, 2 * P * c:2 * P * (c + 1)].rearrange("p (a b d) -> p a b d", a=2, b=2)
                for twin in range(2):
                    d.do(d.eng.tensor_copy, dst[:, :, twin, :],
                         b[0:kn, 0:P].rearrange("p (a d) -> p a d", a=2), after=[t])
        self.attn = ax.take(8, T)
        qs = ax.take(2, T)
        ks = ax.take(L)
        vs = ax.take(3, P)
        s = ax.take(2, L)
        st = ax.take(2, 8)
        pt = ax.take(2, 3 * P)
        dist = self.c("dist").rearrange("p (q t) -> p q t", q=2)
        pr.join(t_k)
        def kv_head(kv):
            t_q = d.do(d.eng.tensor_scalar, qs, pj[:, ds(kv * 2, 2), NMETA:L], HD ** -0.5, None,
                       ALU.mult, ALU.bypass, after=[pe.done.now()])
            d.do(self.copy, ks, kdup[:, ds(kv, 1), :])
            t_k = d.do(self.copy, vs[:, 0:2, :], vt[:, 0:2, ds(kv * P, P)])
            t_k = d.do(self.copy, vs[0:16, 2, :], vt[0:16, 2, ds(kv * P, P)])
            prev = [None, None]
            for u in range(8):
                hh, qt, b = u // 2, u % 2, u % 2
                half = 64 * (hh % 2)
                ps_s, ps_o = bank[b], bank[2 + b]
                t = pe.do(pe.eng.matmul, ps_s[:, 0:L], qs[half:half + 64, hh // 2, P * qt:P * qt + P],
                          ks[half:half + 64, :], start=True, stop=True, after=[t_k, prev[b]])
                d.do(d.eng.scalar_tensor_tensor, s[:, b, :], dist[:, qt, :], self.c("slopes")[:, ds(kv * 4 + hh, 1)],
                     ps_s[:, 0:L], ALU.mult, ALU.add, after=[t])
                yield
                m, nm, z, es, r = (st[:, b, k:k + 1] for k in range(5))
                sink = self.p("sinks")[:, ds(kv * 4 + hh, 1)]
                d.do(d.eng.reduce_max, m, s[:, b, :], AX.X)
                snk = st[:, b, 5:6]
                d.do(self.copy, snk, sink)
                t = d.do(d.eng.tensor_scalar, nm, m, sink, -1.0, ALU.max, ALU.mult)
                a.do(a.eng.activation, s[:, b, :], s[:, b, :], ACT.Exp, bias=nm, accum_out=z, after=[t])
                t = a.do(a.eng.activation, es, snk, ACT.Exp, bias=nm)
                yield
                d.do(d.eng.tensor_tensor, z, z, es, ALU.add, after=[t])
                d.do(d.eng.reciprocal, r, z)
                t = d.do(d.eng.tensor_scalar, s[:, b, :], s[:, b, :], r, None, ALU.mult, ALU.bypass)
                yield
                pe.wait(t)
                for kt, (k0, kn) in enumerate(keys):
                    mm = pe.eng.transpose(ps_s[0:kn, P * kt:P * kt + P], s[:, b, k0:k0 + kn], self.c("ident"))
                t = pe.done.add(mm)
                yield
                d.do(d.eng.tensor_copy, pt[:, b, 0:2 * P], ps_s[:, 0:2 * P], after=[t])
                t = d.do(d.eng.tensor_copy, pt[0:16, b, 2 * P:], ps_s[0:16, 2 * P:3 * P])
                yield
                pe.wait(t)
                for kt, (k0, kn) in enumerate(keys):
                    mm = pe.eng.matmul(ps_o[:, 0:P], vs[0:kn, kt, :], pt[0:kn, b, P * kt:P * kt + P],
                                       start=kt == 0, stop=kt == 2)
                t = pe.done.add(mm)
                prev[b] = d.do(self.copy, self.attn[half:half + 64, ds(kv * 2 + hh // 2, 1), P * qt:P * qt + P],
                               ps_o[half:half + 64, 0:P], after=[t])
                yield

        return kv_head

    def attention_end(self):
        pr, ar, bank = self.prog, self.arena, self.bank
        pr.join()
        ar.reset(20 * L)
        sq = ar.take(8, T)
        self.feature_rms("rms_attn", self.attn, 8, T, 1e-6, sq, bank[0])
        self.normalise("norm_attn", self.attn, self.p("attn_out_g"), self.mix[:, :, :], 8, T)
        pr.join()

    def ssm(self, kv_head):
        d, a, pe, pr, bank, io = self.dve, self.act, self.pe, self.prog, self.bank, self.io
        pj, ar, g = self.pj, self.arena, self.gemm
        G, S, N = 64, 64, 16
        ar.reset(20 * L)
        lre, lim = self.p("lam_re"), self.p("lam_im")
        pr.join()
        p1, p2 = ar.take(G), ar.take(G)
        r, turns = ar.take(G), ar.take(G)
        b1, b2 = ar.take(8, P), ar.take(8, P)
        l1, l2 = ar.take(G, N), ar.take(G, N)
        keep = ar.at
        t_in = [pr.dma(a, "ssm_in", b1, io["ssm_b1"]), pr.dma(a, "ssm_in", b2, io["ssm_b2"])]
        t0, t1, t2, t3, t4, t5, whole = (ar.take(G) for _ in range(7))
        cr, ci, tc = ar.take(G, N), ar.take(G, N), ar.take(G, N)
        t_in += [pr.dma(a, "ssm_in", cr, io["ssm_cr"]), pr.dma(a, "ssm_in", ci, io["ssm_ci"])]

        def ts(o, x, s1, s2, o1, o2=ALU.bypass, after=()):
            return d.do(d.eng.tensor_scalar, o, x, s1, s2, o1, o2, after=after)

        def tt(o, x, y, op, after=()):
            return d.do(d.eng.tensor_tensor, o, x, y, op, after=after)
        wh = self.whole_i32
        self.exp_precise(t0, self.p("log_step"), wh, t1)
        tt(t1, lre, t0, ALU.mult)
        self.exp_precise(r, t1, wh, t2)
        tt(t1, lim, t0, ALU.mult)
        ts(turns, t1, 1.0 / (2 * np.pi), MAGIC, ALU.mult, ALU.add)
        ts(turns, turns, -MAGIC, None, ALU.add)
        for part in (6.28125, 1.9350051879882812e-3, 3.0199159819e-7):
            d.do(d.eng.scalar_tensor_tensor, t1, turns, -part, t1, ALU.mult, ALU.add)
        ts(turns, t1, 1.0 / (2 * np.pi), 0.5, ALU.mult, ALU.min)
        ts(turns, turns, -0.5, None, ALU.max)
        a.do(a.eng.activation, t2, turns, ACT.Sin, scale=TWO_PI_BELOW, after=[d.done.now()])
        t = a.do(a.eng.activation, t3, turns, ACT.Sin, scale=TWO_PI_BELOW / 2)
        tt(t3, t3, t3, ALU.mult, after=[t])
        ts(t3, t3, -2.0, None, ALU.mult)
        tt(t2, t2, r, ALU.mult)
        tt(t3, t3, r, ALU.mult)
        ts(t4, r, -1.0, None, ALU.add)
        tt(t3, t3, t4, ALU.add)
        tt(t4, lre, lre, ALU.mult)
        tt(t5, lim, lim, ALU.mult)
        tt(t4, t4, t5, ALU.add)
        d.do(d.eng.reciprocal, t4, t4)
        tt(t0, t3, lre, ALU.mult)
        tt(t5, t2, lim, ALU.mult)
        tt(t0, t0, t5, ALU.add)
        tt(t0, t0, t4, ALU.mult)
        tt(t1, t2, lre, ALU.mult)
        tt(t5, t3, lim, ALU.mult)
        tt(t1, t1, t5, ALU.subtract)
        tt(t1, t1, t4, ALU.mult)
        d.do(d.eng.tensor_copy, p1[0:64, :], t0[0:64, :])
        d.do(d.eng.tensor_scalar, p1[64:, :], t1[64:, :], -1.0, None, ALU.mult, ALU.bypass)
        d.do(d.eng.tensor_scalar, p2[0:64, :], t1[0:64, :], -1.0, None, ALU.mult, ALU.bypass)
        d.do(d.eng.tensor_scalar, p2[64:, :], t0[64:, :], -1.0, None, ALU.mult, ALU.bypass)
        p1b = p1.unsqueeze(2).broadcast_to((P, G, N))
        p2b = p2.unsqueeze(2).broadcast_to((P, G, N))
        tt(l1, cr, p1b, ALU.mult, after=[t_in[-1]])
        tt(tc, ci, p2b, ALU.mult)
        tt(l1, l1, tc, ALU.add)
        tt(l2, cr, p2b, ALU.mult)
        tt(tc, ci, p1b, ALU.mult)
        tt(l2, l2, tc, ALU.subtract)
        ts(b2[:, :, 64:], b2[:, :, 64:], -1.0, None, ALU.mult)
        pr.join()

        ar.reset(keep)
        lb1, lb2 = ar.take(8, P), ar.take(8, P)
        lp1, lp2 = ar.take(8 * (P + N)), ar.take(8 * (P + N))
        w, cs, sn = ar.take(8, L), ar.take(8, L), ar.take(8, L)
        z = w
        t_u = ar.take(L)
        y = self.mix[:, 8:16, :]
        for lp in (lp1, lp2):
            d.do(d.eng.memset, lp, 0.0)
        mask = self.c("group_mask").unsqueeze(2).broadcast_to((P, 8, P))
        steps = self.c("steps")
        blocks1 = lp1.rearrange("p (j x) -> p j x", x=P + N)[:, :, 0:N]
        blocks2 = lp2.rearrange("p (j x) -> p j x", x=P + N)[:, :, 0:N]
        pr.join()
        pair = self.gemm.psum[2:4]

        def channels(c):
            pe_before = pe.done.now()
            d.wait(pe_before)
            tt(lb1, b1[:, ds(c, 1), :].broadcast_to((P, 8, P)), mask, ALU.mult)
            tt(lb2, b2[:, ds(c, 1), :].broadcast_to((P, 8, P)), mask, ALU.mult)
            d.do(self.copy, blocks1, l1[:, ds(c * 8, 8), :])
            d.do(self.copy, blocks2, l2[:, ds(c * 8, 8), :])
            t_w = d.do(self.copy, t_u, pj[:, ds(12 + c, 1), :])
            yield
            for j in range(8):
                t = d.do(d.eng.tensor_scalar, w[:, j, :], steps, turns[:, ds(c * 8 + j, 1)], None,
                         ALU.mult, ALU.bypass, chain=j == 0)
            yield
            ts(cs, w, MAGIC, -MAGIC, ALU.add, ALU.add)
            yield
            t = tt(w, w, cs, ALU.subtract)
            t_s = a.do(a.eng.activation, sn, w, ACT.Sin, scale=TWO_PI_BELOW, after=[t])
            t = d.do(d.eng.scalar_tensor_tensor, w, w, -1.0, w, ALU.mult, ALU.max, after=[t_s])
            t_s = a.do(a.eng.activation, cs, w, ACT.Sin, scale=-TWO_PI_BELOW, bias=self.c("half_pi"), after=[t])
            yield
            yield
            pe.wait(t_w)
            freed = [None, None]
            for j in range(8):
                b = 0
                pe.do(pe.eng.matmul, pair[0][:, 0:L], lb1[:, j, :], t_u, start=True, stop=True, after=[freed[b]], chain=False)
                t = pe.do(pe.eng.matmul, pair[1][:, 0:L], lb2[:, j, :], t_u, start=True, stop=True, chain=False)
                d.wait(t)
                d.do(d.eng.tensor_tensor, w[:, j, :], cs[:, j, :], pair[0][:, 0:L], ALU.mult, after=[t_s])
                freed[b] = d.do(d.eng.tensor_tensor, self.rstd[:, 0:L], sn[:, j, :], pair[1][:, 0:L], ALU.mult)
                tt(w[:, j, :], w[:, j, :], self.rstd[:, 0:L], ALU.add)
                d.do(d.eng.tensor_tensor_scan, w[:, j, :], self.rcol(r, c * 8 + j), w[:, j, :], 0.0, ALU.mult, ALU.add)
                yield
            tt(cs, cs, z, ALU.mult)
            yield
            t = tt(sn, sn, z, ALU.mult)
            yield
            pe.wait(t)
            for j in range(8):
                pe.eng.matmul(pair[0][:, 0:L], lp1[:, P * j:P * j + P], cs[:, j, :], start=j == 0, stop=False)
                mm = pe.eng.matmul(pair[0][:, 0:L], lp2[:, P * j:P * j + P], sn[:, j, :], start=False, stop=j == 7)
            t = pe.done.add(mm)
            d.do(d.eng.tensor_scalar, t_u, t_u, self.p("ssm_d")[:, ds(c, 1)], None, ALU.mult, ALU.bypass, after=[t])
            yield
            tt(y[:, ds(c, 1), :], t_u[:, NMETA:], pair[0][:, NMETA:L], ALU.add)

        def two(c):
            yield from channels(c)
            yield from channels(c + 1)

        with pr.loop(NKV, "mixers1") as turn:
            beside(lockstep([kv_head(turn), two(turn * 2)]), 56,
                   [self.modulation_group(turn * 6 + n) for n in range(6)])
        self.join_gemm()
        self.attention_end()
        ar.reset(20 * L)
        t3, gl, gate = ar.take(8, T), ar.take(8, T), ar.take(8, T)
        tt(t3, y, y, ALU.mult)
        ts(t3, t3, 0.044715, 1.0, ALU.mult, ALU.add)
        t = tt(t3, t3, y, ALU.mult)
        t = a.do(a.eng.activation, t3, t3, ACT.Sigmoid, scale=2 * np.sqrt(2 / np.pi), after=[t])
        t = tt(gl, y, t3, ALU.mult, after=[t])

        def evacuate(chunk, m, psum, summed):
            d.wait(summed)
            g.drained[m].add(d.eng.tensor_scalar(gate[:, ds(chunk, 1), :], psum, self.p("b_glu")[:, ds(chunk, 1)],
                                                 None, ALU.add, ALU.bypass))
        g.run("w_glu", io["w_glu"], 8, 1024, lambda kc: gl[:, kc, :], T, evacuate, after=[t], groups=2)
        self.join_gemm()
        t = a.do(a.eng.activation, gate, gate, ACT.Sigmoid)
        t = tt(gl, gl, gate, ALU.mult, after=[t])
        pr.join()
        self.feature_rms("rms_ssm", gl, 8, T, 1e-6, t3, bank[0])
        self.normalise("norm_ssm", gl, self.p("ssm_out_g"), self.mix[:, 8:16, :], 8, T)
        pr.join()

    def rcol(self, r, col):
        return r[:, ds(col, 1)].broadcast_to((P, L))

    def add_to_residual(self, dst):
        d, g = self.dve, self.gemm

        def evacuate(chunk, m, psum, summed):
            d.wait(summed)
            g.drained[m].add(d.eng.tensor_tensor(dst[:, ds(chunk, 1), :], dst[:, ds(chunk, 1), :], psum, ALU.add))
        return evacuate

    def squared_relu(self, hid):
        d, a, g, pr = self.dve, self.act, self.gemm, self.prog

        def evacuate(chunk, m, psum, summed):
            tmp = self.sq_tmp[:, m % 4, :]
            d.wait(summed)
            t = pr.relu_done[m % 4].add(d.eng.tensor_scalar(tmp, psum, 0.0, None, ALU.max, ALU.bypass))
            d.wait(t)
            g.drained[m].add(d.eng.tensor_tensor(hid[:, ds(chunk, 1), :], tmp, tmp, ALU.mult))
        return evacuate

    def block1_mlp(self):
        d, g, io, pr = self.dve, self.gemm, self.io, self.prog
        x = self.res[:, :, NMETA:]
        g.run("w_out", io["w_out"], KD, DM, lambda kc: self.mix[:, kc, :], T, self.add_to_residual(x), groups=2)
        self.join_gemm()
        self.arena.reset()
        hid = self.arena.take(DFF // P, T)
        self.sq_tmp = self.arena.take(4, T)
        pr.join()
        self.feature_rms("rms2", x, KD, T, 1e-6, self.mix[:, :, :], self.bank[0])
        t = self.normalise("norm2", x, self.p("norm_mlp_g"), self.xin[:, :, :], KD, T)
        g.run("w_up", io["w_up"], KD, DFF, lambda kc: self.xin[:, kc, 0:T], T, self.squared_relu(hid), after=[t], groups=2)
        self.join_gemm()
        g.run("w_down", io["w_down"], DFF // P, DM, lambda kc: hid[:, kc, :], T, self.add_to_residual(x), groups=2)
        self.modulation_end()


    def modulation_begin(self):
        d, a = self.dve, self.act
        t = a.do(a.eng.activation, self.cc_sig, self.p("c"), ACT.Sigmoid)
        d.do(d.eng.tensor_tensor, self.cc, self.p("c"), self.cc_sig, ALU.mult, after=[t])
        self.prog.join()

    def modulation_group(self, group):
        a, g, pr = self.act, self.gemm, self.prog
        ccv = self.cc.rearrange("p (c m) -> p c m", m=2)

        def evacuate(group, psum, summed):
            a.wait(summed, pr.dma_sems["mods"].now())
            t = g.drained[0].add(a.eng.activation(self.mods_row[0:2, :], psum, ACT.Copy))
            pr.dma(a, "mods", self.io["s_mods"][:, ds(group * 512, 512)], self.mods_row[0:2, :], after=[t])
        return g.wide_group(g.rows(self.io["w_ada"]), KD, lambda kc: ccv[:, kc, :], evacuate, group), 17

    def modulation_end(self):
        d, a, pe, pr = self.dve, self.act, self.pe, self.prog
        self.join_gemm()
        pr.join(pr.dma_sems["mods"].now())
        rows = self.mix[0:96, 0:2, 0:P]
        for r in range(2):
            t = pr.dma(a, "mods", rows[:, r, :], self.io["s_mods"][r:r + 1, :].rearrange("a (c p) -> (a c) p", p=P))
        pe.wait(t)
        for r in range(2):
            t = pe.do(pe.eng.transpose, self.bank[r][:, 0:96], rows[:, r, :], self.c("ident")[0:96, 0:96])
            d.do(d.eng.tensor_tensor, self.mods[:, :, r], self.bank[r][:, 0:96], self.p("b_ada"), ALU.add, after=[t])
        for c in (16, 64):
            d.do(d.eng.tensor_scalar, self.mods[:, c:c + 16, :], self.mods[:, c:c + 16, :], 1.0, None, ALU.add, ALU.bypass)
        pr.join()

    def modulate(self, src, dst, shift, scale, which):
        d = self.dve
        for c in range(KD):
            t = d.do(d.eng.tensor_scalar, dst[:, c, :], src[:, c, :], self.mods[:, scale + c, which:which + 1],
                     self.mods[:, shift + c, which:which + 1], ALU.mult, ALU.add, chain=c == 0)
        return t

    def storing(self, scratch, tokens, key, func=ACT.Copy):
        d, a, g, pr = self.dve, self.act, self.gemm, self.prog
        stage = self.stage
        view = scratch.rearrange("(c p) t -> p c t", p=P)

        def evacuate(chunk, m, psum, summed):
            n = m % 4
            a.wait(summed, pr.dma_sems["st%d" % n].now())
            t = g.drained[m].add(a.eng.activation(stage[:, n, 0:tokens], psum, func))
            pr.dma(a, "st%d" % n, view[:, ds(chunk, 1), :], stage[:, n, 0:tokens], after=[t])
        return evacuate

    def block2_project(self):
        d, a, pe, pr, g, io = self.dve, self.act, self.pe, self.prog, self.gemm, self.io
        self.arena.reset()
        self.stage = self.arena.take(4, 512)
        ab_w = self.arena.take(KD, 32)
        x = self.res[:, :, NMETA:]
        ctx = self.xin[:, :, T:]
        pr.join()
        t_in = pr.dma(a, "ctx", ctx, io["ctxT"].rearrange("(c p) t -> p c t", p=P))
        t_ab = pr.dma(a, "ctx", ab_w, io["w_in2"][:, 4608:4640].rearrange("(c p) n -> p c n", p=P))
        self.modulate(x, self.xin[:, :, 0:T], 0, 16, 0)
        d.wait(t_ab)
        t = self.modulate(ctx, ctx, 0, 16, 1)
        pr.join()
        for tt in range(4):
            bank = self.bank[tt]
            for kc in range(KD):
                mm = pe.eng.matmul(bank[:, 0:32], self.xin[:, kc, P * tt:P * tt + P], ab_w[:, kc, :], start=kc == 0, stop=kc == KD - 1)
            t1 = pe.done.add(mm)
            d.do(d.eng.tensor_copy, self.ab[:, tt, :], bank[:, 0:32], after=[t1])
        g.run("w_in2a", io["w_in2"][:, 0:4608], KD, 4608, lambda kc: self.xin[:, kc, :], 2 * T,
              self.storing(io["s_state"], 2 * T, "a"), after=[t])
        self.join_gemm()
        self.stage = self.arena.tensor[:, ARENA - 1024:].rearrange("p (m t) -> p m t", m=4)
        self.store_read = self.storing(io["s_read"], T, "b")
        self.store_gate = self.storing(io["s_gate"], T, "c", ACT.Sigmoid)
        g.run("w_in2b", io["w_in2"][:, 4640:4640 + 7 * 512], KD, 7 * 512, lambda kc: self.xin[:, kc, 0:T], T, self.store_read)
        self.join_gemm()
        self.stored()
        self.branch = [self.xin[:, 0:8, 0:T], self.xin[:, 0:8, T:], self.xin[:, 8:16, T:]]

    def read_group(self, group):
        return self.gemm.group(self.gemm.rows(self.io["w_in2"][:, 4640:4640 + 6656]), KD,
                               lambda kc: self.xin[:, kc, 0:T], T, self.store_read, group), 36

    def gate_group(self, group):
        return self.gemm.group(self.gemm.rows(self.io["w_in2"][:, 11296:]), KD,
                               lambda kc: self.xin[:, kc, 0:T], T, self.store_gate, group), 36

    def stored(self):
        self.prog.join(*[self.prog.dma_sems["st%d" % m].now() for m in range(4)])

    def hgrn2(self):
        d, a, pe, pr, io, ar = self.dve, self.act, self.pe, self.prog, self.io, self.arena
        NT = 4
        C = P + 2
        fz, k, e1 = [ar.take(NT, P) for _ in range(2)], [ar.take(NT, P) for _ in range(2)], [ar.take(NT, P) for _ in range(2)]
        cum = [ar.take(NT, C) for _ in range(2)]
        ks, kst = [ar.take(NT, P) for _ in range(2)], e1
        att, qe = [ar.take(2, P) for _ in range(2)], [ar.take(2, P) for _ in range(2)]
        lev = [ar.take(2, P) for _ in range(2)]
        st = [ar.take(P) for _ in range(2)]
        eend = [ar.take(NT) for _ in range(2)]
        vf, vt, q, gt = ar.take(NT, P), ar.take(NT, P), ar.take(2, P), ar.take(2, P)
        ones = ar.take(P)
        o, sq = ar.take(T), ar.take(T)
        lb = ar.take(2, 8)
        lb1 = ar.take(2, 8)
        state = io["s_state"].rearrange("(c p) t -> p c t", p=P)
        read = io["s_read"].rearrange("(c p) t -> p c t", p=P)
        logits = self.p("lb_logits").rearrange("p (a c) -> p a c", a=2)
        d.do(d.eng.tensor_tensor, lb, logits, logits, ALU.subtract)
        t = a.do(a.eng.activation, lb, lb, ACT.Exp, after=[d.done.now()])
        d.do(d.eng.reciprocal, lb1, lb, after=[t])
        d.do(d.eng.tensor_tensor, lb1, lb1, lb, ALU.mult)
        d.do(d.eng.tensor_tensor, lb, lb1, lb1, ALU.subtract)
        d.do(d.eng.tensor_scalar, lb1, lb, -1.0, 1.0, ALU.mult, ALU.add)
        d.do(d.eng.memset, ones, 1.0)
        for r in range(2):
            d.do(d.eng.memset, cum[r][:, :, 0:1], 0.0)
        pr.join()
        po = self.gemm.psum[2:4]

        def direction(r, h, ch):
            fwd = r == 0
            bl = bs = bt = po[r]
            f, kk, cm = fz[r], k[r], cum[r]
            lbc, lb1c = lb[:, r, ds(h, 1)], lb1[:, r, ds(h, 1)]
            ch(d, d.eng.tensor_scalar, e1[r], f, -1.0, LN_1E30, ALU.mult, ALU.min)
            yield
            ch(a, a.eng.activation, e1[r], e1[r], ACT.Exp)
            yield
            ch(d, d.eng.tensor_scalar, f, e1[r], 1.0, None, ALU.add, ALU.bypass)
            ch(d, d.eng.reciprocal, f, f)
            ch(d, d.eng.tensor_tensor, kk, e1[r], f, ALU.mult)
            ch(d, d.eng.tensor_scalar, kk, kk, lb1c, None, ALU.mult, ALU.bypass)
            ch(d, d.eng.tensor_scalar, f, f, lb1c, lbc, ALU.mult, ALU.add)
            ch(d, d.eng.tensor_scalar, f, f, 1e-30, None, ALU.max, ALU.bypass)
            ch(d, d.eng.tensor_scalar, ks[r], f, 2.0 ** -50, None, ALU.is_lt, ALU.bypass)
            ch(d, d.eng.tensor_scalar, e1[r], ks[r], 2.0 ** 50 - 1, 1.0, ALU.mult, ALU.add)
            ch(d, d.eng.tensor_tensor, f, f, e1[r], ALU.mult)
            yield
            ch(a, a.eng.activation, f, f, ACT.Ln)
            yield
            ch(d, d.eng.scalar_tensor_tensor, f, ks[r], -50 * float(np.log(2.0)), f, ALU.mult, ALU.add)
            for j in range(NT):
                ch(d, d.eng.tensor_tensor_scan, cm[:, j, 1:P + 1], ones, f[:, j, :], 0.0, ALU.mult, ALU.add)
            after, before, end = cm[:, :, 1:P + 1], cm[:, :, 0:P], cm[:, :, P:P + 1]
            if fwd:
                ch(d, d.eng.tensor_tensor, ks[r], end.broadcast_to((P, NT, P)), after, ALU.subtract)
            else:
                ch(d, d.eng.tensor_copy, ks[r], before)
            yield
            ch(a, a.eng.activation, ks[r], ks[r], ACT.Exp)
            ch(a, a.eng.activation, eend[r], cm[:, :, P], ACT.Exp)
            yield
            ch(d, d.eng.tensor_tensor, ks[r], ks[r], kk, ALU.mult)
            yield
            ch(pe, lambda: [pe.eng.transpose(bt[:, P * j:P * j + P], ks[r][:, j, :], self.c("ident")) for j in range(NT)][-1])
            yield
            ch(d, d.eng.tensor_copy, kst[r], bt[:, :])
            if fwd:
                ch(a, a.eng.activation, qe[r], after[:, 0:2, :], ACT.Exp)
            else:
                ch(d, d.eng.tensor_tensor, qe[r], end[:, 0:2, :].broadcast_to((P, 2, P)), before[:, 0:2, :], ALU.subtract)
                ch(a, a.eng.activation, qe[r], qe[r], ACT.Exp)
            yield
            ch(d, d.eng.tensor_tensor, qe[r], qe[r], q, ALU.mult)
            ch(pe, lambda: [pe.eng.matmul(bs[:, P * j:P * j + P], kk[:, j, :], q[:, j, :], start=True, stop=True) for j in range(2)][-1])
            yield
            ident = self.c("ident").unsqueeze(1).broadcast_to((P, 2, P))
            ch(d, d.eng.tensor_tensor, att[r], bs[:, 0:T].rearrange("p (j t) -> p j t", j=2), ident, ALU.mult)
            for level in range(7):
                half = P >> (level + 1)
                nb = P // (2 * half)
                m = lev[r]

                def halves(x):
                    v = x.rearrange("p j (b two n) -> p j b two n", two=2, n=half)
                    return v[:, :, :, 0, :], v[:, :, :, 1, :]
                mid = cm[:, 0:2, 0:P].rearrange("p j (b n) -> p j b n", n=2 * half)[:, :, :, half:half + 1].broadcast_to((P, 2, nb, half))
                c0, c1 = halves((after if fwd else before)[:, 0:2, :])
                m0, m1 = halves(m)
                k0, k1 = halves(kk[:, 0:2, :])
                q0, q1 = halves(q)
                for j in range(2):
                    ch(d, d.eng.tensor_tensor, m0[:, j], mid[:, j], c0[:, j], ALU.subtract)
                    ch(d, d.eng.tensor_tensor, m1[:, j], c1[:, j], mid[:, j], ALU.subtract)
                yield
                ch(a, a.eng.activation, m, m, ACT.Exp)
                yield
                for j in range(2):
                    ch(d, d.eng.tensor_tensor, m0[:, j], m0[:, j], (k0 if fwd else q0)[:, j], ALU.mult)
                    ch(d, d.eng.tensor_tensor, m1[:, j], m1[:, j], (q1 if fwd else k1)[:, j], ALU.mult)
                yield
                ch(pe, lambda: [pe.eng.matmul(bl[:, P * j:P * j + P], m[:, j, :], m[:, j, :], start=True, stop=True) for j in range(2)][-1])
                yield
                mask = self.masks[r][:, level, :].unsqueeze(1).broadcast_to((P, 2, P)).bitcast(mybir.dt.uint32)
                ch(d, self.copy, eend[r][:, 0:1], eend[r][:, 0:1])
                d.do(d.eng.copy_predicated, att[r], mask, bl[:, 0:T].rearrange("p (j t) -> p j t", j=2), chain=False)
                ch.last = [d.done.now()]
                yield
            order = (2, 3, 0, 1) if fwd else (3, 2, 1, 0)
            for n, j in enumerate(order):
                if j < 2:
                    def out():
                        pe.eng.matmul(po[r][:, P * j:P * j + P], vt[:, j, :], att[r][:, j, :], start=True, stop=False)
                        return pe.eng.matmul(po[r][:, P * j:P * j + P], st[r], qe[r][:, j, :], start=False, stop=True)
                    ch(pe, out)
                if n < 3:
                    ch(pe, lambda: pe.eng.matmul(bs[:, T:T + P], kst[r][:, j, :], vt[:, j, :], start=True, stop=True))
                    yield
                    if n == 0:
                        ch(d, d.eng.tensor_copy, st[r], bs[:, T:T + P])
                    else:
                        ch(d, d.eng.scalar_tensor_tensor, st[r], st[r], eend[r][:, j:j + 1], bs[:, T:T + P], ALU.mult, ALU.add)
                    yield

        flat = "p j t -> p (j t)"

        def load(h):
            for r in range(2):
                pr.dma(a, "mixer_in", fz[r].rearrange(flat), state[:, ds(h + 8 * r, 1), :])
            pr.dma(a, "mixer_in", vf.rearrange(flat), state[:, ds(h + 16, 1), :])
            pr.dma(a, "mixer_in", q.rearrange(flat), read[:, ds(h, 1), :])
            return pr.dma(a, "mixer_in", gt.rearrange(flat), read[:, ds(h + 8, 1), :])

        def strands(h):
            t = pe.do(lambda: [pe.eng.transpose(po[0][:, P * j:P * j + P], vf[:, j, :], self.c("ident")) for j in range(NT)][-1])
            t_v = d.do(d.eng.tensor_copy, vt, po[0][:, :], after=[t])
            t = a.do(a.eng.activation, sq, q.rearrange(flat), ACT.Sigmoid)
            t_q = d.do(d.eng.tensor_tensor, q.rearrange(flat), q.rearrange(flat), sq, ALU.mult, after=[t])
            t_g = a.do(a.eng.activation, gt, gt, ACT.Sigmoid)
            return [direction(r, h, Chain([t_q, t_g, t_v])) for r in range(2)]

        def finish(h):
            d.do(d.eng.tensor_copy, sq, po[1][:, 0:T], after=[pe.done.now(), a.done.now()])
            d.do(d.eng.tensor_tensor, o, po[0][:, 0:T], sq, ALU.add)
            self.head_norm_gate(o, sq, self.p("hg_norm_w"), gt.rearrange(flat), self.branch[1][:, ds(h, 1), :], po[1])
        return load, strands, finish

    def head_norm_gate(self, o, sq, w, gate, dst, bank):
        d, pe = self.dve, self.pe
        t = d.do(d.eng.tensor_tensor, sq, o, o, ALU.mult)
        t = pe.do(pe.eng.matmul, bank[:, 0:T], self.c("ones"), sq, start=True, stop=True, after=[t])
        self.rsqrt(sq, bank[:, 0:T], 1.0 / P, 1e-6, after=[t])
        d.do(d.eng.scalar_tensor_tensor, o, o, w, sq, ALU.mult, ALU.mult)
        d.do(d.eng.tensor_tensor, dst, o, gate, ALU.mult)

    def conv(self, dst, src, w, at, rows):
        d = self.dve
        y, x = (v.rearrange("p (r n) -> p r n", r=rows) for v in (dst, src))
        n = x.shape[2]
        d.do(d.eng.tensor_scalar, y, x, w(1), None, ALU.mult, ALU.bypass)
        d.do(d.eng.scalar_tensor_tensor, y[:, :, 1:], x[:, :, 0:n - 1], w(0), y[:, :, 1:], ALU.mult, ALU.add)
        return d.do(d.eng.scalar_tensor_tensor, y[:, :, 0:n - 1], x[:, :, 1:], w(2), y[:, :, 0:n - 1], ALU.mult, ALU.add)

    def deltanet(self):
        d, a, pe, pr, io, ar = self.dve, self.act, self.pe, self.prog, self.io, self.arena
        NT, W = 4, 512
        ident = self.c("ident")
        ar.reset()
        beta, gl, gc = ar.take(NT, 16), ar.take(NT, 16), ar.take(NT, 16)
        keep = ar.at
        state = io["s_state"].rearrange("(c p) t -> p c t", p=P)
        read = io["s_read"].rearrange("(c p) t -> p c t", p=P)
        raw, y, z, tm = ar.take(W), ar.take(W), ar.take(W), ar.take(W)
        kf, qf, kt, vt = (io[n] for n in ("s_kf", "s_qf", "s_kt", "s_vt"))
        pr.join()

        def taps(name, n, c):
            col = self.p(name).rearrange("p (j c) -> p j c", j=3)
            return lambda j: col[:, j, ds(c, 1)]

        def stream(name, rows, n, w_name, wn, tokens, finish):
            with pr.loop(n, name) as c:
                t = pr.dma(a, "mixer_in", raw[:, 0:tokens], rows(c), after=[d.done.now(), pe.done.now()])
                d.wait(t, a.done.now(), pe.done.now(), pr.dma_sems["dn_out"].now())
                t = self.conv(y[:, 0:T], raw[:, 0:T], taps(w_name, wn, c), 0, 4)
                if tokens > T:
                    t = self.conv(y[:, T:], raw[:, T:], taps(w_name, wn, c), 0, 1)
                t = a.do(a.eng.activation, z[:, 0:tokens], y[:, 0:tokens], ACT.Sigmoid, after=[t])
                d.do(d.eng.tensor_tensor, y[:, 0:tokens], y[:, 0:tokens], z[:, 0:tokens], ALU.mult, after=[t])
                finish(c)
            pr.join(pr.dma_sems["dn_out"].now())

        def unit_length(dst, c, tokens, scale):
            t = d.do(d.eng.tensor_tensor, z[:, 0:tokens], y[:, 0:tokens], y[:, 0:tokens], ALU.mult)
            t = pe.do(pe.eng.matmul, self.bank[0][:, 0:tokens], self.c("ones"), z[:, 0:tokens], start=True, stop=True, after=[t])
            self.rsqrt(z[:, 0:tokens], self.bank[0][:, 0:tokens], 1.0, 1e-6, after=[t])
            t = d.do(d.eng.scalar_tensor_tensor, y[:, 0:tokens], y[:, 0:tokens], scale, z[:, 0:tokens], ALU.mult, ALU.mult)
            pr.dma(a, "dn_out", dst.rearrange("(c p) t -> p c t", p=P)[:, ds(c, 1), :], y[:, 0:tokens], after=[d.done.now()])

        def to_tokens(dst, c):
            t = pe.do(lambda: [pe.eng.transpose(self.bank[1][:, P * j:P * j + P], y[:, P * j:P * j + P], ident) for j in range(NT)][-1],
                      after=[d.done.now()])
            t = d.do(d.eng.tensor_copy, tm, self.bank[1][:, :], after=[t])
            pr.dma(a, "dn_out", dst.rearrange("(c p) t -> p c t", p=P)[:, ds(c, 1), :], tm, after=[t])

        def finish_k(c):
            unit_length(kf, c, W, 1.0)
            to_tokens(kt, c)
        stream("dn_k", lambda c: state[:, ds(c + 24, 1), :], 4, "dn_conv_k", 4, W, finish_k)
        stream("dn_q", lambda c: read[:, ds(c + 16, 1), :], 4, "dn_conv_q", 4, T, lambda c: unit_length(qf, c, T, P ** -0.5))
        stream("dn_v", lambda c: state[:, ds(c + 28, 1), :], 8, "dn_conv_v", 8, W, lambda c: to_tokens(vt, c))

        ar.reset(keep)
        x, u, v, w2 = (ar.take(NT * 16) for _ in range(4))
        ea, tmp16 = ar.take(16), ar.take(16)

        def per_tile(c):
            return c.unsqueeze(1).broadcast_to((P, NT, 16))
        sh = "p (j c) -> p j c"
        x3 = x.rearrange(sh, j=NT)
        a.do(a.eng.activation, beta, self.ab[:, :, 16:32], ACT.Sigmoid)
        d.do(d.eng.tensor_tensor, x3, self.ab[:, :, 0:16], per_tile(self.p("dt_bias")), ALU.add)
        d.do(d.eng.scalar_tensor_tensor, u, x, -1.0, x, ALU.mult, ALU.min)
        self.exp_precise(v, u, self.whole_i32, w2)
        d.do(d.eng.tensor_scalar, u, v, 2.0, None, ALU.add, ALU.bypass)
        d.do(d.eng.reciprocal, u, u)
        d.do(d.eng.tensor_tensor, v, v, u, ALU.mult)
        d.do(d.eng.tensor_tensor, u, v, v, ALU.mult)
        d.do(d.eng.tensor_scalar, w2, u, 1.0 / 17, 1.0 / 15, ALU.mult, ALU.add)
        for n in (13, 11, 9, 7, 5, 3, 1):
            d.do(d.eng.tensor_tensor, w2, w2, u, ALU.mult)
            d.do(d.eng.tensor_scalar, w2, w2, 1.0 / n, None, ALU.add, ALU.bypass)
        d.do(d.eng.scalar_tensor_tensor, w2, w2, 2.0, v, ALU.mult, ALU.mult)
        d.do(d.eng.tensor_scalar, x, x, 0.0, None, ALU.max, ALU.bypass)
        d.do(d.eng.tensor_tensor, x, x, w2, ALU.add)
        self.exp_precise(ea, self.p("a_log"), self.whole_i32[:, 0:16], tmp16)
        d.do(d.eng.tensor_tensor, gl, x3, per_tile(ea), ALU.mult)
        d.do(d.eng.tensor_scalar, gl, gl, -1.0, None, ALU.mult, ALU.bypass)
        for j in range(NT):
            b = self.bank[j]
            t = d.done.now()
            pe.do(pe.eng.matmul, b[:, 0:8], self.upto[0], gl[:, j, 0:8], start=True, stop=True, after=[t])
            t = pe.do(pe.eng.matmul, b[:, 8:16], self.upto[1], gl[:, j, 8:16], start=True, stop=True)
            d.do(d.eng.tensor_copy, gc[:, j, :], b[:, 0:16], after=[t])
        pr.join()

        ar.reset(keep)
        kf_h, qf_h, kt_h, vt_h = ar.take(NT, P), ar.take(2, P), ar.take(NT, P), ar.take(NT, P)
        B = []
        hg_load, hg_strands, hg_finish = self.hgrn2()
        for r in range(2):
            B.append(dict(y=ar.take(NT, P), dec=ar.take(NT, P), nt=ar.take(NT, P), x=ar.take(NT, P),
                          xt=ar.take(NT, P), mt=ar.take(NT, P), att=ar.take(2, P), qe=ar.take(2, P),
                          vn=ar.take(P), s=ar.take(P), cols=ar.take(6, NT)))
        o, zs, zg = ar.take(T), ar.take(T), ar.take(T)
        banks = [self.bank[0:2], self.bank[2:4]]

        def each(op, out, lhs, rhs, n=NT):
            return lambda: [op(out[:, P * j:P * j + P], lhs[:, j, :], rhs(j), start=True, stop=True) for j in range(n)][-1]

        def tiles(b, n=NT):
            return b[:, 0:n * P].rearrange("p (j t) -> p j t", j=n)

        def direction(r, head, ch):
            fwd = r == 0
            b0, b1 = banks[r]
            v = B[r]
            y, dec, nt, x, xt, mt, att, qe, vn, s = (v[n] for n in ("y", "dec", "nt", "x", "xt", "mt", "att", "qe", "vn", "s"))
            g_, gc_, be, eg, el, ek = (v["cols"][:, i, :] for i in range(6))
            hd = head + 8 * r
            for dst, src in ((g_, gl), (gc_, gc), (be, beta)):
                ch(d, self.copy, dst, src[:, :, ds(hd, 1)])
            ch(d, d.eng.tensor_scalar, y, g_.unsqueeze(2).broadcast_to((P, NT, P)), 1.0, None, ALU.mult, ALU.bypass)
            ch(d, d.eng.tensor_scalar, mt, be.unsqueeze(2).broadcast_to((P, NT, P)), 1.0, None, ALU.mult, ALU.bypass)
            yield
            ch(pe, each(pe.eng.matmul, b0, y, lambda j: self.upto[r]))
            ch(pe, each(pe.eng.matmul, b1, mt, lambda j: ident))
            yield
            for j in range(NT):
                ch(d, d.eng.tensor_scalar, dec[:, j, :], b0[:, P * j:P * j + P], gc_[:, j:j + 1], 0.0, ALU.subtract, ALU.min)
            end = P - 1 if fwd else 0
            ch(d, d.eng.tensor_copy, el, tiles(b0)[:, :, end])
            ch(d, d.eng.tensor_tensor, ek, el, gc_, ALU.subtract)
            yield
            ch(a, a.eng.activation, dec, dec, ACT.Exp)
            ch(a, a.eng.activation, qe, tiles(b0, 2), ACT.Exp)
            ch(a, a.eng.activation, eg, gc_, ACT.Exp)
            ch(a, a.eng.activation, el, el, ACT.Exp)
            ch(a, a.eng.activation, ek, ek, ACT.Exp)
            yield
            ch(d, d.eng.tensor_tensor, qe, qe, qf_h, ALU.mult)
            ch(d, d.eng.tensor_tensor, nt, dec, tiles(b1), ALU.mult)
            ch(d, d.eng.tensor_tensor, dec[:, 0:2, :], dec[:, 0:2, :], self.upto[r].unsqueeze(1).broadcast_to((P, 2, P)), ALU.mult)
            ch(pe, each(pe.eng.matmul, b0, kf_h, lambda j: kf_h[:, j, :]))
            ch(pe, each(pe.eng.matmul, b1, kf_h, lambda j: qf_h[:, j, :], 2))
            yield
            ch(d, d.eng.tensor_tensor, nt, nt, tiles(b0), ALU.mult)
            ch(d, d.eng.tensor_tensor, att, dec[:, 0:2, :], tiles(b1, 2), ALU.mult)
            idb = ident.unsqueeze(1).broadcast_to((P, NT, P))
            ch(d, d.eng.tensor_copy, x, idb)
            ch(d, d.eng.tensor_copy, xt, idb)
            for level in range(6, -1, -1):
                mask = self.masks[r][:, level, :].unsqueeze(1).broadcast_to((P, NT, P))
                ch(d, d.eng.tensor_tensor, mt, nt, mask, ALU.mult)
                yield
                ch(pe, each(pe.eng.matmul, b0, mt, lambda j: x[:, j, :]))
                yield
                ch(a, a.eng.copy, y, tiles(b0))
                yield
                if level:
                    ch(pe, each(pe.eng.matmul, b0, xt, lambda j: y[:, j, :]))
                ch(pe, each(pe.eng.matmul, b1, y, lambda j: xt[:, j, :]))
                yield
                if level:
                    ch(d, d.eng.tensor_tensor, x, x, tiles(b0), ALU.subtract)
                ch(d, d.eng.tensor_tensor, xt, xt, tiles(b1), ALU.subtract)
            colb = lambda c: c.unsqueeze(2).broadcast_to((P, NT, P))
            ch(d, d.eng.tensor_tensor, nt, vt_h, colb(be), ALU.mult)
            ch(d, d.eng.tensor_tensor, eg, eg, be, ALU.mult)
            ch(d, d.eng.tensor_tensor, mt, kt_h, colb(eg), ALU.mult)
            ch(d, d.eng.tensor_tensor, x, kt_h, colb(ek), ALU.mult)
            yield
            ch(pe, each(pe.eng.matmul, b0, mt, lambda j: xt[:, j, :]))
            yield
            ch(d, d.eng.tensor_scalar, y, tiles(b0), -1.0, None, ALU.mult, ALU.bypass)
            order = (2, 3, 0, 1) if fwd else (3, 2, 1, 0)
            for n, j in enumerate(order):
                def solve():
                    mm = pe.eng.matmul(b1[:, 0:P], xt[:, j, :], nt[:, j, :], start=True, stop=n == 0)
                    return mm if n == 0 else pe.eng.matmul(b1[:, 0:P], y[:, j, :], s, start=False, stop=True)
                ch(pe, solve)
                yield
                ch(d, d.eng.tensor_copy, vn, b1[:, 0:P])
                yield
                if j < 2:
                    def out():
                        pe.eng.matmul(b0[:, P * j:P * j + P], vn, att[:, j, :], start=True, stop=False)
                        return pe.eng.matmul(b0[:, P * j:P * j + P], s, qe[:, j, :], start=False, stop=True)
                    ch(pe, out)
                if n < 3:
                    ch(pe, lambda: pe.eng.matmul(b1[:, P:2 * P], x[:, j, :], vn, start=True, stop=True))
                    yield
                    if n == 0:
                        ch(d, d.eng.tensor_copy, s, b1[:, P:2 * P])
                    else:
                        ch(d, d.eng.scalar_tensor_tensor, s, s, el[:, j:j + 1], b1[:, P:2 * P], ALU.mult, ALU.add)
                    yield

        with pr.loop(4, "mixers2") as h:
            for twin in range(2):
                head = h * 2 + twin
                a.wait(d.done.now(), pe.done.now())
                hg_load(head)
                flat = "p j t -> p (j t)"

                def rows(src, c):
                    return src.rearrange("(c p) t -> p c t", p=P)[:, ds(c, 1), :]
                if twin == 0:
                    pr.dma(a, "mixer_in", kf_h.rearrange(flat), rows(kf, h))
                    pr.dma(a, "mixer_in", qf_h.rearrange(flat), rows(qf, h))
                    pr.dma(a, "mixer_in", kt_h.rearrange(flat), rows(kt, h))
                pr.dma(a, "mixer_in", vt_h.rearrange(flat), rows(vt, head))
                t = pr.dma(a, "mixer_in", zg, read[:, ds(head + 20, 1), :])
                for e in (a, d, pe):
                    e.wait(t, a.done.now(), d.done.now(), pe.done.now())
                sg = a.do(a.eng.activation, zs, zg, ACT.Sigmoid)
                t_z = d.do(d.eng.tensor_tensor, zg, zg, zs, ALU.mult, after=[sg])
                strands = hg_strands(head) + [direction(r, head, Chain([t_z])) for r in range(2)]
                work = [self.read_group(h + 7), self.gate_group(h * 2), self.gate_group(h * 2 + 1), self.gate_group(h + 8)]
                beside(lockstep(strands), 56, work[2 * twin:2 * twin + 2])
                hg_finish(head)
                d.do(d.eng.tensor_copy, zs, banks[1][0][:, 0:T], after=[pe.done.now(), a.done.now()])
                d.do(d.eng.tensor_tensor, o, banks[0][0][:, 0:T], zs, ALU.add)
                self.head_norm_gate(o, zs, self.p("dn_norm_w"), zg, self.branch[2][:, ds(head, 1), :], self.bank[1])
        with pr.loop(2, "late") as turn:
            for _ in self.read_group(turn + 11)[0]:
                pass
        self.join_gemm()
        self.stored()

    def hyena(self):
        d, a, pe, pr, io, ar = self.dve, self.act, self.pe, self.prog, self.io, self.arena
        H = 1024
        ident = self.c("ident")
        ar.reset()
        z = ar.take(2, 3 * H)
        mats = ar.take(4, 2 * T)
        hs, hd, kr, ki = (ar.take(2, H) for _ in range(4))
        win = ar.take(2, H)
        w3 = ar.take(2, H)
        hid = ar.take(T)
        row = ar.take(H)
        raw, y = row[:, 0:T], row[:, T:2 * T]
        fwd_re, fwd_im, inv_re, inv_im = (mats[:, i, :].rearrange("p (a b) -> p a b", a=2) for i in range(4))
        B = self.bank
        pr.join()
        pr.dma(a, "hy_in", mats, io["dft"])
        t_w = pr.dma(a, "hy_in", win, io["window"])
        hy = io["s_read"].rearrange("(c p) t -> p c t", p=P)
        taps = self.p("hy_conv_w").rearrange("p (j c) -> p j c", j=3)
        with pr.loop(24, "hy_conv") as c:
            t = pr.dma(a, "mixer_in", raw, hy[:, ds(c + 28, 1), :], after=[d.done.now()])
            d.wait(t, pe.done.now())
            self.conv(y, raw, lambda j: taps[:, j, ds(c, 1)], 0, 4)
            t = d.do(d.eng.tensor_scalar, y, y, self.p("hy_conv_b")[:, ds(c, 1)], None, ALU.add, ALU.bypass)
            t = pe.do(lambda: [pe.eng.transpose(B[0][:, P * j:P * j + P], y[:, P * j:P * j + P], ident) for j in range(2)][-1],
                      after=[t])
            d.do(self.copy, z[:, :, ds(c * P, P)], B[0][:, 0:T].rearrange("p (j t) -> p j t", j=2), after=[t])
        pr.join(t_w)

        feats, w1, w2 = kr[0:33, 0, 0:T], kr[0:33, 0, T:T + 64], kr[0:64, 1, 0:64]
        pr.dma(a, "hy_in", feats, io["feats"])
        pr.dma(a, "hy_in", w1, io["hy_w1"])
        t = pr.dma(a, "hy_in", w2, io["hy_w2"])
        pe.wait(t)
        h64, r64 = hid[0:64, :], raw[0:64, :]
        for lhs, rhs, bias in ((w1, feats, "hy_b1"), (w2, h64, "hy_b2")):
            t = pe.do(pe.eng.matmul, B[0][0:64, 0:T], lhs, rhs, start=True, stop=True, after=[a.done.now()])
            d.do(d.eng.tensor_scalar, h64, B[0][0:64, 0:T], self.p(bias)[0:64, :], None, ALU.add, ALU.bypass, after=[t])
            d.do(d.eng.tensor_scalar, r64, h64, 1.0 / (2 * np.pi), MAGIC, ALU.mult, ALU.add)
            d.do(d.eng.tensor_scalar, r64, r64, -MAGIC, None, ALU.add, ALU.bypass)
            for part in (6.28125, 1.9350051879882812e-3, 3.0199159819e-7):
                d.do(d.eng.scalar_tensor_tensor, h64, r64, -part, h64, ALU.mult, ALU.add)
            t = d.do(d.eng.tensor_scalar, h64, h64, 3.1415925, -3.1415925, ALU.min, ALU.max)
            a.do(a.eng.activation, h64, h64, ACT.Sin, after=[t])
        pr.join()

        def transform(dst, mat, src, first=None):
            for m in range(2):
                for half in range(2):
                    b = B[2 * m + half]
                    for j in range(2):
                        mm = pe.eng.matmul(b[:, :], mat[:, j, P * m:P * m + P], src(j, half), start=j == 0, stop=j == 1)
                    t = pe.done.add(mm)
                    d.do(d.eng.tensor_copy, dst[:, m, 512 * half:512 * half + 512], b[:, :], after=[t])
            pe.wait(d.done.now())

        def cols(buf):
            return lambda j, half: buf[:, j, 512 * half:512 * half + 512]

        u = lambda j, half: z[:, j, 512 * half:512 * half + 512]
        for n in range(2):
            t = pr.dma(a, "hy_in", w3[0:64, :, :].rearrange("p a b -> p (a b)"), io["hy_w3"][:, 2 * H * n:2 * H * (n + 1)])
            t = pr.dma(a, "hy_in", row[0:1, :], io["hy_skip"][n:n + 1, :])
            pe.wait(t)
            d.wait(t)
            for m in range(2):
                for half in range(2):
                    bf, bb = B[2 * (half % 2)], B[2 * (half % 2) + 1]
                    sl = slice(512 * half, 512 * half + 512)
                    pe.wait(d.done.now())
                    pe.eng.matmul(bf[:, :], h64[:, P * m:P * m + P], w3[0:64, 0, sl], start=True, stop=True)
                    t = pe.done.add(pe.eng.matmul(bb[:, :], h64[:, P * m:P * m + P], w3[0:64, 1, sl], start=True, stop=True))
                    tmp = kr[:, 0, 0:512]
                    d.do(d.eng.tensor_copy, tmp, bb[:, :], after=[t])
                    if m == 0:
                        d.do(d.eng.memset, tmp[0:1, :], 0.0)
                    d.do(d.eng.tensor_tensor, hs[:, m, sl], bf[:, :], tmp, ALU.add)
                    d.do(d.eng.tensor_tensor, hd[:, m, sl], bf[:, :], tmp, ALU.subtract)
            d.do(d.eng.tensor_tensor, hs, hs, win, ALU.mult)
            d.do(d.eng.tensor_tensor, hd, hd, win, ALU.mult)
            t = d.do(d.eng.tensor_tensor, hs[0:1, 0, :], hs[0:1, 0, :], row[0:1, :], ALU.add)
            pe.wait(t)
            transform(kr, fwd_re, cols(hs))
            transform(ki, fwd_im, cols(hd))
            for half in range(2):
                for j in range(2):
                    mm = pe.eng.matmul(B[half][0:1, :], fwd_im[:, j, 0:1], cols(hs)(j, half), start=j == 0, stop=j == 1)
                t = pe.done.add(mm)
                d.do(d.eng.tensor_copy, ki[0:1, 0, 512 * half:512 * half + 512], B[half][0:1, :], after=[t])
            pe.wait(d.done.now())
            ur, ui, tmp = hs, hd, w3
            transform(ur, fwd_re, u)
            transform(ui, fwd_im, u)
            d.do(d.eng.tensor_tensor, tmp, ui, ki, ALU.mult)
            d.do(d.eng.tensor_copy, row[0:1, :], tmp[0:1, 0, :])
            d.do(d.eng.memset, tmp[0:1, 0, :], 0.0)
            d.do(d.eng.tensor_tensor, ki, ur, ki, ALU.mult)
            d.do(d.eng.tensor_tensor, ui, ui, kr, ALU.mult)
            d.do(d.eng.tensor_tensor, ur, ur, kr, ALU.mult)
            d.do(d.eng.tensor_tensor, ur, ur, tmp, ALU.subtract)
            d.do(d.eng.tensor_tensor, ui, ui, ki, ALU.add)
            t = d.do(d.eng.tensor_copy, ui[0:1, 0, :], row[0:1, :])
            pe.wait(t)
            gate = H * (n + 1)
            for m in range(2):
                for half in range(2):
                    b = B[2 * m + half]
                    for j in range(2):
                        pe.eng.matmul(b[:, :], inv_re[:, j, P * m:P * m + P], cols(ur)(j, half), start=j == 0, stop=False)
                        mm = pe.eng.matmul(b[:, :], inv_im[:, j, P * m:P * m + P], cols(ui)(j, half), start=False, stop=j == 1)
                    t = pe.done.add(mm)
                    d.do(d.eng.tensor_tensor, z[:, m, 512 * half:512 * half + 512], b[:, :],
                         z[:, m, gate + 512 * half:gate + 512 * half + 512], ALU.mult, after=[t])
            pr.join()
        for c in range(8):
            b = B[c % 4]
            t = pe.do(lambda: [pe.eng.transpose(b[:, P * j:P * j + P], z[:, j, P * c:P * c + P], ident) for j in range(2)][-1],
                      after=[d.done.now()])
            d.do(d.eng.tensor_copy, self.branch[0][:, c, :], b[:, 0:T], after=[t])
        pr.join()

    def merge(self):
        d, a, g, pr, io = self.dve, self.act, self.gemm, self.prog, self.io
        self.arena.reset()
        gates = self.arena.take(8, T)
        tmp = self.arena.take(4, T)
        view = io["s_gate"].rearrange("(c p) t -> p c t", p=P)
        for n in range(3):
            def evacuate(chunk, m, psum, summed, n=n, count=[0]):
                slot = (count[0] % 8)
                count[0] += 1
                a.wait(d.done.now())
                t = pr.gate_in[slot].add(a.eng.dma_start(gates[:, slot, :], view[:, ds(chunk + 16 * n, 1), :]), 16)
                d.wait(t, summed)
                t = g.drained[m].add(d.eng.tensor_tensor(tmp[:, m % 4, :], psum, gates[:, slot, :], ALU.mult))
                dst = self.mix[:, ds(chunk, 1), :]
                d.wait(t)
                if n == 0:
                    d.done.add(self.copy(dst, tmp[:, m % 4, :]))
                else:
                    d.done.add(d.eng.tensor_tensor(dst, dst, tmp[:, m % 4, :], ALU.add))
            g.run("w_branch%d" % n, io["w_branch%d" % n], 8, DM, lambda kc: self.branch[n][:, kc, :], T, evacuate, groups=2)
            self.join_gemm()

    def layernorm(self, x, gain, bias, eps, tmp):
        d, a, pe, bank = self.dve, self.act, self.pe, self.bank[0]
        rs = self.rstd[:, 0:T]
        for c in range(KD):
            mm = pe.eng.matmul(bank[:, 0:T], self.c("ones"), x[:, c, :], start=c == 0, stop=c == KD - 1)
        t = pe.done.add(mm)
        d.do(d.eng.tensor_scalar, rs, bank[:, 0:T], 1.0 / DM, None, ALU.mult, ALU.bypass, after=[t])
        t = d.do(d.eng.tensor_tensor, x, x, rs.unsqueeze(1).broadcast_to((P, KD, T)), ALU.subtract)
        t = a.do(a.eng.activation, tmp, x, ACT.Square, after=[t])
        pe.wait(t)
        for c in range(KD):
            mm = pe.eng.matmul(bank[:, 0:T], self.c("ones"), tmp[:, c, :], start=c == 0, stop=c == KD - 1)
        t = pe.done.add(mm)
        self.rsqrt(rs, bank[:, 0:T], 1.0 / DM, eps, after=[t])
        for c in range(KD):
            d.do(d.eng.scalar_tensor_tensor, x[:, c, :], x[:, c, :], gain[:, c:c + 1], rs, ALU.mult, ALU.mult)
            t = d.do(d.eng.tensor_scalar, x[:, c, :], x[:, c, :], bias[:, c:c + 1], None, ALU.add, ALU.bypass)
        return t

    def gated_residual(self, x, gate):
        d, g = self.dve, self.gemm
        d.do(d.eng.tensor_scalar, x, x, ALPHA, None, ALU.mult, ALU.bypass)
        col = self.mods[:, gate:gate + KD, 0]

        def evacuate(chunk, m, psum, summed):
            d.wait(d.done.now(), summed)
            dst = x[:, ds(chunk, 1), :]
            g.drained[m].add(d.eng.scalar_tensor_tensor(dst, psum, col[:, ds(chunk, 1)], dst, ALU.mult, ALU.add))
        return evacuate

    def block2_end(self):
        d, a, g, io, pr = self.dve, self.act, self.gemm, self.io, self.prog
        x = self.res[:, :, NMETA:]
        g.run("w_out2", io["w_out2"], KD, DM, lambda kc: self.mix[:, kc, :], T, self.gated_residual(x, 32), groups=2)
        self.join_gemm()
        self.layernorm(x, self.p("ln1_g"), self.p("ln1_b"), 1e-5, self.mix[:, :, :])
        pr.join()
        t = self.modulate(x, self.xin[:, :, 0:T], 48, 64, 0)
        self.arena.reset()
        hid = self.arena.take(DFF // P, T)
        self.sq_tmp = self.arena.take(4, T)
        g.run("w_ff1", io["w_ff1"], KD, DFF, lambda kc: self.xin[:, kc, 0:T], T, self.squared_relu(hid), after=[t], groups=2)
        self.join_gemm()
        g.run("w_ff2", io["w_ff2"], DFF // P, DM, lambda kc: hid[:, kc, :], T, self.gated_residual(x, 80), groups=2)
        self.join_gemm()
        t = self.layernorm(x, self.p("ln2_g"), self.p("ln2_b"), 1e-5, self.mix[:, :, :])
        pr.dma(a, "out", io["out"].rearrange("(c p) t -> p c t", p=P), x, after=[t])


def program(nc, io, per_turn, pofs, cofs):
    k = Kernel(nc, io, per_turn, pofs, cofs)
    k.load_inputs()
    k.modulation_begin()
    k.block1_project()
    kv_head = k.attention()
    k.ssm(kv_head)
    k.block1_mlp()
    k.block2_project()
    k.deltanet()
    k.hyena()
    k.merge()
    k.block2_end()
    k.act.wait(*[s.now() for n, s in k.prog.dma_sems.items()])
    return k.prog.seen


def kernel(**inputs):
    import concourse.bacc as bacc
    from concourse.bass_utils import run_bass_kernel_spmd as run

    i = {k: np.asarray(v) for k, v in inputs.items()}
    params, pofs = layout_params(i)
    consts, cofs = constants()
    feats, window = filter_features()
    arrays = {
        "params": params, "consts": consts,
        "hT": np.ascontiguousarray(np.concatenate([i["meta_tokens"], i["x"][0]], axis=0).T),
        "w_in": i["w_in"][0], "w_glu": i["w_glu"][0], "w_out": i["w_out"][0],
        "w_up": i["w_up"][0], "w_down": i["w_down"][0],
        **layout_ssm(i),
        "w_ada": i["w_ada_2"][0], "w_in2": i["w_in_2"][0], "ctxT": np.ascontiguousarray(i["ctx_2"][0].T),
        "dft": fourier(), "feats": feats, "window": window,
        "hy_w1": i["hy_filt_w1_2"][0], "hy_w2": i["hy_filt_w2_2"][0], "hy_w3": i["hy_filt_w3_2"][0],
        "hy_skip": i["hy_skip_2"][0],
        **{"w_branch%d" % n: i["w_branch_2"][0, n] for n in range(3)},
        "w_out2": i["w_out_2"][0], "w_ff1": i["w_ff1_2"][0], "w_ff2": i["w_ff2_2"][0],
    }
    outs = {"out": (DM, T)}
    scratch = {"s_state": (4608, 2 * T), "s_read": (6656, T), "s_gate": (6144, T),
               "s_mods": (2, 6 * DM), "s_kf": (512, 512), "s_qf": (512, T), "s_kt": (512, 512), "s_vt": (1024, 512)}

    def built(per_turn):
        nc = bacc.Bacc("TRN2", target_bir_lowering=False, num_devices=1)
        io = {k: nc.dram_tensor("in_" + k, v.shape, F32, kind="ExternalInput").ap() for k, v in arrays.items()}
        io |= {k: nc.dram_tensor("out_" + k, s, F32, kind="ExternalOutput").ap() for k, s in outs.items()}
        io |= {k: nc.dram_tensor(k, s, F32, kind="Internal").ap() for k, s in scratch.items()}
        return nc, program(nc, io, per_turn, pofs, cofs)

    _, seen = built({})
    nc, again = built(seen)
    assert seen == again
    r = run(nc, [{"in_" + k: v for k, v in arrays.items()}], core_ids=[0])
    return np.ascontiguousarray(r.results[0]["out_out"].T)[None]
```
